# Optimizing a Trainium2 kernel written in Bass

```python
import numpy as np
import jax, jax.numpy as jnp
from jax import lax
import math

D_MODEL = 2048
BATCH = 1
SEQ = 256
DEPTH = 2

N_EVEN = (DEPTH + 1) // 2
N_ODD = DEPTH // 2

A_HEADS = 8
A_DK = 128
A_DV = 128
A_QK = A_HEADS * A_DK
A_WIDTH = A_HEADS * A_DV
B_HEADS = 8
B_DK = 128
B_DV = 128
B_QK = B_HEADS * B_DK
B_WIDTH = B_HEADS * B_DV
CONV_K = 4
CHUNK = 64
EVEN_IN = 2 * A_QK + 2 * A_WIDTH + 2 * B_QK + 2 * B_WIDTH + 2 * B_HEADS
EVEN_OUT = A_WIDTH + B_WIDTH

C_HEADS = 16
C_GROUPS = 4
C_HPG = C_HEADS // C_GROUPS
C_DK = 128
C_DV = 128
C_Q = C_HEADS * C_DK
C_KV = C_GROUPS * C_DK
CMP_LEN = 32
CMP_STRIDE = 16
SEL_BLOCK = 64
N_SEL = 8
WINDOW = 512
Q_BLOCK = 128
SEL_Q_BLOCK = 64
SEL_FORCE = 1e4
ODD_IN = C_Q + 6 * C_KV + 3 * C_HEADS
ODD_OUT = C_HEADS * C_DV

D_FF = -(-8 * D_MODEL // (3 * 256)) * 256
NORM_EPS = 1e-6
NEG_INF = -1e30


def rmsnorm(x, g):
    xf = x.astype(jnp.float32)
    y = xf * lax.rsqrt(jnp.mean(xf * xf, axis=-1, keepdims=True) + NORM_EPS)
    return (y * g.astype(jnp.float32)).astype(x.dtype)

def l2norm(x):
    return x * lax.rsqrt(jnp.sum(x * x, axis=-1, keepdims=True) + NORM_EPS)

def masked_softmax(s, mask):
    return jax.nn.softmax(jnp.where(mask, s, NEG_INF), axis=-1) * mask

def alibi_slopes(n):
    return jnp.asarray(2.0 ** (-8.0 * np.arange(1, n + 1) / n), jnp.float32)

def _chunks(x):
    b, t, h = x.shape[:3]
    x = x.reshape((b, t // CHUNK, CHUNK, h) + x.shape[3:])
    return jnp.moveaxis(x, 3, 1)

def _unchunk(o):
    n, b, h, c, d = o.shape
    return o.transpose(1, 0, 3, 2, 4).reshape(b, n * c, h, d)

def _causal_conv(x, w):
    return lax.conv_general_dilated(x, w[:, None, :], window_strides=(1,), padding=[(CONV_K - 1, 0)],
                                    dimension_numbers=('NWC', 'WIO', 'NWC'), feature_group_count=x.shape[-1])

def _hgrn2(q, f_logit, i, lb):
    b_, t_, h_, dk = q.shape
    dv = i.shape[-1]
    f = lb + (1.0 - lb) * jax.nn.sigmoid(f_logit)
    log_f = jnp.log(f)
    k = 1.0 - f
    xs = tuple(jnp.moveaxis(_chunks(a), 2, 0) for a in (q, k, i, log_f))
    tril = jnp.tril(jnp.ones((CHUNK, CHUNK), bool))[:, :, None]

    def step(S, inp):
        qn, kn, vn, ln = inp
        b = jnp.cumsum(ln, axis=2)
        decay = jnp.exp(jnp.where(tril, b[:, :, :, None, :] - b[:, :, None, :, :], -jnp.inf))
        intra = jnp.einsum('bhtd,bhsd,bhtsd->bhts', qn, kn, decay)
        o = jnp.einsum('bhts,bhse->bhte', intra, vn) + jnp.einsum('bhtd,bhde->bhte', qn * jnp.exp(b), S)
        b_end = b[:, :, -1:, :]
        S = jnp.exp(b_end[:, :, 0, :, None]) * S + jnp.einsum('bhsd,bhse->bhde', kn * jnp.exp(b_end - b), vn)
        return S, o

    S0 = jnp.zeros((b_, h_, dk, dv), jnp.float32)
    _, o = lax.scan(step, S0, xs)
    return _unchunk(o)

def _gated_delta(q, k, v, beta, log_decay):
    b_, t_, h_, dk = q.shape
    dv = v.shape[-1]
    qc, kc, vc = _chunks(q), _chunks(k), _chunks(v)
    bc = _chunks(beta)
    gc = jnp.cumsum(_chunks(log_decay), axis=-1)
    eye = jnp.eye(CHUNK, dtype=bool)
    tril = jnp.tril(jnp.ones((CHUNK, CHUNK), bool))
    decay = jnp.exp(jnp.where(tril, gc[..., :, None] - gc[..., None, :], -jnp.inf))
    kb = kc * bc[..., None]
    L = jnp.where(tril & ~eye, jnp.einsum('bhncd,bhnsd->bhncs', kb, kc) * decay, 0.0)
    rhs = jnp.concatenate([vc * bc[..., None], kb * jnp.exp(gc)[..., None]], axis=-1)
    sol = lax.linalg.triangular_solve(L + eye, rhs, left_side=True, lower=True, unit_diagonal=True)
    u, w = sol[..., :dv], sol[..., dv:]
    qk = jnp.einsum('bhncd,bhnsd->bhncs', qc, kc) * decay
    xs = tuple(jnp.moveaxis(a, 2, 0) for a in (qc, kc, u, w, qk, gc))

    def step(S, inp):
        qn, kn, un, wn, qkn, gn = inp
        v_new = un - jnp.einsum('bhcd,bhde->bhce', wn, S)
        o = (jnp.einsum('bhcd,bhde->bhce', qn * jnp.exp(gn)[..., None], S)
             + jnp.einsum('bhcs,bhse->bhce', qkn, v_new))
        g_end = gn[..., -1:]
        S = (jnp.exp(g_end)[..., None] * S
             + jnp.einsum('bhcd,bhce->bhde', kn * jnp.exp(g_end - gn)[..., None], v_new))
        return S, o

    S0 = jnp.zeros((b_, h_, dk, dv), jnp.float32)
    _, o = lax.scan(step, S0, xs)
    return _unchunk(o)

def _even_mixer(u, w_in, lb, conv_w, a_log, dt_bias, hgrn_g, gdn_g, w_out):
    b_, t_, _ = u.shape
    z = (u @ w_in).astype(jnp.float32)
    cuts = [int(c) for c in np.cumsum([A_QK, A_QK, A_WIDTH, A_WIDTH, B_QK, B_QK, B_WIDTH, B_WIDTH, B_HEADS])]
    aq, af, ai, ag, bq, bk, bv, bg, ba, bb = jnp.split(z, cuts, axis=-1)
    o_a = _hgrn2(aq.reshape(b_, t_, A_HEADS, A_DK), af.reshape(b_, t_, A_HEADS, A_DK),
                 ai.reshape(b_, t_, A_HEADS, A_DV), lb)
    o_a = rmsnorm(o_a, hgrn_g) * jax.nn.silu(ag.reshape(b_, t_, A_HEADS, A_DV))
    qkv = jax.nn.silu(_causal_conv(jnp.concatenate([bq, bk, bv], axis=-1), conv_w.astype(jnp.float32)))
    bq, bk, bv = jnp.split(qkv, [B_QK, 2 * B_QK], axis=-1)
    q = l2norm(bq.reshape(b_, t_, B_HEADS, B_DK)) * (B_DK ** -0.5)
    k = l2norm(bk.reshape(b_, t_, B_HEADS, B_DK))
    beta = jax.nn.sigmoid(bb)
    log_decay = -jnp.exp(a_log.astype(jnp.float32)) * jax.nn.softplus(ba + dt_bias.astype(jnp.float32))
    o_b = _gated_delta(q, k, bv.reshape(b_, t_, B_HEADS, B_DV), beta, log_decay)
    o_b = rmsnorm(o_b, gdn_g) * jax.nn.silu(bg.reshape(b_, t_, B_HEADS, B_DV))
    o = jnp.concatenate([o_a.reshape(b_, t_, A_WIDTH), o_b.reshape(b_, t_, B_WIDTH)], axis=-1)
    return o.astype(u.dtype) @ w_out

def _nsa_mixer(u, w_in, cmp_pos, cmp_w1, cmp_w2, w_out):
    b_, t_, _ = u.shape
    G, HP = C_GROUPS, C_HPG
    z = (u @ w_in).astype(jnp.float32)
    cuts = [C_Q + j * C_KV for j in range(7)]
    q, kc, vc, ks, vs, kw, vw, gl = jnp.split(z, cuts, axis=-1)
    kv = lambda a: a.reshape(b_, t_, G, C_DK)
    kc, vc, ks, vs, kw, vw = (kv(a) for a in (kc, vc, ks, vs, kw, vw))
    qg = q.reshape(b_, t_, G, HP, C_DK).transpose(0, 2, 3, 1, 4) * (C_DK ** -0.5)
    gates = jax.nn.sigmoid(gl.reshape(b_, t_, G, HP, 3)).transpose(0, 2, 3, 1, 4)
    slopes = alibi_slopes(C_HEADS).reshape(G, HP)
    tpos = jnp.arange(t_)

    n_cmp = (t_ - CMP_LEN) // CMP_STRIDE + 1
    cstart = jnp.arange(n_cmp) * CMP_STRIDE
    cidx = cstart[:, None] + jnp.arange(CMP_LEN)[None, :]

    def compress(a, pos, w1, w2):
        blk = a[:, cidx] + pos[None, None, :, None, :]
        blk = blk.transpose(0, 1, 3, 2, 4).reshape(b_, n_cmp, G, CMP_LEN * C_DK)
        return jax.nn.silu(blk @ w1) @ w2

    k_cmp = compress(kc, cmp_pos[0], cmp_w1[0], cmp_w2[0])
    v_cmp = compress(vc, cmp_pos[1], cmp_w1[1], cmp_w2[1])
    dist_c = tpos[:, None] - (cstart + CMP_LEN - 1)[None, :]
    s_c = jnp.einsum('bghtd,bjgd->bghtj', qg, k_cmp) - slopes[:, :, None, None] * dist_c
    p_c = masked_softmax(s_c, dist_c >= 0)
    o_cmp = jnp.einsum('bghtj,bjge->bghte', p_c, v_cmp)

    n_blk = t_ // SEL_BLOCK
    n_sel = min(N_SEL, n_blk)
    bstart = jnp.arange(n_blk) * SEL_BLOCK
    overlap = ((cstart[:, None] < bstart[None, :] + SEL_BLOCK)
               & (cstart[:, None] + CMP_LEN > bstart[None, :])).astype(jnp.float32)
    imp = jnp.einsum('bghtj,ji->bgti', p_c, overlap)
    cur = (tpos // SEL_BLOCK)[:, None]
    bi = jnp.arange(n_blk)[None, :]
    forced = (bi == 0) | (bi == cur) | (bi == cur - 1)
    score = jnp.where(forced, SEL_FORCE, jnp.where(bi > cur, -SEL_FORCE, imp))
    _, sel_idx = lax.top_k(score, n_sel)

    ks_blocks = ks.reshape(b_, n_blk, SEL_BLOCK, G, C_DK).transpose(0, 3, 1, 2, 4)
    vs_blocks = vs.reshape(b_, n_blk, SEL_BLOCK, G, C_DV).transpose(0, 3, 1, 2, 4)
    nqb = t_ // SEL_Q_BLOCK
    q_b = qg.reshape(b_, G, HP, nqb, SEL_Q_BLOCK, C_DK).transpose(3, 0, 1, 2, 4, 5)
    idx_b = sel_idx.reshape(b_, G, nqb, SEL_Q_BLOCK, n_sel).transpose(2, 0, 1, 3, 4)
    t_b = tpos.reshape(nqb, SEL_Q_BLOCK)
    gather = jax.vmap(jax.vmap(lambda blocks, ix: blocks[ix]))
    n_keys = n_sel * SEL_BLOCK

    def sel_block(args):
        qb, ib, tb = args
        kg = gather(ks_blocks, ib).reshape(b_, G, SEL_Q_BLOCK, n_keys, C_DK)
        vg = gather(vs_blocks, ib).reshape(b_, G, SEL_Q_BLOCK, n_keys, C_DV)
        kpos = (ib[..., None] * SEL_BLOCK + jnp.arange(SEL_BLOCK)).reshape(b_, G, SEL_Q_BLOCK, n_keys)
        dist = tb[None, None, :, None] - kpos
        s = (jnp.einsum('bghqd,bgqkd->bghqk', qb, kg)
             - slopes[None, :, :, None, None] * dist[:, :, None])
        p = masked_softmax(s, (dist >= 0)[:, :, None])
        return jnp.einsum('bghqk,bgqke->bghqe', p, vg)

    o_slc = lax.map(sel_block, (q_b, idx_b, t_b))
    o_slc = o_slc.transpose(1, 2, 3, 0, 4, 5).reshape(b_, G, HP, t_, C_DV)

    nwb = t_ // Q_BLOCK
    band = jnp.arange(nwb)[:, None] * Q_BLOCK + jnp.arange(Q_BLOCK + WINDOW)[None, :]
    pad = ((0, 0), (0, 0), (WINDOW, 0), (0, 0))
    kb = jnp.pad(kw.transpose(0, 2, 1, 3), pad)[:, :, band]
    vb = jnp.pad(vw.transpose(0, 2, 1, 3), pad)[:, :, band]
    kpos = band - WINDOW
    dist_w = tpos.reshape(nwb, Q_BLOCK)[:, :, None] - kpos[:, None, :]
    valid_w = (dist_w >= 0) & (dist_w < WINDOW) & (kpos[:, None, :] >= 0)
    qw = qg.reshape(b_, G, HP, nwb, Q_BLOCK, C_DK)
    s_w = jnp.einsum('bghnqd,bgnkd->bghnqk', qw, kb) - slopes[:, :, None, None, None] * dist_w
    p_w = masked_softmax(s_w, valid_w)
    o_win = jnp.einsum('bghnqk,bgnke->bghnqe', p_w, vb).reshape(b_, G, HP, t_, C_DV)

    o = gates[..., 0:1] * o_cmp + gates[..., 1:2] * o_slc + gates[..., 2:3] * o_win
    o = o.transpose(0, 3, 1, 2, 4).reshape(b_, t_, ODD_OUT)
    return o.astype(u.dtype) @ w_out

def _swiglu(u, w_gu, w_down):
    gate, up = jnp.split(u @ w_gu, 2, axis=-1)
    return (jax.nn.silu(gate) * up) @ w_down

def first_inputs(seed: int = 0) -> dict:
    key = jax.random.key(seed)
    ks = jax.random.split(key, 20)
    f32 = jnp.float32
    nrm = lambda k, shape: jax.random.normal(k, shape, f32)
    w = lambda k, shape, fan_in: nrm(k, shape) * fan_in ** -0.5
    dt = jnp.exp(jax.random.uniform(ks[6], (N_EVEN, B_HEADS), f32, np.log(1e-3), np.log(1e-1)))
    return {
        'x': nrm(ks[0], (BATCH, SEQ, D_MODEL)),
        'norm_g': 1.0 + 0.05 * nrm(ks[1], (DEPTH, 4, D_MODEL)),
        'ab_w_in': w(ks[2], (N_EVEN, D_MODEL, EVEN_IN), D_MODEL),
        'hgrn_lb_logits': 0.5 * nrm(ks[3], (N_EVEN, A_QK)),
        'gdn_conv_w': w(ks[4], (N_EVEN, CONV_K, 2 * B_QK + B_WIDTH), CONV_K),
        'gdn_a_log': jnp.log(jax.random.uniform(ks[5], (N_EVEN, B_HEADS), f32, 1.0, 16.0)),
        'gdn_dt_bias': dt + jnp.log(-jnp.expm1(-dt)),
        'hgrn_norm_g': 1.0 + 0.05 * nrm(ks[7], (N_EVEN, A_DV)),
        'gdn_norm_g': 1.0 + 0.05 * nrm(ks[8], (N_EVEN, B_DV)),
        'ab_w_out': w(ks[9], (N_EVEN, EVEN_OUT, D_MODEL), EVEN_OUT),
        'nsa_w_in': w(ks[10], (N_ODD, D_MODEL, ODD_IN), D_MODEL),
        'nsa_cmp_pos': 0.1 * nrm(ks[11], (N_ODD, 2, CMP_LEN, C_DK)),
        'nsa_cmp_w1': w(ks[12], (N_ODD, 2, CMP_LEN * C_DK, C_DK), CMP_LEN * C_DK),
        'nsa_cmp_w2': w(ks[13], (N_ODD, 2, C_DK, C_DK), C_DK),
        'nsa_w_out': w(ks[14], (N_ODD, ODD_OUT, D_MODEL), ODD_OUT),
        'ffn_w_gu': w(ks[15], (DEPTH, D_MODEL, 2 * D_FF), D_MODEL),
        'ffn_w_down': w(ks[16], (DEPTH, D_FF, D_MODEL), D_FF),
    }

def first_block(x, norm_g, ab_w_in, hgrn_lb_logits, gdn_conv_w, gdn_a_log, gdn_dt_bias, hgrn_norm_g,
              gdn_norm_g, ab_w_out, nsa_w_in, nsa_cmp_pos, nsa_cmp_w1, nsa_cmp_w2, nsa_w_out,
              ffn_w_gu, ffn_w_down):
    lb_all = jnp.cumsum(jax.nn.softmax(hgrn_lb_logits.astype(jnp.float32), axis=0), axis=0)
    lb_all = lb_all - lb_all[:1]
    h = x
    for layer in range(DEPTH):
        j = layer // 2
        u = rmsnorm(h, norm_g[layer, 0])
        if layer % 2 == 0:
            m = _even_mixer(u, ab_w_in[j], lb_all[j].reshape(A_HEADS, A_DK), gdn_conv_w[j], gdn_a_log[j],
                            gdn_dt_bias[j], hgrn_norm_g[j], gdn_norm_g[j], ab_w_out[j])
        else:
            m = _nsa_mixer(u, nsa_w_in[j], nsa_cmp_pos[j], nsa_cmp_w1[j], nsa_cmp_w2[j], nsa_w_out[j])
        h = h + rmsnorm(m, norm_g[layer, 1])
        u = rmsnorm(h, norm_g[layer, 2])
        h = h + rmsnorm(_swiglu(u, ffn_w_gu[layer], ffn_w_down[layer]), norm_g[layer, 3])
    return h


HEAD_DIM = 64
MIX_WIDTH = D_MODEL // 4
BRANCH_W = MIX_WIDTH // 2
N_HEADS = BRANCH_W // HEAD_DIM
N_IN_PARTS = 8
ROPE_THETA = 10000.0
DIL_PAIRS = ((128, 1), (512, 4), (2048, 16))
DIL_STEPS = 128
MOBA_BLOCK = 256
MOBA_TOPK = 3
DIFF_HEAD_DIM = HEAD_DIM // 2
RMS_EPS = 1e-6
N_ODD_2 = DEPTH // 2


def _rmsnorm(x, g):
    xf = x.astype(jnp.float32)
    y = xf * lax.rsqrt(jnp.mean(xf * xf, axis=-1, keepdims=True) + RMS_EPS)
    return (y * g.astype(jnp.float32)).astype(x.dtype)

def _rope(t, pos):
    d = t.shape[-1]
    half = d // 2
    inv = ROPE_THETA ** (-jnp.arange(half, dtype=jnp.float32) / half)
    ang = pos.astype(jnp.float32)[:, None] * inv[None, :]
    cos, sin = jnp.cos(ang), jnp.sin(ang)
    tf = t.astype(jnp.float32)
    t1, t2 = tf[..., :half], tf[..., half:]
    return jnp.concatenate([t1 * cos - t2 * sin, t1 * sin + t2 * cos], axis=-1).astype(t.dtype)

def _heads(t):
    b, s, _ = t.shape
    return t.reshape(b, s, N_HEADS, -1).transpose(0, 2, 1, 3)

def _merge(t):
    b, h, s, d = t.shape
    return t.transpose(0, 2, 1, 3).reshape(b, s, h * d)

def _dilated_branch(q, k, v, r):
    b, h, s, d = q.shape
    L = -(-s // (r * DIL_STEPS)) * DIL_STEPS
    pad = L * r - s
    nb = L // DIL_STEPS

    def to_phase(t):
        t = jnp.pad(t, ((0, 0), (0, 0), (0, pad), (0, 0)))
        t = t.reshape(b, h, L, r, d).transpose(0, 1, 3, 2, 4)
        return t.reshape(b, h, r, nb, DIL_STEPS, d)

    qb, kb, vb = to_phase(q), to_phase(k), to_phase(v)
    prev = lambda t: jnp.pad(t, ((0, 0), (0, 0), (0, 0), (1, 0), (0, 0), (0, 0)))[:, :, :, :-1]
    kk = jnp.concatenate([prev(kb), kb], axis=4)
    vv = jnp.concatenate([prev(vb), vb], axis=4)
    sc = jnp.einsum('bhrnqd,bhrnkd->bhrnqk', qb, kk).astype(jnp.float32) / math.sqrt(d)
    i = jnp.arange(DIL_STEPS)[:, None]
    j = jnp.arange(2 * DIL_STEPS)[None, :]
    band = (j >= i) & (j <= i + DIL_STEPS)
    exists = (jnp.arange(nb)[:, None, None] > 0) | (j[None] >= DIL_STEPS)
    mask = band[None] & exists
    sc = jnp.where(mask, sc, -jnp.inf)
    m = jnp.max(sc, axis=-1, keepdims=True)
    p = jnp.exp(sc - m)
    den = jnp.sum(p, axis=-1)
    o = jnp.einsum('bhrnqk,bhrnkd->bhrnqd', p, vv.astype(jnp.float32)) / den[..., None]
    lse = m[..., 0] + jnp.log(den)
    o = o.reshape(b, h, r, L, d).transpose(0, 1, 3, 2, 4).reshape(b, h, L * r, d)[:, :, :s]
    lse = lse.reshape(b, h, r, L).transpose(0, 1, 3, 2).reshape(b, h, L * r)[:, :, :s]
    return o, lse

def _dilated_mixture(q, k, v):
    outs, lses = [], []
    for _, r in DIL_PAIRS:
        o, l = _dilated_branch(q, k, v, r)
        outs.append(o)
        lses.append(l)
    w = jax.nn.softmax(jnp.stack(lses, axis=0), axis=0)[..., None]
    return jnp.sum(w * jnp.stack(outs, axis=0), axis=0).astype(q.dtype)

def _moba(q, k, v):
    b, h, s, d = q.shape
    sp = -(-s // MOBA_BLOCK) * MOBA_BLOCK
    nblk = sp // MOBA_BLOCK
    kp = jnp.pad(k, ((0, 0), (0, 0), (0, sp - s), (0, 0)))
    vp = jnp.pad(v, ((0, 0), (0, 0), (0, sp - s), (0, 0)))
    kb = kp.reshape(b, h, nblk, MOBA_BLOCK, d)
    vb = vp.reshape(b, h, nblk, MOBA_BLOCK, d)
    kmean = jnp.mean(kb.astype(jnp.float32), axis=3)
    n_sel = min(MOBA_TOPK, nblk)
    nch = s // Q_BLOCK
    qc = q.reshape(b, h, nch, Q_BLOCK, d).transpose(2, 0, 1, 3, 4)
    starts = jnp.arange(nch, dtype=jnp.int32) * Q_BLOCK
    b_ix = jnp.arange(b)[:, None, None, None]
    h_ix = jnp.arange(h)[None, :, None, None]
    scale = 1.0 / math.sqrt(d)
    kpos_blk = jnp.arange(MOBA_BLOCK)

    def chunk(args):
        qch, t0 = args
        cur = t0 // MOBA_BLOCK
        gate = jnp.einsum('bhqd,bhnd->bhqn', qch.astype(jnp.float32), kmean)
        gate = jnp.where(jnp.arange(nblk) < cur, gate, -jnp.inf)
        _, sel = lax.top_k(gate, n_sel)
        kg = kb[b_ix, h_ix, sel]
        vg = vb[b_ix, h_ix, sel]
        k_own = lax.dynamic_slice_in_dim(kp, cur * MOBA_BLOCK, MOBA_BLOCK, axis=2)
        v_own = lax.dynamic_slice_in_dim(vp, cur * MOBA_BLOCK, MOBA_BLOCK, axis=2)
        s_sel = jnp.einsum('bhqd,bhqnkd->bhqnk', qch, kg).astype(jnp.float32) * scale
        s_sel = jnp.where((jnp.arange(n_sel) < cur)[:, None], s_sel, -jnp.inf)
        s_own = jnp.einsum('bhqd,bhkd->bhqk', qch, k_own).astype(jnp.float32) * scale
        qpos = t0 + jnp.arange(Q_BLOCK)
        s_own = jnp.where(cur * MOBA_BLOCK + kpos_blk[None, :] <= qpos[:, None], s_own, -jnp.inf)
        n_sk = n_sel * MOBA_BLOCK
        p = jax.nn.softmax(jnp.concatenate([s_sel.reshape(b, h, Q_BLOCK, n_sk), s_own], axis=-1), axis=-1)
        p_sel = p[..., :n_sk].reshape(b, h, Q_BLOCK, n_sel, MOBA_BLOCK).astype(v.dtype)
        p_own = p[..., n_sk:].astype(v.dtype)
        return (jnp.einsum('bhqnk,bhqnkd->bhqd', p_sel, vg)
                + jnp.einsum('bhqk,bhkd->bhqd', p_own, v_own))

    out = lax.map(chunk, (qc, starts))
    return out.transpose(1, 2, 0, 3, 4).reshape(b, h, s, d)

def _diff_attention(q, k, v, lam, subln_g, lambda_init):
    s = k.shape[-2]
    scale = 1.0 / math.sqrt(q.shape[-1])
    lf = lam.astype(jnp.float32)
    lam_val = jnp.exp(jnp.sum(lf[0] * lf[1])) - jnp.exp(jnp.sum(lf[2] * lf[3])) + lambda_init
    outs = []
    for t0 in range(0, s, Q_BLOCK):
        kl = t0 + Q_BLOCK
        sc = jnp.einsum('bhiqd,bhikd->bhiqk', q[:, :, :, t0:kl], k[:, :, :, :kl]).astype(jnp.float32) * scale
        causal = jnp.arange(kl)[None, :] <= (t0 + jnp.arange(Q_BLOCK))[:, None]
        p = jax.nn.softmax(jnp.where(causal, sc, -jnp.inf), axis=-1)
        a = p[:, :, 0] - lam_val * p[:, :, 1]
        outs.append(jnp.einsum('bhqk,bhkd->bhqd', a.astype(v.dtype), v[:, :, :kl]))
    o = _rmsnorm(jnp.concatenate(outs, axis=2), subln_g)
    return (o.astype(jnp.float32) * (1.0 - lambda_init)).astype(v.dtype)

def _stick_breaking(q, k, v):
    b, h, s, d = q.shape
    scale = 1.0 / math.sqrt(d)
    ar = jnp.arange(Q_BLOCK)
    tri = (ar[:, None] > ar[None, :]).astype(jnp.float32)
    outs = []
    for i, t0 in enumerate(range(0, s, Q_BLOCK)):
        nc = i + 1
        kl = nc * Q_BLOCK
        z = jnp.einsum('bhqd,bhkd->bhqk', q[:, :, t0:kl], k[:, :, :kl]).astype(jnp.float32) * scale
        before = jnp.arange(kl)[None, :] < (t0 + ar)[:, None]
        ln1m = jnp.where(before, jax.nn.log_sigmoid(-z), 0.0)
        ln1m_c = ln1m.reshape(b, h, Q_BLOCK, nc, Q_BLOCK)
        tri_c = (jnp.arange(nc)[:, None] > jnp.arange(nc)[None, :]).astype(jnp.float32)
        tail = (jnp.einsum('bhqcj,js->bhqcs', ln1m_c, tri)
                + jnp.einsum('bhqe,ec->bhqc', jnp.sum(ln1m_c, axis=-1), tri_c)[..., None])
        log_a = jnp.where(before, z + ln1m + tail.reshape(b, h, Q_BLOCK, kl), -jnp.inf)
        outs.append(jnp.einsum('bhqk,bhkd->bhqd', jnp.exp(log_a).astype(v.dtype), v[:, :, :kl]))
    return jnp.concatenate(outs, axis=2)

def second_inputs(seed: int = 0) -> dict:
    key = jax.random.key(seed)
    ks = jax.random.split(key, 8)
    x = jax.random.normal(ks[0], (BATCH, SEQ, D_MODEL), jnp.float32)
    norm_g = 1.0 + 0.02 * jax.random.normal(ks[1], (DEPTH, D_MODEL), jnp.float32)
    w_in = jax.random.normal(ks[2], (DEPTH, D_MODEL, N_IN_PARTS * BRANCH_W), jnp.float32) * D_MODEL ** -0.5
    w_out = jax.random.normal(ks[3], (DEPTH, MIX_WIDTH, D_MODEL), jnp.float32) * MIX_WIDTH ** -0.5
    diff_lam = 0.1 * jax.random.normal(ks[4], (N_ODD_2, 4, DIFF_HEAD_DIM), jnp.float32)
    diff_subln_g = 1.0 + 0.02 * jax.random.normal(ks[5], (N_ODD_2, HEAD_DIM), jnp.float32)
    final_norm_g = 1.0 + 0.02 * jax.random.normal(ks[6], (D_MODEL,), jnp.float32)
    return {"x": x, "norm_g": norm_g, "w_in": w_in, "w_out": w_out,
            "diff_lam": diff_lam, "diff_subln_g": diff_subln_g,
            "final_norm_g": final_norm_g}

def second_block(x, norm_g, w_in, w_out, diff_lam, diff_subln_g, final_norm_g):
    b, s, _ = x.shape
    pos = jnp.arange(s)
    for layer in range(DEPTH):
        h = _rmsnorm(x, norm_g[layer])
        proj = jnp.einsum('bsd,de->bse', h, w_in[layer])
        parts = jnp.split(proj, N_IN_PARTS, axis=-1)
        if layer % 2 == 0:
            qa, ka, va, ga, qb, kb, vb, gb = parts
            oa = _dilated_mixture(_rope(_heads(qa), pos), _rope(_heads(ka), pos), _heads(va))
            ob = _moba(_rope(_heads(qb), pos), _rope(_heads(kb), pos), _heads(vb))
            y = jnp.concatenate([_merge(oa) * jax.nn.silu(ga),
                                 _merge(ob) * jax.nn.silu(gb)], axis=-1)
        else:
            qc, kc, vc, gc, qd, kd, vd, gd = parts
            li = layer // 2
            lambda_init = 0.8 - 0.6 * math.exp(-0.3 * layer)
            split2 = lambda t: t.reshape(b, s, N_HEADS, 2, DIFF_HEAD_DIM).transpose(0, 2, 3, 1, 4)
            oc = _diff_attention(_rope(split2(qc), pos), _rope(split2(kc), pos), _heads(vc),
                                 diff_lam[li], diff_subln_g[li], lambda_init)
            od = _stick_breaking(_heads(qd), _heads(kd), _heads(vd))
            y = jnp.concatenate([_merge(oc) * jax.nn.silu(gc),
                                 _merge(od) * jax.nn.silu(gd)], axis=-1)
        x = x + jnp.einsum('bse,ed->bsd', y.astype(x.dtype), w_out[layer])
    return _rmsnorm(x, final_norm_g)


def setup_inputs(seed=0):
    out = dict(first_inputs(seed))
    for name, value in second_inputs(seed + 1).items():
        if name != "x":
            out[name + "_2"] = value
    return out


def reference(
    x, norm_g, ab_w_in, hgrn_lb_logits, gdn_conv_w, gdn_a_log, gdn_dt_bias, hgrn_norm_g,
    gdn_norm_g, ab_w_out, nsa_w_in, nsa_cmp_pos, nsa_cmp_w1, nsa_cmp_w2, nsa_w_out, ffn_w_gu,
    ffn_w_down, norm_g_2, w_in_2, w_out_2, diff_lam_2, diff_subln_g_2, final_norm_g_2,
):
    x = first_block(
        x, norm_g, ab_w_in, hgrn_lb_logits, gdn_conv_w, gdn_a_log, gdn_dt_bias, hgrn_norm_g,
        gdn_norm_g, ab_w_out, nsa_w_in, nsa_cmp_pos, nsa_cmp_w1, nsa_cmp_w2, nsa_w_out,
        ffn_w_gu, ffn_w_down,
    )
    return second_block(
        x, norm_g_2, w_in_2, w_out_2, diff_lam_2, diff_subln_g_2, final_norm_g_2,
    )


_drawn_inputs = setup_inputs


def setup_inputs(seed=0):
    import zlib

    import numpy as np

    out = dict(_drawn_inputs(seed))
    spreads = {}
    factors = {'norm_g_2': 8.0, 'diff_lam_2': 8.0, 'diff_subln_g_2': 50.02, 'final_norm_g_2': 8.061}
    for name, (base, spread) in spreads.items():
        noise = np.random.default_rng([zlib.crc32(name.encode()), seed]).standard_normal(out[name].shape)
        drawn = base * np.exp(spread * noise) if base else spread * noise
        out[name] = __import__('jax').numpy.asarray(drawn.astype(out[name].dtype))
    for name, factor in factors.items():
        out[name] = (out[name] * factor).astype(out[name].dtype)
    return out
```

```python
from contextlib import ExitStack

import numpy as np

import concourse.bass as bass
from concourse import mybir

F32 = mybir.dt.float32
F32R = mybir.dt.float32r
ALU = mybir.AluOpType
ACTF = mybir.ActivationFunctionType
AX = mybir.AxisListType.X

D = 2048
NKT = 16
DFF = 5632
SLOT = 1024
NRAW = 4
NW = 3
LEAD = 2
EPS = 1e-6
QSCALE = 128 ** -0.5
CHUNKS_EVEN = 8208
STAGE = 99


def constants():
    r = np.arange(128)[:, None]
    t = np.arange(128)[None, :]
    levels = [1, 2, 4, 8, 16, 32, 64]
    wc, mk = [], []
    for m in levels:
        same = (r // (2 * m)) == (t // (2 * m))
        mid = (t // (2 * m)) * 2 * m + m
        second = (t >= mid) & (r >= mid) & (r <= t)
        first = (t < mid) & (r > t) & (r < mid)
        wc.append((same & (second | first)).astype(np.float32))
        mk.append((same & (r < mid) & (t >= mid)).astype(np.float32))
    wc.append((r > t).astype(np.float32))
    wc.append((r <= t).astype(np.float32))
    mk.append((r == t).astype(np.float32))
    out = {
        "c_wc": np.concatenate(wc, 1),
        "c_mk": np.concatenate(mk, 1),
        "c_one": np.ones((128, 128), np.float32),
    }
    slope = 2.0 ** (-8.0 * np.arange(1, 5) / 16)
    tt = np.arange(256)
    db = []
    for i in range(2):
        nk = 128 * (i + 1)
        dist = tt[128 * i:128 * i + 128, None] - tt[None, :nk]
        dist = np.where(dist >= 0, dist, 1e32)
        db.append((-slope[None, :, None] * dist[:, None, :]).reshape(128, -1))
    out["c_db"] = np.concatenate(db, 1).astype(np.float32)
    cst = np.arange(15) * 16 + 31
    dc = tt[:, None] - cst[None, :]
    mc = (dc >= 0).astype(np.float32)
    dc = np.where(dc >= 0, dc, 1e32)
    dc4 = -slope[None, :, None] * dc[:, None, :]
    out["c_dc"] = np.concatenate([dc4[:128].reshape(128, -1), dc4[128:].reshape(128, -1)], 1).astype(np.float32)
    mc4 = np.repeat(mc[:, None, :], 4, 1)
    out["c_mc"] = np.concatenate([mc4[:128].reshape(128, -1), mc4[128:].reshape(128, -1)], 1)
    dist = tt[:, None] - tt[None, :]
    cnt = ((dist >= 0) & (dist <= 128)).astype(int) + ((dist >= 0) & (dist % 4 == 0)) + ((dist >= 0) & (dist % 16 == 0))
    lc = np.where(cnt > 0, np.log(np.maximum(cnt, 1)), -1e30).astype(np.float32)
    ca = np.where(dist >= 0, 0.0, -1e30).astype(np.float32)
    out["c_lc"] = np.concatenate([lc[:128, :128], lc[128:, :]], 1)
    out["c_ca"] = np.concatenate([ca[:128, :128], ca[128:, :]], 1)

    def rope(half):
        inv = np.float32(10000.0) ** (-np.arange(half, dtype=np.float32) / np.float32(half))
        ang = (tt.astype(np.float32)[:, None] * inv.astype(np.float32)[None, :]).astype(np.float64)
        cs = np.concatenate([np.cos(ang), np.sin(ang)], 1).astype(np.float32)
        return cs.reshape(2, 128, 2 * half).transpose(1, 0, 2).reshape(128, 4 * half)

    out["c_r32"] = rope(32)
    out["c_r16"] = rope(16)
    out["c_lt"] = (r < t).astype(np.float32)
    return {k: np.ascontiguousarray(v) for k, v in out.items()}


def tokens(after):
    out = []
    for a in after:
        if isinstance(a, list):
            out += tokens(a)
        elif a is not None:
            out.append(a)
    return out


class Queue:

    def __init__(self, sem):
        self.sem, self.items, self.count = sem, [], 0

    def __call__(self, fn, *after):
        self.count += 1
        self.items.append((fn, tokens(after), self.sem, 1))
        return (self.sem, self.count)

    def dma(self, fn, sem_count, *after):
        sem_count[1] += 16
        self.items.append((fn, tokens(after), sem_count[0], 16))
        return (sem_count[0], sem_count[1])

    def wait(self, *after):
        self.items.append((None, tokens(after), None, 0))

    def emit(self, eng):
        seen = {}

        for fn, after, sem, inc in self.items:
            need = {}
            for s, n in after:
                if n > max(seen.get(id(s), 0), need.get(id(s), (s, 0))[1]):
                    need[id(s)] = (s, n)
            for s, n in need.values():
                seen[id(s)] = n
                eng.wait_ge(s, n)
            if fn is not None:
                fn(eng).then_inc(sem, inc)


class Bank:

    def __init__(self, ap):
        self.ap, self.free = ap, []


def build(nc, A, out):
    with ExitStack() as ctx:
        def sb(name, n, dt=F32):
            return ctx.enter_context(nc.sbuf_tensor(name, [128, n], dt))

        def sem(name):
            return ctx.enter_context(nc.semaphore(name))

        H = sb("H", 2 * D)[:].rearrange("p (t n) -> p t n", t=2)
        UTH = sb("UTH", NKT * 256, F32R)[:].rearrange("p (k n) -> p k n", k=NKT)
        UTL = sb("UTL", NKT * 256, F32R)[:].rearrange("p (k n) -> p k n", k=NKT)
        RAW = [sb(f"RAW{i}", SLOT)[:] for i in range(NRAW)]
        WH = [sb(f"WH{i}", SLOT, F32R)[:] for i in range(NW)]
        WL = [sb(f"WL{i}", SLOT, F32R)[:] for i in range(NW)]
        XS = [(sb(f"XSH{i}", 256, F32R)[:], sb(f"XSL{i}", 256, F32R)[:]) for i in range(3)]
        BIG = sb("BIG", 2 * CHUNKS_EVEN)[:]
        WORK = sb("WORK", 7168)[:]
        GB = sb("GB", D)[:]
        WC = sb("WC", 9 * 128)[:]
        MK = sb("MK", 8 * 128)[:]
        ONE = sb("ONE", 128)[:]
        SM = sb("SM", 512)[:]
        GP = sb("GP", 96)[:].rearrange("p (v k) -> p v k", v=6)
        ident = MK[:, 896:1024]
        PRE = WC[:, 1024:1152]
        SUF = WC[:, 896:1024]
        PS = ctx.enter_context(nc.psum_tensor("PS", [128, 8, 512], F32))
        banks = [Bank(PS[:, i, :]) for i in range(8)]

        sPE, sACT, sDVE, sPOOL = sem("s_pe"), sem("s_act"), sem("s_dve"), sem("s_pool")
        PE, ACT, DVE, POOL, SP = Queue(sPE), Queue(sACT), Queue(sDVE), Queue(sPOOL), Queue(None)
        raw_sems = [[sem(f"s_raw{i}"), 0] for i in range(NRAW)]
        d_const = [sem("s_const"), 0]
        d_par = [[sem(f"s_par{i}"), 0] for i in range(4)]
        d_out = [sem("s_out"), 0]

        def mm(out_, pairs, start=True, stop=True):
            def fn(e):
                last = None
                for j, (l, r) in enumerate(pairs):
                    last = e.matmul(out_, l, r, start=start and j == 0, stop=stop and j == len(pairs) - 1)
                return last
            return fn

        def many(*fns):
            def fn(e):
                last = None
                for f in fns:
                    last = f(e)
                return last
            return fn

        def tr(out_, in_):
            p = in_.shape[0]
            return lambda e: e.transpose(out_, in_, ident[0:p, 0:p])

        def copy(o, i, scale=1.0):
            return lambda e: e.activation(o, i, ACTF.Copy, scale=scale)

        def act(o, i, f, **k):
            return lambda e: e.activation(o, i, f, **k)

        def tt(o, a, b, op):
            return lambda e: e.tensor_tensor(o, a, b, op)

        def ts(o, a, s1, s2, op0, op1=None):
            if op1 is None:
                return lambda e: e.tensor_scalar(o, a, s1, None, op0)
            return lambda e: e.tensor_scalar(o, a, s1, s2, op0, op1)

        def stt(o, a, s, b, op0, op1):
            return lambda e: e.scalar_tensor_tensor(out=o, in0=a, scalar=s, in1=b, op0=op0, op1=op1)

        def cp(o, i):
            return lambda e: e.tensor_copy(o, i)

        def red(o, i, op):
            return lambda e: e.tensor_reduce(o, i, AX, op)

        def bc(ap, n):
            return ap.unsqueeze(2).to_broadcast([ap.shape[0], ap.shape[1], n])

        def rep(ap, n):
            return ap.unsqueeze(1).to_broadcast([ap.shape[0], n, ap.shape[1]])

        def v3(ap, a):
            return ap.rearrange("p (a b) -> p a b", a=a)

        t_const = None
        for dst, name in ((WC, "c_wc"), (MK, "c_mk"), (ONE, "c_one")):
            t_const = SP.dma(lambda e, d=dst, n=name: e.dma_start(d, A[n]), d_const)
        t_const = SP.dma(lambda e: e.dma_start(GP, A["g_pre"]), d_const)
        t_const = SP.dma(lambda e: e.dma_start(H, A["x"].rearrange("o (t p) n -> p (o t) n", p=128)), d_const)

        stream = []

        def add_cols(w, n0, n1, ktiles=NKT):
            wd = n1 - n0
            kk = min(ktiles, SLOT // 512 if wd > 64 else SLOT // wd)
            for k in range(0, ktiles, kk):
                src = w[128 * k:128 * (k + kk), n0:n1].rearrange("(k p) n -> p k n", p=128)
                stream.append((src, kk, wd))

        def add_rows(w, ktiles):
            for k in range(ktiles):
                for hf in range(2):
                    stream.append((w[128 * k:128 * k + 128, 1024 * hf:1024 * hf + 1024].unsqueeze(1), 1, 1024))

        def cuts(n):
            return [(a, min(a + 512, n)) for a in range(0, n, 512)]

        order_even = [(8192, 8208)] + [(a, a + 512) for a in
                                       (4096, 5120, 6144, 7168, 4608, 5632, 6656, 7680,
                                        1024, 0, 2048, 3072, 1536, 512, 2560, 3584)]
        for a, b in order_even:
            add_cols(A["ab_w_in"][0], a, b)
        add_rows(A["ab_w_out"][0], 16)

        def add_ffn(l):
            for c in range(11):
                add_cols(A["ffn_w_gu"][l], 512 * c, 512 * c + 512)
                add_cols(A["ffn_w_gu"][l], DFF + 512 * c, DFF + 512 * c + 512)
            add_rows(A["ffn_w_down"][l], 44)

        add_ffn(0)
        for a, b in cuts(5168):
            add_cols(A["nsa_w_in"][0], a, b)
        add_rows(A["nsa_w_out"][0], 16)
        add_ffn(1)
        for l in range(2):
            for a, b in cuts(2048):
                add_cols(A["w_in_2"][l], a, b)
            add_rows(A["w_out_2"][l], 4)

        hi_tok, lo_tok, used_tok = {}, {}, {}
        state = {"dma": 0, "prep": 0, "use": 0}

        def load(i):
            src, kk, wd = stream[i]
            dst = v3(RAW[i % NRAW][:, 0:kk * wd], kk)
            SP_tok = SP.dma(lambda e: e.dma_start(dst, src), raw_sems[i % NRAW],
                            hi_tok.get(i - NRAW), lo_tok.get(i - NRAW))
            return SP_tok

        raw_tok = {}

        def prep(upto):
            while state["prep"] <= min(upto, len(stream) - 1):
                i = state["prep"]
                while state["dma"] < min(i + NRAW, len(stream)):
                    raw_tok[state["dma"]] = load(state["dma"])
                    state["dma"] += 1
                n = stream[i][1] * stream[i][2]
                raw, wh, wl = (x[:, 0:n] for x in (RAW[i % NRAW], WH[i % NW], WL[i % NW]))
                hi_tok[i] = ACT(copy(wh, raw), raw_tok[i], used_tok.get(i - NW))
                lo_tok[i] = DVE(tt(wl, raw, wh.bitcast(F32), ALU.subtract), hi_tok[i], used_tok.get(i - NW))
                state["prep"] += 1

        def next_slot():
            i = state["use"]
            state["use"] += 1
            prep(i + LEAD)
            kk, wd = stream[i][1:]
            return i, v3(WH[i % NW][:, 0:kk * wd], kk), v3(WL[i % NW][:, 0:kk * wd], kk)

        def use_cols(widths, xh, xl, after, sink, ktiles=NKT):
            for c, wd in enumerate(widths):
                pair = [banks[2 * (c % 2) + t] for t in range(2)]
                k = 0
                while k < ktiles:
                    i, wh, wl = next_slot()
                    kk = stream[i][1]
                    fns = []
                    for j in range(kk):
                        for t in range(2):
                            o = pair[t].ap[:, 0:wd]
                            lh, ll = xh[:, k + j, 128 * t:128 * t + 128], xl[:, k + j, 128 * t:128 * t + 128]
                            fns.append(mm(o, [(lh, wh[:, j]), (lh, wl[:, j]), (ll, wh[:, j])],
                                          start=k + j == 0, stop=k + j == ktiles - 1))
                    used_tok[i] = PE(many(*fns), hi_tok[i], lo_tok[i], after, pair[0].free, pair[1].free)
                    k += kk
                    if k < ktiles:
                        yield
                for t in range(2):
                    pair[t].free = [sink(c, t, pair[t].ap[:, 0:wd], used_tok[i])]
                yield

        def use_rows(ktiles, operand, after):
            busy = [b.free for b in banks]
            for k in range(ktiles):
                xh, xl, ready = operand(k)
                for hf in range(2):
                    i, wh, wl = next_slot()
                    fns = []
                    for t in range(2):
                        for n in range(2):
                            o = banks[4 * t + 2 * hf + n].ap
                            cs = slice(512 * n, 512 * n + 512)
                            lh, ll = xh[:, 128 * t:128 * t + 128], xl[:, 128 * t:128 * t + 128]
                            fns.append(mm(o, [(lh, wh[:, 0, cs]), (lh, wl[:, 0, cs]), (ll, wh[:, 0, cs])],
                                          start=k == 0, stop=k == ktiles - 1))
                    used_tok[i] = PE(many(*fns), hi_tok[i], lo_tok[i], after, ready, busy)
                yield used_tok[i]

        ring = {"n": 0}

        def bank():
            ring["n"] += 1
            return banks[4 + ring["n"] % 4]

        def drain(g):
            last = None
            for x in g:
                last = x if x is not None else last
            return last

        def together(main, side, per=1):
            for _ in main:
                for _ in range(per):
                    next(side, None)
            drain(side)

        def to_T(src, tiles, after, gain=None):
            toks = []
            for k in range(0, tiles, 2):
                b = bank()
                fns = [tr(b.ap[:, 256 * j + 128 * t:256 * j + 128 * t + 128], src(k + j, t))
                       for j in range(2) for t in range(2)]
                p = PE(many(*fns), after, b.free, t_const)
                b.free = []
                gs = [1.0 if gain is None else gain[:, k + j:k + j + 1] for j in range(2)]
                for j in range(2):
                    hi = ACT(copy(UTH[:, k + j], b.ap[:, 256 * j:256 * j + 256], gs[j]), p)
                for j in range(2):
                    lo = DVE(stt(UTL[:, k + j], b.ap[:, 256 * j:256 * j + 256], gs[j],
                                 UTH[:, k + j].bitcast(F32), ALU.mult, ALU.subtract), hi)
                b.free = [lo]
                toks = [hi, lo]
            return toks

        RSQ = sb("RSQ", 16 * 12)[:]
        rsq = {"n": 0, "free": [None] * 16}

        def rstd(o, ss, n, after, gain=1.0):
            j = rsq["n"] % 16
            rsq["n"] += 1
            w = ss.shape[1]
            x, y, z = (RSQ[:, 12 * j + 4 * i:12 * j + 4 * i + w] for i in range(3))
            a = DVE(ts(x, ss, 1.0 / n, EPS, ALU.mult, ALU.add), after, rsq["free"][j])
            b = ACT(act(y, x, ACTF.Ln), a)
            b = ACT(act(y, y, ACTF.Exp, scale=-0.5), b)
            a = DVE(tt(z, y, y, ALU.mult), b)
            a = DVE(tt(z, z, x, ALU.mult), a)
            a = DVE(ts(z, z, -0.5 * gain, 1.5 * gain, ALU.mult, ALU.add), a)
            a = DVE(tt(o, y, z, ALU.mult), a)
            rsq["free"][j] = a
            return a

        def rec(o, i):
            return lambda e: e.reciprocal(o, i)

        def sigm(e_, after):
            a = DVE(ts(e_, e_, 1.0, None, ALU.add), after)
            return DVE(rec(e_, e_), a)

        def pre_norm(gain, after):
            tmp = v3(BIG[:, 0:4096], 2)
            toks = []
            for t in range(2):
                a = ACT(act(BIG[:, 4096 + D * t:4096 + D * t + D], H[:, t], ACTF.Square,
                            accum_out=SM[:, t:t + 1]), after)
                r = rstd(SM[:, 2 + t:3 + t], SM[:, t:t + 1], D, a)
                toks.append(DVE(ts(tmp[:, t], H[:, t], SM[:, 2 + t:3 + t], None, ALU.mult), r))
            return to_T(lambda k, t: tmp[:, t, 128 * k:128 * k + 128], NKT, toks, gain)

        def load_gb(row, n, after):
            return POOL.dma(lambda e: e.dma_start(GB, row.partition_broadcast(128)), d_par[n], after)

        def post_norm(t_gb, after):
            junk = WORK[:, 0:512]
            sq = []
            for t in range(2):
                for n in range(4):
                    sq.append(ACT(act(junk, banks[4 * t + n].ap, ACTF.Square,
                                      accum_out=SM[:, 8 + 4 * t + n:9 + 4 * t + n]), after, sq))
            a = DVE(red(SM[:, 16:18], v3(SM[:, 8:16], 2), ALU.add), sq)
            r = rstd(SM[:, 18:20], SM[:, 16:18], D, a)
            adds = []
            for t in range(2):
                for n in range(4):
                    j = 4 * t + n
                    tmp = WORK[:, 512 + 512 * (j % 4):1024 + 512 * (j % 4)]
                    m = DVE(stt(tmp, banks[j].ap, SM[:, 18 + t:19 + t], GB[:, 512 * n:512 * n + 512],
                                ALU.mult, ALU.mult), r, t_gb, adds[j - 4] if j >= 4 else None)
                    banks[j].free = [m]
                    h = H[:, t, 512 * n:512 * n + 512]
                    adds.append(POOL(tt(h, h, tmp, ALU.add), m))
            return adds

        def plain_add(after):
            toks = []
            for t in range(2):
                for n in range(4):
                    h = H[:, t, 512 * n:512 * n + 512]
                    m = DVE(tt(h, banks[4 * t + n].ap, h, ALU.add), after)
                    banks[4 * t + n].free = [m]
                    toks.append(m)
            return toks

        def finish(after):
            o = out.rearrange("o (t p) n -> p (o t) n", p=128)
            SP.dma(lambda e: e.dma_start(o, H), d_out, after)
            SP.wait((d_out[0], d_out[1]))

        def ffn(l, row, gain, after):
            u = pre_norm(gain, after)
            t_gb = load_gb(row, 0, after)
            HT = BIG[:, 0:44 * 256].rearrange("p (k n) -> p k n", k=44)
            G = [[BIG[:, 11264 + 1024 * x + 512 * t:11264 + 1024 * x + 512 * t + 512] for t in range(2)]
                 for x in range(4)]
            gate_tok, trs_tok, ht_tok = {}, {}, []

            def sink(c, t, ap, tok):
                x = (c // 2) % 2
                g = G[x][t]
                if c % 2 == 0:
                    gate_tok[t] = ACT(act(g, ap, ACTF.Silu), tok, trs_tok.get((x, t)))
                    return gate_tok[t]
                f = DVE(tt(g, ap, g, ALU.mult), tok, gate_tok[t])
                b = bank()
                fns = [tr(b.ap[:, 128 * j:128 * j + 128], g[:, 128 * j:128 * j + 128]) for j in range(4)]
                p = PE(many(*fns), f, b.free)
                trs_tok[(x, t)] = p
                k = 4 * (c // 2)
                e = ACT(copy(HT[:, k:k + 4, 128 * t:128 * t + 128], v3(b.ap, 4)), p)
                b.free = [e]
                ht_tok.append(e)
                return f

            drain(use_cols([512] * 22, UTH, UTL, u, sink))

            used = {}

            def operand(k):
                xh, xl = XS[k % 3]
                hi = ACT(copy(xh, HT[:, k]), ht_tok, used.get(k - 3))
                lo = DVE(tt(xl, HT[:, k], xh.bitcast(F32), ALU.subtract), hi, used.get(k - 3))
                return xh, xl, [hi, lo]

            pending = {0: operand(0), 1: operand(1)}

            def ahead(k):
                return pending[k]

            last = None
            for k, last in enumerate(use_rows(44, ahead, None)):
                used[k] = last
                if k + 2 < 44:
                    pending[k + 2] = operand(k + 2)
            return post_norm(t_gb, last)

        Z = v3(BIG, 2)

        def zcol(t, c, n):
            return Z[:, t, c:c + n]

        zt = {}

        def z_sink_even(c, t, ap, tok):
            a, b = order_even[c]
            zt[(a, t)] = ACT(copy(zcol(t, a, b - a), ap), tok)
            return zt[(a, t)]

        SMG = SM[:, 32:512]
        LD = v3(SMG[:, 0:16], 2)
        BETA = v3(SMG[:, 16:32], 2)
        EG = v3(SMG[:, 32:80], 2)
        TMP = SMG[:, 80:176]
        DTB, NEA = SMG[:, 176:184], SMG[:, 184:192]
        HG = sb("HG", 128)[:]
        DG = sb("DG", 128)[:]
        CW = sb("CW", 96)[:].rearrange("p (c j) -> p c j", j=4)
        for dst, src in ((DTB, A["gdn_dt_bias"][0:1]), (NEA, A["gdn_a_log"][0:1]),
                         (HG, A["hgrn_norm_g"][0:1]), (DG, A["gdn_norm_g"][0:1])):
            t_const = SP.dma(lambda e, d=dst, s=src: e.dma_start(d, s[0].partition_broadcast(128)), d_const)
        t_const = SP.dma(lambda e: e.dma_start(CW, A["conv_w"]), d_const)
        ones_act = ACT(copy(SM[:, 30:31], ONE[:, 0:1]), t_const)
        one_b = SM[:, 30:31]

        def gdn_gates():
            ba = Z[:, :, 8192:8200]
            bb = Z[:, :, 8200:8208]
            z = [zt[(8192, 0)], zt[(8192, 1)]]
            x, ax, e1, l1 = (v3(TMP[:, 16 * j:16 * j + 16], 2) for j in range(4))
            a = DVE(tt(x, ba, rep(DTB, 2), ALU.add), z, t_const)
            b = ACT(act(ax, x, ACTF.Abs), a)
            b = ACT(act(e1, ax, ACTF.Exp, scale=-1.0), b)
            b = ACT(act(l1, e1, ACTF.Ln, bias=one_b), b, ones_act)
            c = DVE(stt(x, x, 0.0, l1, ALU.max, ALU.add), b)
            n = ACT(act(NEA, NEA, ACTF.Exp), t_const)
            n = DVE(ts(NEA, NEA, -1.0, None, ALU.mult), n)
            ld = DVE(tt(LD, x, rep(NEA, 2), ALU.mult), c, n)
            s = ACT(act(e1, bb, ACTF.Exp, scale=-1.0), z, c)
            beta = DVE(ts(e1, e1, 1.0, None, ALU.add), s)
            beta = DVE(rec(BETA, e1), beta)
            yield
            b_ = bank()
            fns = []
            for i in range(2):
                for j, m in enumerate((PRE, SUF, ONE)):
                    fns.append(mm(b_.ap[:, 24 * i + 8 * j:24 * i + 8 * j + 8], [(m, LD[:, i])]))
            p = PE(many(*fns), ld, b_.free)
            eg = ACT(act(EG, v3(b_.ap[:, 0:48], 2), ACTF.Exp), p)
            b_.free = [eg]
            zt["gates"] = [ld, beta, eg]
            yield

        def w3(o, n, a):
            return v3(WORK[:, o:o + n], a)

        def silu_parts(dst, e_, src, after):
            a = ACT(act(e_, src, ACTF.Exp, scale=-1.0), after)
            b = sigm(e_, a)
            return DVE(tt(dst, e_, src, ALU.mult), b)

        done = {"work": []}

        def conv_half(hf):
            F = [w3(0, 1024, 4), w3(1024, 1024, 4)]
            E = [w3(2048, 1024, 4), w3(3072, 1024, 4)]
            last = {}
            for part, c0 in enumerate((4096, 5120, 6144)):
                f, e_ = F[part % 2], E[part % 2]
                z = [zt[(c0 + 512 * hf, t)] for t in range(2)]
                taps = []
                trs = []
                for pr in range(2):
                    b = bank()
                    fns = [tr(b.ap[:, 256 * j + 128 * t:256 * j + 128 * t + 128],
                              zcol(t, c0 + 512 * hf + 256 * pr + 128 * j, 128)) for j in range(2) for t in range(2)]
                    p = PE(many(*fns), z, b.free)
                    trs.append(p)
                    rd = []
                    for j in range(2):
                        ch = 8 * part + 4 * hf + 2 * pr + j
                        k0 = ACT(copy(f[:, 2 * pr + j], b.ap[:, 256 * j:256 * j + 256], CW[:, ch, 3:4]),
                                 p, last.get(part - 2), done["work"], t_const)
                    for j in range(2):
                        h = 2 * pr + j
                        ch = 8 * part + 4 * hf + h
                        k = k0
                        for d in range(1, 4):
                            k = DVE(stt(f[:, h, d:256], b.ap[:, 256 * j:256 * j + 256 - d], CW[:, ch, 3 - d:4 - d],
                                        f[:, h, d:256], ALU.mult, ALU.add), k)
                        rd.append(k)
                    b.free = rd
                    taps += rd
                    yield
                s = silu_parts(f, e_, f, [taps, last.get(part - 2), done["work"]])
                yield
                reads = []
                for t in range(2):
                    b = bank()
                    p = PE(many(*[tr(b.ap[:, 128 * j:128 * j + 128], f[:, j, 128 * t:128 * t + 128])
                                  for j in range(4)]), s, b.free)
                    reads.append(p)
                    dst = zcol(t, c0 + 512 * hf, 512)
                    if part == 2:
                        w = ACT(copy(dst, b.ap), p, trs)
                        b.free = [w]
                    else:
                        sq = ACT(act(e_[:, 2 * t:2 * t + 2], b.ap, ACTF.Square), p, s)
                        ss = TMP[:, 4 * t + 8 * part:4 * t + 8 * part + 4]
                        r = DVE(red(ss, e_[:, 2 * t:2 * t + 2].rearrange("p a (b c) -> p (a b) c", b=2), ALU.add), sq)
                        r = rstd(ss, ss, 1, r, QSCALE if part == 0 else 1.0)
                        w = DVE(tt(v3(dst, 4), v3(b.ap, 4), bc(ss, 128), ALU.mult), r, trs)
                        b.free = [w]
                        reads.append(r)
                    zt[("n", part, hf, t)] = w
                    yield
                last[part] = reads
            done["work"] = [last[p] for p in range(3)] + [zt[("n", p, hf, t)] for p in range(3) for t in range(2)]

        def gdn_group(hf, i, carry):
            ld, beta, eg = zt["gates"]
            free = done["work"]
            hs = range(4)
            ADEC, DEC, KB, KT = (w3(512 * j, 512, 4) for j in range(4))
            KBT, QT, LT, QK = (w3(2048 + 512 * j, 512, 4) for j in range(4))
            XX = WORK[:, 4096:5120].rearrange("p (h x n) -> p h x n", h=4, x=2)
            Y, LTM = w3(5120, 512, 4), w3(5632, 512, 4)
            S = w3(6144, 512, 4)
            RV, RW = ADEC, DEC
            qz, kz, vz = (v3(zcol(i, c + 512 * hf, 512), 4) for c in (4096, 5120, 6144))
            tq, tk, tv = (zt[("n", p, hf, i)] for p in range(3))
            hsl = slice(4 * hf, 4 * hf + 4)
            a = POOL(tt(ADEC, rep(SUF, 4), bc(LD[:, i, hsl], 128), ALU.mult), ld, free)
            kb = DVE(tt(KB, kz, bc(BETA[:, i, hsl], 128), ALU.mult), beta, tk, free)
            x0 = POOL(cp(XX[:, :, 0], rep(ident, 4)), free)
            x1 = POOL(cp(XX[:, :, 1], rep(ident, 4)), free)
            yield
            b = bank()
            p = PE(many(*[mm(b.ap[:, 128 * h:128 * h + 128], [(ADEC[:, h], PRE)]) for h in hs]), a, b.free)
            dec = ACT(act(DEC, v3(b.ap, 4), ACTF.Exp), p, free)
            b.free = [dec]
            toks = []
            for src, dst, tok, eng in ((kz, KT, tk, 0), (KB, KBT, kb, 1), (qz, QT, tq, 0)):
                b = bank()
                p = PE(many(*[tr(b.ap[:, 128 * h:128 * h + 128], src[:, h]) for h in hs]), tok, b.free)
                if eng:
                    w = DVE(cp(dst, v3(b.ap, 4)), p, free)
                else:
                    w = ACT(copy(dst, v3(b.ap, 4)), p, free)
                b.free = [w]
                toks.append(w)
            tkT, tkbT, tqT = toks
            yield
            b = bank()
            p = PE(many(*[mm(b.ap[:, 128 * h:128 * h + 128], [(KT[:, h], KBT[:, h])]) for h in hs]), tkT, tkbT, b.free)
            lt = DVE(tt(LT, v3(b.ap, 4), DEC, ALU.mult), p, dec, free)
            b.free = [lt]
            b = bank()
            p = PE(many(*[mm(b.ap[:, 128 * h:128 * h + 128], [(KT[:, h], QT[:, h])]) for h in hs]), tqT, b.free)
            qk0 = DVE(tt(QK, v3(b.ap, 4), DEC, ALU.mult), p, free)
            b.free = [qk0]
            qk = POOL(tt(QK, QK, rep(PRE, 4), ALU.mult), qk0)
            yield
            xx = [x0, x1]
            py = None
            for l in range(7):
                m = POOL(tt(LTM, LT, rep(MK[:, 128 * l:128 * l + 128], 4), ALU.mult), lt, py)
                b = bank()
                py = PE(many(*[mm(b.ap[:, 128 * h:128 * h + 128], [(LTM[:, h], XX[:, h, 0])]) for h in hs]),
                        m, xx, b.free)
                y = ACT(copy(Y, v3(b.ap, 4)), py)
                b.free = [y]
                yield
                b0, b1 = bank(), bank()
                fns = []
                for h in hs:
                    bb = (b0, b1)[h // 2].ap[:, 256 * (h % 2):256 * (h % 2) + 256]
                    fns.append(mm(bb[:, 0:128], [(XX[:, h, 1], Y[:, h])]))
                    fns.append(mm(bb[:, 128:256], [(Y[:, h], XX[:, h, 1])]))
                p = PE(many(*fns), y, b0.free, b1.free)
                xx = []
                for j, bb in enumerate((b0, b1)):
                    o = XX[:, 2 * j:2 * j + 2].rearrange("p h x n -> p (h x n)")
                    u = DVE(tt(o, o, bb.ap, ALU.subtract), p)
                    bb.free = [u]
                    xx.append(u)
                yield
            rv = DVE(tt(RV, vz, bc(BETA[:, i, hsl], 128), ALU.mult), tv, dec, qk0)
            bu = bank()
            pu = PE(many(*[mm(bu.ap[:, 128 * h:128 * h + 128], [(XX[:, h, 1], RV[:, h])]) for h in hs]),
                    rv, xx, bu.free)
            U = KB
            if i == 0:
                u = ACT(copy(U, v3(bu.ap, 4)), pu, tkbT)
                bu.free = [u]
                KD = RW
                kd = POOL(tt(KD, kz, bc(EG[:, i, 8 + 4 * hf:12 + 4 * hf], 128), ALU.mult), eg, lt, qk0)
                yield
                bs = bank()
                ps = PE(many(*[mm(bs.ap[:, 128 * h:128 * h + 128], [(KD[:, h], U[:, h])]) for h in hs]),
                        u, kd, bs.free)
                s = DVE(cp(S, v3(bs.ap, 4)), ps, free)
                bs.free = [s]
                bo = bank()
                po = PE(many(*[mm(bo.ap[:, 128 * h:128 * h + 128], [(QK[:, h], U[:, h])]) for h in hs]), qk, u, bo.free)
                carry["s"] = s
                used = [po, ps]
            else:
                rw = POOL(tt(RW, KB, bc(EG[:, i, hsl], 128), ALU.mult), eg, lt, qk0)
                bw = bank()
                pw = PE(many(*[mm(bw.ap[:, 128 * h:128 * h + 128], [(RW[:, h], XX[:, h, 1])]) for h in hs]),
                        rw, bw.free)
                WT = KBT
                wt = ACT(copy(WT, v3(bw.ap, 4)), pw)
                bw.free = [wt]
                QE = Y
                qe = POOL(tt(QE, qz, bc(EG[:, i, hsl], 128), ALU.mult), eg, tq, xx)
                u0 = ACT(copy(U, v3(bu.ap, 4)), pu, rw, tkbT)
                bu.free = [u0]
                yield
                bs = bank()
                ps = PE(many(*[mm(bs.ap[:, 128 * h:128 * h + 128], [(WT[:, h], S[:, h])]) for h in hs]),
                        wt, carry["s"], bs.free)
                u = DVE(tt(U, U, v3(bs.ap, 4), ALU.subtract), ps, u0)
                bs.free = [u]
                bq = bank()
                pq = PE(many(*[tr(bq.ap[:, 128 * h:128 * h + 128], QE[:, h]) for h in hs]), qe, bq.free)
                qt = ACT(copy(QT, v3(bq.ap, 4)), pq)
                bq.free = [qt]
                yield
                bo = bank()
                po = PE(many(*[mm(bo.ap[:, 128 * h:128 * h + 128], [(QT[:, h], S[:, h]), (QK[:, h], U[:, h])])
                               for h in hs]), qt, u, qk, bo.free)
                used = [po]
            w = ACT(copy(zcol(i, 4096 + 512 * hf, 512), bo.ap), po, tqT, used)
            bo.free = [w]
            zt[("ob", hf, i)] = w
            done["work"] = [used, w]
            yield

        def out_gate(o, g, gain, to, tg, key, base, cmax=0):
            o3, g3 = v3(o, 4), v3(g, 4)
            e_ = w3(base, 512, 4)
            ss = TMP[:, 64 + 4 * (base // 512 % 4):68 + 4 * (base // 512 % 4)]
            a = POOL(tt(e_, o3, o3, ALU.mult), to, done["work"])
            a = DVE(red(ss, e_, ALU.add), a)
            r = rstd(ss, ss, 128, a)
            m = DVE(tt(o3, o3, bc(ss, 128), ALU.mult), r)
            m = POOL(tt(o3, o3, rep(gain, 4), ALU.mult), m)
            e = ACT(act(e_, g3, ACTF.Exp, scale=-1.0), tg, a)
            e = sigm(e_, e)
            e = POOL(tt(e_, e_, g3, ALU.mult), e)
            zt[key] = POOL(tt(o3, o3, e_, ALU.mult), e, m)
            return zt[key]

        def gdn():
            yield from gdn_gates()
            for hf in range(2):
                yield from conv_half(hf)
                carry = {}
                for i in range(2):
                    yield from gdn_group(hf, i, carry)
                ends = []
                for i in range(2):
                    ends.append(out_gate(zcol(i, 4096 + 512 * hf, 512), zcol(i, 7168 + 512 * hf, 512), DG,
                                         zt[("ob", hf, i)], zt[(7168 + 512 * hf, i)], ("o", 1, hf, i), 512 * i))
                    yield
                done["work"] = ends

        def hgrn():
            for hf in range(2):
                KK = w3(0, 1024, 2)
                L1 = w3(1024, 1024, 2)
                x = Z[:, :, 1024 + 512 * hf:1536 + 512 * hf]
                tz = [zt[(1024 + 512 * hf, t)] for t in range(2)]
                a = ACT(act(L1, x, ACTF.Abs), tz, done["work"])
                a = ACT(act(L1, L1, ACTF.Exp, scale=-1.0), a)
                a = ACT(act(L1, L1, ACTF.Ln, bias=one_b), a)
                k0 = DVE(stt(KK, x, 0.0, L1, ALU.max, ALU.add), a, done["work"])
                lf = DVE(stt(x, x, 0.0, L1, ALU.min, ALU.subtract), a, k0)
                kk = ACT(act(KK, KK, ACTF.Exp, scale=-1.0), k0)
                yield
                o0 = 1024
                QKT = [w3(o0 + 256 * j, 256, 2) for j in range(2)]
                E = [w3(o0 + 512 + 512 * j, 512, 4) for j in range(2)]
                QE = [w3(o0 + 1536 + 512 * j, 512, 4) for j in range(2)]
                KE = [w3(o0 + 2560 + 512 * j, 512, 4) for j in range(2)]
                KE7 = WORK[:, o0 + 3584:o0 + 3712]
                ATM = w3(o0 + 3712, 1024, 8)
                AT = [WORK[:, o0 + 4736 + 128 * j:o0 + 4864 + 128 * j] for j in range(4)]
                start = [lf, done["work"]]
                fr = {"qk": [start, start], "e": [start, start], "s": [start, start], "atm": start,
                      "at": [start] * 4, "ke7": start}
                ends = []
                for h in range(4):
                    for i in range(2):
                        n = 2 * h + i
                        cq = 512 * hf + 128 * h
                        qk_ = QKT[n % 2]
                        b = bank()
                        p = PE(many(tr(b.ap[:, 0:128], zcol(i, cq, 128)),
                                    tr(b.ap[:, 128:256], KK[:, i, 128 * h:128 * h + 128])),
                               zt[(512 * hf, i)], kk, b.free)
                        tqk = ACT(copy(qk_, v3(b.ap[:, 0:256], 2)), p, fr["qk"][n % 2])
                        b.free = [tqk]
                        pref = zcol(i, 1024 + cq, 128)
                        es = []
                        for g in range(2):
                            b = bank()
                            if g == 1 and i == 1:
                                f = many(mm(b.ap[:, 0:384], [(pref, WC[:, 512:896])]),
                                         mm(b.ap[:, 384:512], [(pref, PRE)]))
                            else:
                                f = mm(b.ap, [(pref, WC[:, 512 * g:512 * g + 512])])
                            p = PE(f, lf, b.free)
                            e = ACT(act(E[g], v3(b.ap, 4), ACTF.Exp), p, fr["e"][g])
                            b.free = [e]
                            es.append(e)
                        yield
                        qT, kT = qk_[:, 0], qk_[:, 1]
                        at = []
                        for g in range(2):
                            qe = DVE(tt(QE[g], E[g], rep(qT, 4), ALU.mult), es[g], tqk, fr["s"][g])
                            if g == 1 and i == 0:
                                ke = POOL(tt(KE[g][:, 0:3], E[g][:, 0:3], rep(kT, 3), ALU.mult), es[g], tqk, fr["s"][g])
                                k7 = POOL(tt(KE7, E[g][:, 3], kT, ALU.mult), es[g], tqk, fr["ke7"])
                            else:
                                ke = POOL(tt(KE[g], E[g], rep(kT, 4), ALU.mult), es[g], tqk, fr["s"][g])
                                if g == 0:
                                    pass
                            fr["e"][g] = [qe, ke, k7] if (g == 1 and i == 0) else [qe, ke]
                            b = bank()
                            fns = [mm(b.ap[:, 128 * l:128 * l + 128], [(KE[g][:, l], QE[g][:, l])])
                                   for l in range(4 - g)]
                            if g == 1:
                                fns.append(mm(b.ap[:, 384:512], [(kT, qT)]))
                            p = PE(many(*fns), qe, ke, b.free)
                            mtok = DVE(tt(ATM[:, 4 * g:4 * g + 4].rearrange("p a b -> p (a b)"), b.ap,
                                          MK[:, 512 * g:512 * g + 512], ALU.mult), p, fr["atm"])
                            b.free = [mtok]
                            fr["s"][g] = [p]
                            at.append(mtok)
                        yield
                        ra = DVE(red(AT[n % 2], ATM.rearrange("p l t -> p t l"), ALU.add), at, fr["at"][n % 2])
                        fr["atm"] = [ra]
                        toks = [ra]
                        v = zcol(i, 2048 + cq, 128)
                        pairs = [(AT[n % 2], v)]
                        if i == 1:
                            b = bank()
                            p = PE(mm(b.ap[:, 0:128], [(KE7, QE[1][:, 3])]), k7, b.free)
                            fr["ke7"] = [p]
                            fr["s"][1] = [p]
                            c7 = ACT(copy(AT[2 + h % 2], b.ap[:, 0:128]), p, fr["at"][2 + h % 2])
                            b.free = [c7]
                            pairs.append((AT[2 + h % 2], zcol(0, 2048 + cq, 128)))
                            toks.append(c7)
                        yield
                        b = bank()
                        p = PE(mm(b.ap[:, 0:128], pairs), toks, zt[(2048 + 512 * hf, 0)], zt[(2048 + 512 * hf, 1)], b.free)
                        fr["at"][n % 2] = [p]
                        if i == 1:
                            fr["at"][2 + h % 2] = [p]
                        fr["qk"][n % 2] = [p, qe, ke]
                        w = ACT(copy(zcol(i, cq, 128), b.ap[:, 0:128]), p)
                        b.free = [w]
                        zt[("oa", hf, i)] = w
                        ends.append(w)
                        yield
                done["work"] = [ends, p]
                gs = []
                for i in range(2):
                    gs.append(out_gate(zcol(i, 512 * hf, 512), zcol(i, 3072 + 512 * hf, 512), HG, ends,
                                       zt[(3072 + 512 * hf, i)], ("o", 0, hf, i), 512 * i))
                    yield
                done["work"] = gs

        ZN = v3(BIG[:, 0:2 * 5168], 2)
        SP0 = 2 * 5168

        def nsa_sink(c, t, ap, tok):
            a, b = cuts(5168)[c]
            zt[("nsa", c, t)] = ACT(copy(ZN[:, t, a:b], ap), tok)
            return zt[("nsa", c, t)]

        def nsa(tables):
            z = {c: [zt[("nsa", c, t)] for t in range(2)] for c in range(11)}
            W1 = BIG[:, SP0:SP0 + 4096].rearrange("p (l n) -> p l n", l=32)
            BLK = BIG[:, SP0 + 4096:SP0 + 6016].rearrange("p (j g l) -> p j g l", j=15, g=4)
            POS = w3(0, 64, 2)
            W2 = w3(64, 256, 2)
            CT = WORK[:, 320:1344].rearrange("p (g t) -> p g t", g=4)
            HC = WORK[:, 1344:1404]
            HE = WORK[:, 1404:1464]
            KC = WORK[:, 1472:1532].rearrange("p (j g) -> p j g", g=4)
            VC = w3(1536, 512, 4)
            GT = v3(SM[:, 32:128], 2)
            ST = SM[:, 128:192]
            tp = POOL.dma(lambda e: e.dma_start(POS, A["pos"]), d_par[1], tables)
            tp = POOL.dma(lambda e: e.dma_start(W2, A["nsa_cmp_w2"][0].rearrange("c p n -> p c n")), d_par[1], tables)
            gt = ACT(act(GT, ZN[:, :, 5120:5168], ACTF.Exp, scale=-1.0), z[10])
            gt = sigm(GT, gt)
            w1free, cfree = tables, tables
            kc = vc = None
            for part in range(2):
                tw = POOL.dma(lambda e, part=part: e.dma_start(
                    W1, A["nsa_cmp_w1"][0, part].rearrange("(l p) n -> p l n", p=128)), d_par[2], w1free)
                cw = []
                for pr in range(2):
                    b = bank()
                    p = PE(many(*[tr(b.ap[:, 256 * j + 128 * t:256 * j + 128 * t + 128],
                                     ZN[:, t, 2048 + 512 * part + 256 * pr + 128 * j:
                                        2048 + 512 * part + 256 * pr + 128 * j + 128])
                                  for j in range(2) for t in range(2)]), z[4 + part], b.free)
                    w = ACT(copy(CT[:, 2 * pr:2 * pr + 2], v3(b.ap, 2)), p, cfree)
                    b.free = [w]
                    cw.append(w)
                bl = []
                for j in range(15):
                    bl.append(DVE(tt(BLK[:, j], CT[:, :, 16 * j:16 * j + 32], rep(POS[:, part], 4), ALU.add),
                                  cw, tp, w1free))
                yield
                b = bank()
                p = PE(mm(b.ap[:, 0:60], [(W1[:, l], BLK[:, :, :, l].rearrange("p j g -> p (j g)"))
                                          for l in range(32)]), tw, bl, b.free)
                w1free = [p]
                cfree = bl
                e = ACT(act(HE, b.ap[:, 0:60], ACTF.Exp, scale=-1.0), p, kc, vc)
                e = sigm(HE, e)
                e = DVE(tt(HC, HE, b.ap[:, 0:60], ALU.mult), e)
                b.free = [e]
                b = bank()
                if part == 0:
                    p = PE(mm(b.ap[:, 0:60], [(W2[:, 0], HC)]), e, b.free)
                    kc = ACT(copy(KC.rearrange("p j g -> p (j g)"), b.ap[:, 0:60]), p)
                    b.free = [kc]
                else:
                    hc = HC.rearrange("p (j g) -> p j g", g=4)
                    p = PE(many(*[mm(b.ap[0:15, 128 * g:128 * g + 128], [(hc[:, :, g], W2[:, 1])])
                                  for g in range(4)]), e, b.free)
                    vc = ACT(copy(VC[0:15], v3(b.ap[0:15, :], 4)), p)
                    b.free = [vc]
                yield
            DB = BIG[:, SP0:SP0 + 1536]
            DC = v3(BIG[:, SP0 + 1536:SP0 + 1656], 2)
            MC = v3(BIG[:, SP0 + 1656:SP0 + 1776], 2)
            for dst, nm in ((DB, "c_db"), (BIG[:, SP0 + 1536:SP0 + 1656], "c_dc"), (BIG[:, SP0 + 1656:SP0 + 1776], "c_mc")):
                td = POOL.dma(lambda e, d=dst, nm=nm: e.dma_start(d, A[nm]), d_par[2], w1free)
            P4 = [BIG[:, SP0 + 1792 + 1024 * j:SP0 + 2816 + 1024 * j] for j in range(2)]
            PT = [w3(2048 + 1024 * j, 1024, 8) for j in range(2)]
            K2 = [w3(4096 + 512 * j, 512, 2) for j in range(2)]
            QT = [w3(5120 + 512 * j, 512, 4) for j in range(2)]
            OT = [w3(6144 + 512 * j, 512, 4) for j in range(2)]
            f_p, f_pt, f_k2, f_q, f_o = [w1free, w1free], [tables, tables], [cfree, cfree], [tables, tables], [tables, tables]
            unit = 0
            for g in range(4):
                K = K2[g % 2]
                kts = []
                for br in range(2):
                    b = bank()
                    p = PE(many(*[tr(b.ap[:, 128 * t:128 * t + 128],
                                     ZN[:, t, 3072 + 1024 * br + 128 * g:3200 + 1024 * br + 128 * g])
                                  for t in range(2)]), z[6 + 2 * br], b.free)
                    w = ACT(copy(K[:, br], b.ap[:, 0:256]), p, f_k2[g % 2])
                    b.free = [w]
                    kts.append(w)
                yield
                k_readers = []
                for i in range(2):
                    n = 2 * g + i
                    Q, O = QT[n % 2], OT[n % 2]
                    b = bank()
                    p = PE(many(*[tr(b.ap[:, 128 * h:128 * h + 128], ZN[:, i, 512 * g + 128 * h:512 * g + 128 * h + 128])
                                  for h in range(4)]), z[g], b.free)
                    tq = ACT(copy(Q, v3(b.ap, 4), QSCALE), p, f_q[n % 2])
                    q_read = p
                    b.free = [tq]
                    osum = None
                    for br in range(3):
                        u = unit % 2
                        unit += 1
                        P, T = P4[u], PT[u]
                        nk = 15 if br == 0 else 128 * (i + 1)
                        ktile = 1 if br == 0 else i + 1
                        P_ = v3(P[:, 0:4 * nk], 4)
                        c0 = 16 + 16 * u
                        mx, sm, rs = ST[:, c0:c0 + 4], ST[:, c0 + 4:c0 + 8], ST[:, c0 + 8:c0 + 12]
                        if br == 0:
                            b = bank()
                            p = PE(many(*[mm(b.ap[:, 15 * h:15 * h + 15], [(Q[:, h], KC[:, :, g])]) for h in range(4)]),
                                   tq, kc, b.free)
                            s = [DVE(stt(P[:, 0:60], DC[:, i], 4.0 ** -g, b.ap[:, 0:60], ALU.mult, ALU.add),
                                     p, td, f_p[u])]
                            b.free = s
                        else:
                            s = []
                            for hb in range(i + 1):
                                b = bank()
                                hh = range(2 * hb, 2 * hb + 2) if i else range(4)
                                p = PE(many(*[mm(b.ap[:, nk * (h - hh[0]):nk * (h - hh[0]) + nk],
                                                 [(Q[:, h], K[:, br - 1, 0:nk])]) for h in hh]), tq, kts, b.free)
                                k_readers.append(p)
                                o_ = P[:, 512 * hb:512 * hb + 512]
                                dd = DB[:, 512 * i + 512 * hb:512 * i + 512 * hb + 512]
                                w = DVE(stt(o_, dd, 4.0 ** -g, b.ap, ALU.mult, ALU.add), p, td, f_p[u])
                                b.free = [w]
                                s.append(w)
                        yield
                        m = DVE(red(mx, P_, ALU.max), s)
                        if br == 0:
                            x = DVE(tt(P_, P_, bc(mx, 15), ALU.subtract), m)
                            x = ACT(act(P_, P_, ACTF.Exp), x)
                            x = DVE(red(sm, P_, ALU.add), x)
                            xs = [DVE(tt(P[:, 0:60], P[:, 0:60], MC[:, i], ALU.mult), x)]
                        else:
                            m = DVE(ts(mx, mx, -1.0, None, ALU.mult), m)
                            xs = [ACT(act(P_[:, h], P_[:, h], ACTF.Exp, bias=mx[:, h:h + 1],
                                          accum_out=sm[:, h:h + 1]), m) for h in range(4)]
                        r = DVE(rec(rs, sm), xs)
                        gv = GT[:, i, 12 * g:12 * g + 12].rearrange("p (h b) -> p h b", b=3)[:, :, br]
                        r = DVE(tt(rs, rs, gv, ALU.mult), r, gt)
                        yield
                        evs = []
                        for kt_ in range(ktile):
                            b = bank()
                            w_ = 15 if br == 0 else 128
                            p = PE(many(*[tr(b.ap[0:w_, 128 * h:128 * h + 128], P_[:, h, 128 * kt_:128 * kt_ + w_])
                                          for h in range(4)]), xs, b.free)
                            w = ACT(copy(T[0:w_, 4 * kt_:4 * kt_ + 4], v3(b.ap[0:w_, :], 4)), p, f_pt[u])
                            b.free = [w]
                            evs.append(w)
                        f_p[u] = [p]
                        yield
                        b = bank()
                        fns = []
                        for h in range(4):
                            if br == 0:
                                prs = [(T[0:15, h], VC[0:15, g])]
                            else:
                                c = (3584, 4608)[br - 1] + 128 * g
                                prs = [(T[:, 4 * kt_ + h], ZN[:, kt_, c:c + 128]) for kt_ in range(ktile)]
                            fns.append(mm(b.ap[:, 128 * h:128 * h + 128], prs))
                        p = PE(many(*fns), evs, vc, z[7], z[9], b.free)
                        f_pt[u] = [p]
                        if br == 0:
                            osum = DVE(tt(O, v3(b.ap, 4), bc(rs, 128), ALU.mult), p, r, f_o[n % 2])
                            b.free = [osum]
                        else:
                            tmp = v3(P[:, 0:512], 4)
                            w = DVE(tt(tmp, v3(b.ap, 4), bc(rs, 128), ALU.mult), p, r)
                            b.free = [w]
                            dst = O if br == 1 else v3(ZN[:, i, 512 * g:512 * g + 512], 4)
                            osum = POOL(tt(dst, O, tmp, ALU.add), w, osum, q_read)
                            f_p[u] = [osum]
                        yield
                    f_q[n % 2] = k_readers[-1:]
                    f_o[n % 2] = [osum]
                    zt[("no", g, i)] = osum
                f_k2[g % 2] = k_readers
            yield

        Z2 = v3(BIG[:, 0:4096], 2)

        def z2_sink(c, t, ap, tok):
            zt[("z2", c, t)] = ACT(copy(Z2[:, t, 512 * c:512 * c + 512], ap), tok)
            return zt[("z2", c, t)]

        RT = BIG[:, 4096:4096 + 128]
        RT16 = BIG[:, 4224:4224 + 64]
        LC = BIG[:, 4288:4288 + 384]
        CA = BIG[:, 4672:4672 + 384]
        LTT = BIG[:, 5056:5056 + 128]
        ROT = BIG[:, 5184:5184 + 1024]
        SLN = BIG[:, 6208:6272]
        LAM = BIG[:, 6272:6400]
        QF = BIG[:, 6400:6400 + 4096]
        Y2 = v3(BIG[:, 10496:10496 + 1024], 2)
        TB = BIG[:, 11520:11520 + 2048]
        LAMV = SM[:, 200:210]

        def block2_tables(after):
            for dst, nm in ((RT, "c_r32"), (RT16, "c_r16"), (LC, "c_lc"), (CA, "c_ca"), (LTT, "c_lt")):
                t = POOL.dma(lambda e, d=dst, n=nm: e.dma_start(d, A[n]), d_par[3], after)
            t = POOL.dma(lambda e: e.dma_start(SLN, A["diff_subln_g_2"][0].partition_broadcast(128)), d_par[3], after)
            t = POOL.dma(lambda e: e.dma_start(LAM, A["diff_lam_2"][0].rearrange("a b -> (a b)").partition_broadcast(128)),
                       d_par[3], after)
            return t

        def rope(chunk, half, tab, tt_):
            n = 512 // (2 * half)
            res = []
            for t in range(2):
                x = Z2[:, t, 512 * chunk:512 * chunk + 512].rearrange("p (a two d) -> p a two d", two=2, d=half)
                x1, x2 = x[:, :, 0], x[:, :, 1]
                r = ROT[:, 0:1024].rearrange("p (k a d) -> p k a d", k=4, d=half)
                cos = rep(tab[:, 2 * half * t:2 * half * t + half], n)
                sin = rep(tab[:, 2 * half * t + half:2 * half * t + 2 * half], n)
                z = [zt[("z2", chunk, t)], tt_, zt.get("rot")]
                a = DVE(tt(r[:, 0], x1, cos, ALU.mult), z)
                b = POOL(tt(r[:, 1], x2, sin, ALU.mult), z)
                c = POOL(tt(r[:, 2], x1, sin, ALU.mult), z)
                d = DVE(tt(r[:, 3], x2, cos, ALU.mult), z)
                e = DVE(tt(x1, r[:, 0], r[:, 1], ALU.subtract), a, b, c, d)
                f = POOL(tt(x2, r[:, 2], r[:, 3], ALU.add), c, d, b, a)
                zt["rot"] = [e, f]
                res.append([e, f])
            return res

        def feature(chunk, dh, off, ready, free):
            n = 512 // dh
            dst = QF[0:dh, off:off + n * 256].rearrange("p (a t) -> p a t", a=n)
            w = []
            for a in range(0, n, 2):
                b = bank()
                p = PE(many(*[tr(b.ap[0:dh, 256 * j + 128 * t:256 * j + 128 * t + 128],
                                 Z2[:, t, 512 * chunk + dh * (a + j):512 * chunk + dh * (a + j) + dh])
                              for j in range(2) for t in range(2)]), ready, b.free)
                x = ACT(copy(dst[:, a:a + 2], v3(b.ap[0:dh, :], 2)), p, free)
                b.free = [x]
                w.append(x)
            return dst, w

        fq = {"tb": [[], []], "y": [], "pt": [[], []], "qf": []}

        def softmax_unit(q, k, nk, scale, bias, tabtok, tq, u, st):
            P = TB[:, 1024 * u:1024 * u + nk]
            b = bank()
            p = PE(mm(b.ap[:, 0:nk], [(q, k)]), tq, b.free)
            s = DVE(stt(P, b.ap[:, 0:nk], scale, bias, ALU.mult, ALU.add), p, tabtok, fq["tb"][u])
            b.free = [s]
            m = DVE(lambda e: e.tensor_reduce(st[:, 0:1], P, AX, ALU.max, negate=True), s)
            x = ACT(act(P, P, ACTF.Exp, bias=st[:, 0:1], accum_out=st[:, 1:2]), m)
            r = DVE(rec(st[:, 2:3], st[:, 1:2]), x)
            return P, x, r, p

        def pv_unit(P, x, nt, u, v, tv):
            T = TB[:, 1024 * u + 512:1024 * u + 512 + 128 * nt]
            b = bank()
            p = PE(many(*[tr(b.ap[:, 128 * k:128 * k + 128], P[:, 128 * k:128 * k + 128]) for k in range(nt)]), x, b.free)
            w = ACT(copy(T, b.ap[:, 0:128 * nt]), p, fq["pt"][u])
            b.free = [w]
            fq["tb"][u] = [p]
            b = bank()
            p = PE(mm(b.ap[:, 0:64], [(T[:, 128 * k:128 * k + 128], v(k)) for k in range(nt)]), w, tv, b.free)
            fq["pt"][u] = [p]
            return b, p

        def gate2(chunk, dst_c, i, ready):
            g = Z2[:, i, 512 * chunk + 256:512 * chunk + 512]
            e_ = ROT[:, 256 * i:256 * i + 256]
            y = Y2[:, i, dst_c:dst_c + 256]
            a = ACT(act(e_, g, ACTF.Exp, scale=-1.0), zt[("z2", chunk, i)], zt.get("rot"))
            a = sigm(e_, a)
            a = POOL(tt(e_, e_, g, ALU.mult), a)
            a = POOL(tt(y, y, e_, ALU.mult), a, ready)
            zt["rot"] = [zt.get("rot"), a]
            return a

        def attend2(layer, tabs):
            outs = []
            unit = 0
            st = SM[:, 64:128]
            if layer == 0:
                for br in range(2):
                    rot = rope(2 * br, 32, RT, tabs)
                    qk, w = feature(2 * br, 64, 2048 * br, rot, fq["qf"])
                    bias = (LC, CA)[br]
                    yield
                    for i in range(2):
                        ends = []
                        nk = 128 * (i + 1)
                        for h in range(4):
                            u = unit % 2
                            s_ = st[:, 4 * (unit % 8):4 * (unit % 8) + 4]
                            unit += 1
                            P, x, r, _ = softmax_unit(qk[:, h, 128 * i:128 * i + 128], qk[:, 4 + h, 0:nk], nk, 0.125,
                                                      bias[:, 128 * i:128 * i + nk], tabs, w, u, s_)
                            yield
                            c = 512 * (2 * br + 1) + 64 * h
                            b, p = pv_unit(P, x, i + 1, u, lambda k, c=c: Z2[:, k, c:c + 64],
                                           [zt[("z2", 2 * br + 1, t)] for t in range(2)])
                            d = DVE(ts(Y2[:, i, 256 * br + 64 * h:256 * br + 64 * h + 64], b.ap[:, 0:64], s_[:, 2:3],
                                       None, ALU.mult), p, r, fq["y"])
                            b.free = [d]
                            ends.append(d)
                            yield
                        outs.append(gate2(2 * br + 1, 256 * br, i, ends))
                zt["y2"] = outs
                return
            l1, l2 = LAM[:, 0:64].rearrange("p (a b) -> p a b", a=2), LAM[:, 64:128].rearrange("p (a b) -> p a b", a=2)
            pr = v3(ROT[:, 0:64], 2)
            a = DVE(tt(pr[:, 0], l1[:, 0], l1[:, 1], ALU.mult), tabs, zt.get("rot"))
            a = DVE(tt(pr[:, 1], l2[:, 0], l2[:, 1], ALU.mult), a)
            a = DVE(red(LAMV[:, 0:2], pr, ALU.add), a)
            a = ACT(act(LAMV[:, 2:4], LAMV[:, 0:2], ACTF.Exp), a)
            li = 0.8 - 0.6 * float(np.exp(-0.3))
            a = DVE(tt(LAMV[:, 4:5], LAMV[:, 3:4], LAMV[:, 2:3], ALU.subtract), a)
            lam = DVE(ts(LAMV[:, 5:6], LAMV[:, 4:5], -li, None, ALU.add), a)
            zt["rot"] = [lam]
            rot = rope(0, 16, RT16, tabs)
            qk, w = feature(0, 32, 0, rot, fq["qf"])
            yield
            for i in range(2):
                ends = []
                nk = 128 * (i + 1)
                for h in range(4):
                    s2 = [st[:, 8 * (h % 2):8 * (h % 2) + 4], st[:, 8 * (h % 2) + 4:8 * (h % 2) + 8]]
                    un = [softmax_unit(qk[:, 2 * h + j, 128 * i:128 * i + 128], qk[:, 8 + 2 * h + j, 0:nk], nk,
                                       32 ** -0.5, CA[:, 128 * i:128 * i + nk], tabs, w, j, s2[j]) for j in range(2)]
                    yield
                    (P0, x0, r0, _), (P1, x1, r1, _) = un
                    c1 = DVE(tt(s2[1][:, 2:3], s2[1][:, 2:3], LAMV[:, 5:6], ALU.mult), r1, lam)
                    a = DVE(ts(P0, P0, s2[0][:, 2:3], None, ALU.mult), r0, x0)
                    a = DVE(stt(P0, P1, s2[1][:, 2:3], P0, ALU.mult, ALU.add), a, c1, x1)
                    fq["tb"][1] = [a]
                    b, p = pv_unit(P0, a, i + 1, 0, lambda k, h=h: Z2[:, k, 512 + 64 * h:576 + 64 * h],
                                   [zt[("z2", 1, t)] for t in range(2)])
                    d = ACT(copy(Y2[:, i, 64 * h:64 * h + 64], b.ap[:, 0:64]), p, fq["y"])
                    b.free = [d]
                    ends.append(d)
                    yield
                y = v3(Y2[:, i, 0:256], 4)
                sq = v3(ROT[:, 512:768], 4)
                ss = st[:, 32 + 4 * i:36 + 4 * i]
                a = POOL(tt(sq, y, y, ALU.mult), ends, zt["rot"])
                a = DVE(red(ss, sq, ALU.add), a)
                zt["rot"] = [zt["rot"], a]
                r = rstd(ss, ss, 64, a, 1.0 - li)
                a = DVE(tt(y, y, bc(ss, 64), ALU.mult), r)
                a = POOL(tt(y, y, rep(SLN, 4), ALU.mult), a)
                outs.append(gate2(1, 0, i, a))
                yield
            diff_reads = fq["pt"][0] + fq["tb"][0] + fq["tb"][1]
            qd, wd = feature(2, 64, 0, [zt[("z2", 2, t)] for t in range(2)], diff_reads)
            for h in range(4):
                u = h % 2
                base = 1024 * u
                b = bank()
                q, k = qd[:, h], qd[:, 4 + h]
                p = PE(many(mm(b.ap[:, 0:256], [(k[:, 0:128], q)]),
                            mm(b.ap[:, 256:384], [(k[:, 128:256], q[:, 128:256])])), wd, b.free)
                Zs, L = TB[:, base:base + 384], TB[:, base + 384:base + 768]
                fr_ = [fq["tb"][u], fq["pt"][0], fq["pt"][1], fq.get(("sb", u))]
                zz = ACT(copy(Zs, b.ap[:, 0:384], 0.125), p, fr_)
                b.free = [zz]
                a = ACT(act(L, Zs, ACTF.Abs), zz, fr_)
                a = ACT(act(L, L, ACTF.Exp, scale=-1.0), a)
                a = ACT(act(L, L, ACTF.Ln, bias=one_b), a)
                yield
                a = DVE(stt(L, Zs, 0.0, L, ALU.max, ALU.add), a)
                m1 = POOL(tt(L[:, 0:128], L[:, 0:128], LTT, ALU.mult), a)
                m2 = POOL(tt(L[:, 256:384], L[:, 256:384], LTT, ALU.mult), a)
                b = bank()
                p = PE(many(mm(b.ap[:, 0:128], [(SUFI, L[:, 0:128])]),
                            mm(b.ap[:, 128:256], [(SUFI, L[:, 128:256]), (ONE, L[:, 256:384])]),
                            mm(b.ap[:, 256:384], [(SUFI, L[:, 256:384])])), m1, m2, tabs2, b.free)
                a = DVE(tt(Zs, Zs, b.ap[:, 0:384], ALU.subtract), p)
                b.free = [a]
                yield
                a = DVE(ts(Zs, Zs, 0.0, None, ALU.min), a)
                a = ACT(act(L, Zs, ACTF.Exp), a)
                m1 = POOL(tt(L[:, 0:128], L[:, 0:128], LTT, ALU.mult), a)
                m2 = POOL(tt(L[:, 256:384], L[:, 256:384], LTT, ALU.mult), a)
                yield
                b = bank()
                c = 1536 + 64 * h
                p = PE(many(mm(b.ap[:, 0:64], [(L[:, 0:128], Z2[:, 0, c:c + 64])]),
                            mm(b.ap[:, 64:128], [(L[:, 128:256], Z2[:, 0, c:c + 64]),
                                                 (L[:, 256:384], Z2[:, 1, c:c + 64])])),
                       m1, m2, [zt[("z2", 3, t)] for t in range(2)], b.free)
                fq[("sb", u)] = [p]
                d = ACT(copy(Y2[:, :, 256 + 64 * h:320 + 64 * h], v3(b.ap[:, 0:128], 2)), p, fq["y"])
                b.free = [d]
                yield
                fq.setdefault("sends", []).append(d)
            for i in range(2):
                outs.append(gate2(3, 256, i, fq["sends"]))
            zt["y2"] = outs

        SUFI = BIG[:, 13568:13696]
        tabs2 = None

        def whole():
            nonlocal tabs2
            last = pre_norm(GP[:, 0], t_const)
            t_gb = load_gb(A["norm_g"][0, 1], 0, None)
            zwidths = [b - a for a, b in order_even]

            main = use_cols(zwidths, UTH, UTL, last, z_sink_even)
            drain(main)
            drain(gdn())
            drain(hgrn())
            if STAGE == 1:
                gs = [zt[("o", a, hf, i)] for a in range(2) for hf in range(2) for i in range(2)]
                cps = [POOL(cp(H[:, t, 1024 * a:1024 * a + 1024], zcol(t, 4096 * a, 1024)), gs) for t in range(2) for a in range(2)]
                finish(cps)
                return
            gs = [zt[("o", a, hf, i)] for a in range(2) for hf in range(2) for i in range(2)]
            u = to_T(lambda k, t: zcol(t, 128 * k if k < 8 else 4096 + 128 * (k - 8), 128), NKT, gs)
            lastp = drain(use_rows(16, lambda k: (UTH[:, k], UTL[:, k], u), None))
            hdone = post_norm(t_gb, lastp)
            if STAGE == 2:
                return finish(hdone)
            hdone = ffn(0, A["norm_g"][0, 3], GP[:, 1], hdone)
            if STAGE == 3:
                return finish(hdone)
            u = pre_norm(GP[:, 2], hdone)
            t_gb = load_gb(A["norm_g"][1, 1], 0, hdone)
            drain(use_cols([b - a for a, b in cuts(5168)], UTH, UTL, u, nsa_sink))
            drain(nsa([hdone, u]))
            gs = [zt[("no", g, i)] for g in range(4) for i in range(2)]
            u = to_T(lambda k, t: ZN[:, t, 128 * k:128 * k + 128], NKT, gs)
            lastp = drain(use_rows(16, lambda k: (UTH[:, k], UTL[:, k], u), None))
            hdone = post_norm(t_gb, lastp)
            if STAGE == 4:
                return finish(hdone)
            hdone = ffn(1, A["norm_g"][1, 3], GP[:, 3], hdone)
            if STAGE == 5:
                return finish(hdone)
            for layer in range(2):
                u = pre_norm(GP[:, 4 + layer], hdone)
                if layer == 0:
                    t_gb = load_gb(A["final_norm_g_2"], 0, hdone)
                tabs = block2_tables(u)
                sf = POOL(ts(SUFI, LTT, -1.0, 1.0, ALU.mult, ALU.add), tabs)
                tabs2 = sf
                drain(use_cols([512] * 4, UTH, UTL, u, z2_sink))
                drain(attend2(layer, tabs))
                u = to_T(lambda k, t: Y2[:, t, 128 * k:128 * k + 128], 4, zt["y2"])
                lastp = drain(use_rows(4, lambda k: (UTH[:, k], UTL[:, k], u), None))
                hdone = plain_add(lastp)
                if STAGE == 6 + layer:
                    return finish(hdone)
            for t in range(2):
                a = ACT(act(BIG[:, D * t:D * t + D], H[:, t], ACTF.Square, accum_out=SM[:, t:t + 1]), hdone)
                r = rstd(SM[:, 2 + t:3 + t], SM[:, t:t + 1], D, a)
                o = DVE(stt(H[:, t], H[:, t], SM[:, 2 + t:3 + t], GB, ALU.mult, ALU.mult), r, t_gb)
            finish(o)

        whole()

        block = ctx.enter_context(nc.Block())

        @block.sync
        def _(e):
            SP.emit(e)

        @block.scalar
        def _(e):
            ACT.emit(e)

        @block.vector
        def _(e):
            DVE.emit(e)

        @block.gpsimd
        def _(e):
            POOL.emit(e)

        @block.tensor
        def _(e):
            PE.emit(e)


_NAMES = ["x", "norm_g", "ab_w_in", "gdn_a_log", "gdn_dt_bias", "hgrn_norm_g", "gdn_norm_g", "ab_w_out",
          "nsa_w_in", "nsa_cmp_w1", "nsa_cmp_w2", "nsa_w_out", "ffn_w_gu", "ffn_w_down",
          "w_in_2", "w_out_2", "diff_lam_2", "diff_subln_g_2", "final_norm_g_2"]


def kernel(**inputs):
    import concourse.bacc as _bacc
    from concourse.bass_utils import run_bass_kernel_spmd as _run

    nc = _bacc.Bacc("TRN2", target_bir_lowering=False, num_devices=1)
    host = {n: np.ascontiguousarray(inputs[n]) for n in _NAMES}
    ng, n2 = np.asarray(inputs["norm_g"]), np.asarray(inputs["norm_g_2"])
    pre = np.stack([ng[0, 0], ng[0, 2], ng[1, 0], ng[1, 2], n2[0], n2[1]])
    host["g_pre"] = np.ascontiguousarray(pre.reshape(6, 16, 128).transpose(2, 0, 1))
    host["conv_w"] = np.ascontiguousarray(np.asarray(inputs["gdn_conv_w"])[0].reshape(4, 24, 128).transpose(2, 1, 0))
    host["pos"] = np.ascontiguousarray(np.asarray(inputs["nsa_cmp_pos"])[0].transpose(2, 0, 1))
    host.update(constants())
    arrays, A = {}, {}
    for name, a in host.items():
        arrays[f"in_{name}"] = a
        A[name] = nc.dram_tensor(f"in_{name}", a.shape, mybir.dt.from_np(a.dtype), kind="ExternalInput").ap()
    out = nc.dram_tensor("out_0", (1, 256, 2048), F32, kind="ExternalOutput").ap()
    build(nc, A, out)
    r = _run(nc, [arrays], core_ids=[0])
    return r.results[0]["out_0"]
```

```python
from contextlib import ExitStack

import numpy as np

import concourse.bass as bass
from concourse import mybir

F32 = mybir.dt.float32
F32R = mybir.dt.float32r
ALU = mybir.AluOpType
ACTF = mybir.ActivationFunctionType
AX = mybir.AxisListType.X

D = 2048
NKT = 16
DFF = 5632
SLOT = 1024
NRAW = 4
NW = 3
LEAD = 2
EPS = 1e-6
QSCALE = 128 ** -0.5
CHUNKS_EVEN = 8208
STAGE = 99


def constants():
    r = np.arange(128)[:, None]
    t = np.arange(128)[None, :]
    levels = [1, 2, 4, 8, 16, 32, 64]
    wc, mk = [], []
    for m in levels:
        same = (r // (2 * m)) == (t // (2 * m))
        mid = (t // (2 * m)) * 2 * m + m
        second = (t >= mid) & (r >= mid) & (r <= t)
        first = (t < mid) & (r > t) & (r < mid)
        wc.append((same & (second | first)).astype(np.float32))
        mk.append((same & (r < mid) & (t >= mid)).astype(np.float32))
    wc.append((r > t).astype(np.float32))
    wc.append((r <= t).astype(np.float32))
    mk.append((r == t).astype(np.float32))
    out = {
        "c_wc": np.concatenate(wc, 1),
        "c_mk": np.concatenate(mk, 1),
        "c_one": np.ones((128, 128), np.float32),
    }
    slope = 2.0 ** (-8.0 * np.arange(1, 5) / 16)
    tt = np.arange(256)
    db = []
    for i in range(2):
        nk = 128 * (i + 1)
        dist = tt[128 * i:128 * i + 128, None] - tt[None, :nk]
        dist = np.where(dist >= 0, dist, 1e32)
        db.append((-slope[None, :, None] * dist[:, None, :]).reshape(128, -1))
    out["c_db"] = np.concatenate(db, 1).astype(np.float32)
    cst = np.arange(15) * 16 + 31
    dc = tt[:, None] - cst[None, :]
    mc = (dc >= 0).astype(np.float32)
    dc = np.where(dc >= 0, dc, 1e32)
    dc4 = -slope[None, :, None] * dc[:, None, :]
    out["c_dc"] = np.concatenate([dc4[:128].reshape(128, -1), dc4[128:].reshape(128, -1)], 1).astype(np.float32)
    mc4 = np.repeat(mc[:, None, :], 4, 1)
    out["c_mc"] = np.concatenate([mc4[:128].reshape(128, -1), mc4[128:].reshape(128, -1)], 1)
    dist = tt[:, None] - tt[None, :]
    cnt = ((dist >= 0) & (dist <= 128)).astype(int) + ((dist >= 0) & (dist % 4 == 0)) + ((dist >= 0) & (dist % 16 == 0))
    lc = np.where(cnt > 0, np.log(np.maximum(cnt, 1)), -1e30).astype(np.float32)
    ca = np.where(dist >= 0, 0.0, -1e30).astype(np.float32)
    out["c_lc"] = np.concatenate([lc[:128, :128], lc[128:, :]], 1)
    out["c_ca"] = np.concatenate([ca[:128, :128], ca[128:, :]], 1)

    def rope(half):
        inv = np.float32(10000.0) ** (-np.arange(half, dtype=np.float32) / np.float32(half))
        ang = (tt.astype(np.float32)[:, None] * inv.astype(np.float32)[None, :]).astype(np.float64)
        cs = np.concatenate([np.cos(ang), np.sin(ang)], 1).astype(np.float32)
        return cs.reshape(2, 128, 2 * half).transpose(1, 0, 2).reshape(128, 4 * half)

    out["c_r32"] = rope(32)
    out["c_r16"] = rope(16)
    out["c_lt"] = (r < t).astype(np.float32)
    return {k: np.ascontiguousarray(v) for k, v in out.items()}


def tokens(after):
    out = []
    for a in after:
        if isinstance(a, list):
            out += tokens(a)
        elif a is not None:
            out.append(a)
    return out


class Queue:

    def __init__(self, sem):
        self.sem, self.items, self.count = sem, [], 0

    def __call__(self, fn, *after):
        self.count += 1
        self.items.append((fn, tokens(after), self.sem, 1))
        return (self.sem, self.count)

    def dma(self, fn, sem_count, *after):
        sem_count[1] += 16
        self.items.append((fn, tokens(after), sem_count[0], 16))
        return (sem_count[0], sem_count[1])

    def wait(self, *after):
        self.items.append((None, tokens(after), None, 0))

    def emit(self, eng):
        seen = {}

        for fn, after, sem, inc in self.items:
            need = {}
            for s, n in after:
                if n > max(seen.get(id(s), 0), need.get(id(s), (s, 0))[1]):
                    need[id(s)] = (s, n)
            for s, n in need.values():
                seen[id(s)] = n
                eng.wait_ge(s, n)
            if fn is not None:
                fn(eng).then_inc(sem, inc)


class Bank:

    def __init__(self, ap):
        self.ap, self.free = ap, []


def build(nc, A, out):
    with ExitStack() as ctx:
        def sb(name, n, dt=F32):
            return ctx.enter_context(nc.sbuf_tensor(name, [128, n], dt))

        def sem(name):
            return ctx.enter_context(nc.semaphore(name))

        H = sb("H", 2 * D)[:].rearrange("p (t n) -> p t n", t=2)
        UTH = sb("UTH", NKT * 256, F32R)[:].rearrange("p (k n) -> p k n", k=NKT)
        UTL = sb("UTL", NKT * 256, F32R)[:].rearrange("p (k n) -> p k n", k=NKT)
        RAW = [sb(f"RAW{i}", SLOT)[:] for i in range(NRAW)]
        WH = [sb(f"WH{i}", SLOT, F32R)[:] for i in range(NW)]
        WL = [sb(f"WL{i}", SLOT, F32R)[:] for i in range(NW)]
        XS = [(UTH[:, i], UTL[:, i]) for i in range(3)]
        BIG = sb("BIG", 2 * CHUNKS_EVEN)[:]
        WORK = sb("WORK", 10752)[:]
        GB = WORK[:, 8704:10752]
        WC = sb("WC", 9 * 128)[:]
        MK = sb("MK", 8 * 128)[:]
        ONE = sb("ONE", 128)[:]
        SM = sb("SM", 512)[:]
        GP = sb("GP", 96)[:].rearrange("p (v k) -> p v k", v=6)
        ident = MK[:, 896:1024]
        PRE = WC[:, 1024:1152]
        SUF = WC[:, 896:1024]
        PS = ctx.enter_context(nc.psum_tensor("PS", [128, 8, 512], F32))
        banks = [Bank(PS[:, i, :]) for i in range(8)]

        sPE, sACT, sDVE, sPOOL = sem("s_pe"), sem("s_act"), sem("s_dve"), sem("s_pool")
        PE, ACT, DVE, POOL, SP = Queue(sPE), Queue(sACT), Queue(sDVE), Queue(sPOOL), Queue(None)
        raw_sems = [[sem(f"s_raw{i}"), 0] for i in range(NRAW)]
        d_const = [sem("s_const"), 0]
        d_par = [[sem(f"s_par{i}"), 0] for i in range(4)]
        d_out = [sem("s_out"), 0]

        def mm(out_, pairs, start=True, stop=True):
            def fn(e):
                last = None
                for j, (l, r) in enumerate(pairs):
                    last = e.matmul(out_, l, r, start=start and j == 0, stop=stop and j == len(pairs) - 1)
                return last
            return fn

        def many(*fns):
            def fn(e):
                last = None
                for f in fns:
                    last = f(e)
                return last
            return fn

        def tr(out_, in_):
            p = in_.shape[0]
            return lambda e: e.transpose(out_, in_, ident[0:p, 0:p])

        def copy(o, i, scale=1.0):
            return lambda e: e.activation(o, i, ACTF.Copy, scale=scale)

        def act(o, i, f, **k):
            return lambda e: e.activation(o, i, f, **k)

        def tt(o, a, b, op):
            return lambda e: e.tensor_tensor(o, a, b, op)

        def ts(o, a, s1, s2, op0, op1=None):
            if op1 is None:
                return lambda e: e.tensor_scalar(o, a, s1, None, op0)
            return lambda e: e.tensor_scalar(o, a, s1, s2, op0, op1)

        def stt(o, a, s, b, op0, op1):
            return lambda e: e.scalar_tensor_tensor(out=o, in0=a, scalar=s, in1=b, op0=op0, op1=op1)

        def cp(o, i):
            return lambda e: e.tensor_copy(o, i)

        def red(o, i, op):
            return lambda e: e.tensor_reduce(o, i, AX, op)

        def bc(ap, n):
            return ap.unsqueeze(2).to_broadcast([ap.shape[0], ap.shape[1], n])

        def rep(ap, n):
            return ap.unsqueeze(1).to_broadcast([ap.shape[0], n, ap.shape[1]])

        def v3(ap, a):
            return ap.rearrange("p (a b) -> p a b", a=a)

        t_const = None
        for dst, name in ((WC, "c_wc"), (MK, "c_mk"), (ONE, "c_one")):
            t_const = SP.dma(lambda e, d=dst, n=name: e.dma_start(d, A[n]), d_const)
        t_const = SP.dma(lambda e: e.dma_start(GP, A["g_pre"]), d_const)
        t_const = SP.dma(lambda e: e.dma_start(H, A["x"].rearrange("o (t p) n -> p (o t) n", p=128)), d_const)

        stream = []

        def add_cols(w, n0, n1, ktiles=NKT):
            wd = n1 - n0
            kk = min(ktiles, SLOT // 512 if wd > 64 else SLOT // wd)
            for k in range(0, ktiles, kk):
                src = w[128 * k:128 * (k + kk), n0:n1].rearrange("(k p) n -> p k n", p=128)
                stream.append((src, kk, wd))

        def add_rows(w, ktiles):
            for k in range(ktiles):
                for hf in range(2):
                    stream.append((w[128 * k:128 * k + 128, 1024 * hf:1024 * hf + 1024].unsqueeze(1), 1, 1024))

        def cuts(n):
            return [(a, min(a + 512, n)) for a in range(0, n, 512)]

        order_even = [(a, a + 512) for a in (4096, 5120, 6144)] + [(8192, 8208)] + [
            (a, a + 512) for a in (4608, 5632, 6656, 1024, 0, 2048, 1536, 512, 2560, 7168, 3072, 7680, 3584)]
        for a, b in order_even:
            add_cols(A["ab_w_in"][0], a, b)
        add_rows(A["ab_w_out"][0], 16)

        def add_ffn(l):
            for c in range(11):
                add_cols(A["ffn_w_gu"][l], 512 * c, 512 * c + 512)
                add_cols(A["ffn_w_gu"][l], DFF + 512 * c, DFF + 512 * c + 512)
            add_rows(A["ffn_w_down"][l], 44)

        add_ffn(0)
        order_nsa = [(a, a + 512) for a in (2048, 2560, 3072, 3584, 4096, 4608)] + [(5120, 5168)] + cuts(2048)
        for a, b in order_nsa:
            add_cols(A["nsa_w_in"][0], a, b)
        add_rows(A["nsa_w_out"][0], 16)
        add_ffn(1)
        for l in range(2):
            for a, b in cuts(2048):
                add_cols(A["w_in_2"][l], a, b)
            add_rows(A["w_out_2"][l], 4)

        hi_tok, lo_tok, used_tok = {}, {}, {}
        state = {"dma": 0, "prep": 0, "use": 0}

        def load(i):
            src, kk, wd = stream[i]
            dst = v3(RAW[i % NRAW][:, 0:kk * wd], kk)
            SP_tok = SP.dma(lambda e: e.dma_start(dst, src), raw_sems[i % NRAW],
                            hi_tok.get(i - NRAW), lo_tok.get(i - NRAW))
            return SP_tok

        raw_tok = {}

        def prep(upto):
            while state["prep"] <= min(upto, len(stream) - 1):
                i = state["prep"]
                while state["dma"] < min(i + NRAW, len(stream)):
                    raw_tok[state["dma"]] = load(state["dma"])
                    state["dma"] += 1
                n = stream[i][1] * stream[i][2]
                raw, wh, wl = (x[:, 0:n] for x in (RAW[i % NRAW], WH[i % NW], WL[i % NW]))
                hi_tok[i] = ACT(copy(wh, raw), raw_tok[i], used_tok.get(i - NW))
                lo_tok[i] = DVE(tt(wl, raw, wh.bitcast(F32), ALU.subtract), hi_tok[i], used_tok.get(i - NW))
                state["prep"] += 1

        def next_slot():
            i = state["use"]
            state["use"] += 1
            prep(i + LEAD)
            kk, wd = stream[i][1:]
            return i, v3(WH[i % NW][:, 0:kk * wd], kk), v3(WL[i % NW][:, 0:kk * wd], kk)

        def use_cols(widths, xh, xl, after, feed, sink, ktiles=NKT):
            for c, wd in enumerate(widths):
                pair = [banks[2 * (c % 2) + t] for t in range(2)]
                k = 0
                while k < ktiles:
                    kk = stream[state["use"]][1]
                    while len(after) < min(k + kk + 2, ktiles):
                        next(feed)
                    i, wh, wl = next_slot()
                    fns = []
                    for j in range(kk):
                        for t in range(2):
                            o = pair[t].ap[:, 0:wd]
                            lh, ll = xh[:, k + j, 128 * t:128 * t + 128], xl[:, k + j, 128 * t:128 * t + 128]
                            fns.append(mm(o, [(lh, wh[:, j]), (lh, wl[:, j]), (ll, wh[:, j])],
                                          start=k + j == 0, stop=k + j == ktiles - 1))
                    used_tok[i] = PE(many(*fns), hi_tok[i], lo_tok[i], [after[j] for j in range(k, k + kk)],
                                     pair[0].free, pair[1].free)
                    k += kk
                    if k < ktiles:
                        yield
                drain(feed)
                for t in range(2):
                    pair[t].free = [sink(c, t, pair[t].ap[:, 0:wd], used_tok[i])]
                yield

        def use_rows(ktiles, operand, after):
            busy = [b.free for b in banks]
            for k in range(ktiles):
                xh, xl, ready = operand(k)
                for hf in range(2):
                    i, wh, wl = next_slot()
                    fns = []
                    for t in range(2):
                        for n in range(2):
                            o = banks[4 * t + 2 * hf + n].ap
                            cs = slice(512 * n, 512 * n + 512)
                            lh, ll = xh[:, 128 * t:128 * t + 128], xl[:, 128 * t:128 * t + 128]
                            fns.append(mm(o, [(lh, wh[:, 0, cs]), (lh, wl[:, 0, cs]), (ll, wh[:, 0, cs])],
                                          start=k == 0, stop=k == ktiles - 1))
                    used_tok[i] = PE(many(*fns), hi_tok[i], lo_tok[i], after, ready, busy)
                yield used_tok[i]

        ring = {"n": 0}

        def bank():
            ring["n"] += 1
            return banks[4 + ring["n"] % 4]

        def drain(g):
            last = None
            for x in g:
                last = x if x is not None else last
            return last

        def together(main, *sides):
            sides = list(sides)
            for _ in main:
                for g in sides:
                    next(g, None)
            while sides:
                sides = [g for g in sides if next(g, "end") != "end"]

        def need(*keys):
            while any(k not in zt for k in keys):
                yield

        def to_T(toks, src, tiles, after, gain=None):
            for k in range(0, tiles, 2):
                b = bank()
                fns = [tr(b.ap[:, 256 * j + 128 * t:256 * j + 128 * t + 128], src(k + j, t))
                       for j in range(2) for t in range(2)]
                p = PE(many(*fns), after[k], after[k + 1], b.free, t_const)
                if gain is None:
                    hi = ACT(copy(UTH[:, k:k + 2], v3(b.ap, 2)), p)
                    lo = DVE(tt(UTL[:, k:k + 2], v3(b.ap, 2), UTH[:, k:k + 2].bitcast(F32), ALU.subtract), hi)
                else:
                    for j in range(2):
                        hi = ACT(copy(UTH[:, k + j], b.ap[:, 256 * j:256 * j + 256], gain[:, k + j:k + j + 1]), p)
                    for j in range(2):
                        lo = DVE(stt(UTL[:, k + j], b.ap[:, 256 * j:256 * j + 256], gain[:, k + j:k + j + 1],
                                     UTH[:, k + j].bitcast(F32), ALU.mult, ALU.subtract), hi)
                b.free = [lo]
                toks += [[hi, lo]] * 2
                yield

        RSQ = sb("RSQ", 16 * 12)[:]
        rsq = {"n": 0, "free": [None] * 16}
        JUNK = BIG[:, 15360:15872]
        NS = SM[:, 440:504]
        BNS, BNA = v3(NS[:, 32:56], 4), NS[:, 56:58]
        HSQ, HS2, HR, MSQ, MS2, MR = (NS[:, a:b] for a, b in ((0, 8), (8, 10), (10, 12), (12, 20), (20, 22), (22, 24)))

        def rstd(o, ss, n, after, gain=1.0, free=None):
            j = rsq["n"] % 16
            rsq["n"] += 1
            w = ss.shape[1]
            x, y, z = (RSQ[:, 12 * j + 4 * i:12 * j + 4 * i + w] for i in range(3))
            a = DVE(ts(x, ss, 1.0 / n, EPS, ALU.mult, ALU.add), after, rsq["free"][j])
            b = ACT(act(y, x, ACTF.Ln), a)
            b = ACT(act(y, y, ACTF.Exp, scale=-0.5), b)
            a = DVE(tt(z, y, y, ALU.mult), b)
            a = DVE(tt(z, z, x, ALU.mult), a)
            a = DVE(ts(z, z, -0.5 * gain, 1.5 * gain, ALU.mult, ALU.add), a)
            a = DVE(tt(o, y, z, ALU.mult), a, free)
            rsq["free"][j] = a
            return a

        def rec(o, i):
            return lambda e: e.reciprocal(o, i)

        def sigm(e_, after):
            a = DVE(ts(e_, e_, 1.0, None, ALU.add), after)
            return DVE(rec(e_, e_), a)

        junk = {"tok": None}

        def square(t, n, after):
            junk["tok"] = ACT(act(JUNK, H[:, t, 512 * n:512 * n + 512], ACTF.Square,
                                  accum_out=HSQ[:, 4 * t + n:4 * t + n + 1]), after, junk["tok"])
            return junk["tok"]

        def pre_norm(gain, h):
            toks = []

            def feed():
                sq = h["sq"] = []
                inner = to_T(toks, lambda k, t: H[:, t, 128 * k:128 * k + 128], NKT,
                             [[h[(t, k // 4)] for t in range(2)] for k in range(NKT)], gain)
                for k, _ in enumerate(inner):
                    if k % 2:
                        for t in range(2):
                            sq.append(square(t, k // 2, h[(t, k // 2)]))
                    if k < NKT // 2 - 1:
                        yield
                a = DVE(red(HS2, v3(HSQ, 2), ALU.add), sq)
                zt["r"] = rstd(HR, HS2, D, a, 1.0, h.get("z"))
                yield

            return toks, feed()

        def warm(func):
            ACT(act(SM[:, 31:32], one_b, func), ones_act)

        def load_gb(row, n, after):
            return POOL.dma(lambda e: e.dma_start(GB, row.partition_broadcast(128)), d_par[n], after)

        def post_norm(t_gb, after, z=None):
            sq = [[], []]
            for n in range(4):
                junk["tok"] = ACT(act(JUNK, banks[n].ap, ACTF.Square, accum_out=MSQ[:, n:n + 1]), after, junk["tok"])
                sq[0].append(junk["tok"])
                sq[1].append(DVE(lambda e, n=n: e.bn_stats(out=BNS[:, n], in_=banks[4 + n].ap), after))
            a = DVE(lambda e: e.bn_aggr(out=BNA, in_=BNS), sq[1])
            a = DVE(stt(MS2[:, 1:2], BNA[:, 0:1], BNA[:, 0:1], BNA[:, 1:2], ALU.mult, ALU.add), a)
            a = [DVE(ts(MS2[:, 1:2], MS2[:, 1:2], float(D), None, ALU.mult), a)]
            a.append(DVE(red(MS2[:, 0:1], MSQ[:, 0:4], ALU.add), sq[0]))
            r = rstd(MR, MS2, D, a)
            h, adds = {}, []
            for n in range(4):
                for t in range(2):
                    j = 2 * n + t
                    bk = banks[4 * t + n]
                    tmp = WORK[:, 1024 + 512 * (j % 4):1536 + 512 * (j % 4)]
                    m = DVE(stt(tmp, bk.ap, MR[:, t:t + 1], GB[:, 512 * n:512 * n + 512],
                                ALU.mult, ALU.mult), r, t_gb, adds[j - 4] if j >= 4 else None)
                    bk.free = [m]
                    hc = H[:, t, 512 * n:512 * n + 512]
                    adds.append((POOL if t else DVE)(tt(hc, hc, tmp, ALU.add), m))
                    h[(t, n)] = adds[-1]
            h["z"] = z
            return h

        def plain_add(after):
            h = {}
            for n in range(4):
                for t in range(2):
                    hc = H[:, t, 512 * n:512 * n + 512]
                    m = DVE(tt(hc, banks[4 * t + n].ap, hc, ALU.add), after)
                    banks[4 * t + n].free = [m]
                    h[(t, n)] = m
            return h

        def out_proj(tiles, src, after):
            u = []
            drain(to_T(u, src, tiles, after))
            return drain(use_rows(tiles, lambda k: (UTH[:, k], UTL[:, k], u[k]), None))

        def finish(after):
            o = out.rearrange("o (t p) n -> p (o t) n", p=128)
            SP.dma(lambda e: e.dma_start(o, H), d_out, after)
            SP.wait((d_out[0], d_out[1]))

        def all_of(h):
            return [h[(t, n)] for t in range(2) for n in range(4)]

        def ffn(l, row, gain, h):
            u, feed = pre_norm(gain, h)
            t_gb = load_gb(row, 0, all_of(h))
            HT = BIG[:, 0:44 * 256].rearrange("p (k n) -> p k n", k=44)
            G = [[BIG[:, 11264 + 1024 * x + 512 * t:11264 + 1024 * x + 512 * t + 512] for t in range(2)]
                 for x in range(4)]
            gate_tok, trs_tok, ht_tok, z = {}, {}, [], []

            def sink(c, t, ap, tok):
                x = (c // 2) % 2
                g = G[x][t]
                if c % 2 == 0:
                    gate_tok[t] = ACT(act(g, ap, ACTF.Silu, scale=HR[:, t:t + 1]), tok, zt["r"], trs_tok.get((x, t)))
                    return gate_tok[t]
                f = DVE(stt(g, ap, HR[:, t:t + 1], g, ALU.mult, ALU.mult), tok, gate_tok[t], zt["r"])
                z.append(f)
                b = bank()
                fns = [tr(b.ap[:, 128 * j:128 * j + 128], g[:, 128 * j:128 * j + 128]) for j in range(4)]
                p = PE(many(*fns), f, b.free)
                trs_tok[(x, t)] = p
                k = 4 * (c // 2)
                e = ACT(copy(HT[:, k:k + 4, 128 * t:128 * t + 128], v3(b.ap, 4)), p)
                b.free = [e]
                ht_tok.append(e)
                return f

            drain(use_cols([512] * 22, UTH, UTL, u, feed, sink))
            warm(ACTF.Exp)

            used = {}

            def operand(k):
                xh, xl = XS[k % 3]
                hi = ACT(copy(xh, HT[:, k]), ht_tok, used.get(k - 3))
                lo = DVE(tt(xl, HT[:, k], xh.bitcast(F32), ALU.subtract), hi, used.get(k - 3))
                return xh, xl, [hi, lo]

            pending = {0: operand(0), 1: operand(1)}

            def ahead(k):
                return pending[k]

            last = None
            for k, last in enumerate(use_rows(44, ahead, None)):
                used[k] = last
                if k + 2 < 44:
                    pending[k + 2] = operand(k + 2)
            return post_norm(t_gb, last, z)

        Z = v3(BIG, 2)

        def zcol(t, c, n):
            return Z[:, t, c:c + n]

        zt = {}

        def z_sink_even(c, t, ap, tok):
            a, b = order_even[c]
            zt[(a, t)] = ACT(copy(zcol(t, a, b - a), ap, HR[:, t:t + 1]), tok, zt["r"])
            return zt[(a, t)]

        SMG = SM[:, 32:512]
        LD = v3(SMG[:, 0:16], 2)
        BETA = v3(SMG[:, 16:32], 2)
        EG = v3(SMG[:, 32:80], 2)
        TMP = SMG[:, 80:240]
        DTB, NEA = SMG[:, 240:248], SMG[:, 248:256]
        HG = sb("HG", 128)[:]
        DG = sb("DG", 128)[:]
        CW = sb("CW", 96)[:].rearrange("p (c j) -> p c j", j=4)
        for dst, src in ((DTB, A["gdn_dt_bias"][0:1]), (NEA, A["gdn_a_log"][0:1]),
                         (HG, A["hgrn_norm_g"][0:1]), (DG, A["gdn_norm_g"][0:1])):
            t_const = SP.dma(lambda e, d=dst, s=src: e.dma_start(d, s[0].partition_broadcast(128)), d_const)
        t_const = SP.dma(lambda e: e.dma_start(CW, A["conv_w"]), d_const)
        ones_act = ACT(copy(SM[:, 30:31], ONE[:, 0:1]), t_const)
        one_b = SM[:, 30:31]

        def gdn_gates():
            ba = Z[:, :, 8192:8200]
            bb = Z[:, :, 8200:8208]
            z = [zt[(8192, 0)], zt[(8192, 1)]]
            x, ax, e1, l1 = (v3(TMP[:, 16 * j:16 * j + 16], 2) for j in range(4))
            a = DVE(tt(x, ba, rep(DTB, 2), ALU.add), z, t_const)
            b = ACT(act(ax, x, ACTF.Abs), a)
            b = ACT(act(e1, ax, ACTF.Exp, scale=-1.0), b)
            b = ACT(act(l1, e1, ACTF.Ln, bias=one_b), b, ones_act)
            c = DVE(stt(x, x, 0.0, l1, ALU.max, ALU.add), b)
            n = ACT(act(NEA, NEA, ACTF.Exp), t_const)
            n = DVE(ts(NEA, NEA, -1.0, None, ALU.mult), n)
            ld = DVE(tt(LD, x, rep(NEA, 2), ALU.mult), c, n)
            s = ACT(act(e1, bb, ACTF.Exp, scale=-1.0), z, c)
            beta = DVE(ts(e1, e1, 1.0, None, ALU.add), s)
            beta = DVE(rec(BETA, e1), beta)
            yield
            b_ = bank()
            fns = []
            for i in range(2):
                for j, m in enumerate((PRE, SUF, ONE)):
                    fns.append(mm(b_.ap[:, 24 * i + 8 * j:24 * i + 8 * j + 8], [(m, LD[:, i])]))
            p = PE(many(*fns), ld, b_.free)
            eg = ACT(act(EG, v3(b_.ap[:, 0:48], 2), ACTF.Exp), p)
            b_.free = [eg]
            zt["gates"] = [ld, beta, eg]
            yield

        def w3(o, n, a):
            return v3(WORK[:, o:o + n], a)

        done = {"g": [], "h": []}

        def conv_half(hf):
            F = [w3(5632, 1024, 4), w3(6656, 1024, 4)]
            E = [w3(7680, 1024, 4), w3(8704, 1024, 4)]
            last = {}
            for part, c0 in enumerate((4096, 5120, 6144)):
                yield from need((c0 + 512 * hf, 0), (c0 + 512 * hf, 1))
                f, e_ = F[part % 2], E[part % 2]
                z = [zt[(c0 + 512 * hf, t)] for t in range(2)]
                taps = []
                trs = []
                for pr in range(2):
                    b = bank()
                    fns = [tr(b.ap[:, 256 * j + 128 * t:256 * j + 128 * t + 128],
                              zcol(t, c0 + 512 * hf + 256 * pr + 128 * j, 128)) for j in range(2) for t in range(2)]
                    p = PE(many(*fns), z, b.free)
                    trs.append(p)
                    rd = []
                    for j in range(2):
                        ch = 8 * part + 4 * hf + 2 * pr + j
                        k0 = ACT(copy(f[:, 2 * pr + j], b.ap[:, 256 * j:256 * j + 256], CW[:, ch, 3:4]),
                                 p, last.get(part - 2), done["h"], t_const)
                    for j in range(2):
                        h = 2 * pr + j
                        ch = 8 * part + 4 * hf + h
                        k = k0
                        for d in range(1, 4):
                            k = DVE(stt(f[:, h, d:256], b.ap[:, 256 * j:256 * j + 256 - d], CW[:, ch, 3 - d:4 - d],
                                        f[:, h, d:256], ALU.mult, ALU.add), k)
                        rd.append(k)
                    b.free = rd
                    taps += rd
                    yield
                s = ACT(act(f, f, ACTF.Silu), taps)
                yield
                reads = []
                for t in range(2):
                    b = bank()
                    p = PE(many(*[tr(b.ap[:, 128 * j:128 * j + 128], f[:, j, 128 * t:128 * t + 128])
                                  for j in range(4)]), s, b.free)
                    reads.append(p)
                    dst = zcol(t, c0 + 512 * hf, 512)
                    if part == 2:
                        w = ACT(copy(dst, b.ap), p, trs)
                        b.free = [w]
                    else:
                        sq = ACT(act(e_[:, 2 * t:2 * t + 2], b.ap, ACTF.Square), p, s)
                        ss = TMP[:, 4 * t + 8 * part:4 * t + 8 * part + 4]
                        r = DVE(red(ss, e_[:, 2 * t:2 * t + 2].rearrange("p a (b c) -> p (a b) c", b=2), ALU.add), sq)
                        r = rstd(ss, ss, 1, r, QSCALE if part == 0 else 1.0)
                        w = DVE(tt(v3(dst, 4), v3(b.ap, 4), bc(ss, 128), ALU.mult), r, trs)
                        b.free = [w]
                        reads.append(r)
                    zt[("n", part, hf, t)] = w
                    yield
                last[part] = reads
            done["h"] = [last[p] for p in range(3)] + [zt[("n", p, hf, t)] for p in range(3) for t in range(2)]

        def gdn_group(hf, i, carry):
            yield from need("gates", *[("n", p, hf, i) for p in range(3)])
            ld, beta, eg = zt["gates"]
            free = done["g"]
            hs = range(4)
            ADEC, DEC, KB, KT = (w3(512 * j, 512, 4) for j in range(4))
            KBT, QT, LT, QK = (w3(2048 + 512 * j, 512, 4) for j in range(4))
            XX = WORK[:, 4096:5120].rearrange("p (h x n) -> p h x n", h=4, x=2)
            Y, LTM = KT, QT
            S = w3(5120, 512, 4)
            RV, RW = ADEC, DEC
            qz, kz, vz = (v3(zcol(i, c + 512 * hf, 512), 4) for c in (4096, 5120, 6144))
            tq, tk, tv = (zt[("n", p, hf, i)] for p in range(3))
            hsl = slice(4 * hf, 4 * hf + 4)
            a = POOL(tt(ADEC, rep(SUF, 4), bc(LD[:, i, hsl], 128), ALU.mult), ld, free)
            kb = DVE(tt(KB, kz, bc(BETA[:, i, hsl], 128), ALU.mult), beta, tk, free)
            x0 = POOL(cp(XX[:, :, 0], rep(ident, 4)), free)
            x1 = POOL(cp(XX[:, :, 1], rep(ident, 4)), free)
            yield
            b = bank()
            p = PE(many(*[mm(b.ap[:, 128 * h:128 * h + 128], [(ADEC[:, h], PRE)]) for h in hs]), a, b.free)
            dec = ACT(act(DEC, v3(b.ap, 4), ACTF.Exp), p, free)
            b.free = [dec]
            toks = []
            for src, dst, tok, eng in ((kz, KT, tk, 0), (KB, KBT, kb, 1), (qz, QT, tq, 0)):
                b = bank()
                p = PE(many(*[tr(b.ap[:, 128 * h:128 * h + 128], src[:, h]) for h in hs]), tok, b.free)
                if eng:
                    w = DVE(cp(dst, v3(b.ap, 4)), p, free)
                else:
                    w = ACT(copy(dst, v3(b.ap, 4)), p, free)
                b.free = [w]
                toks.append(w)
            tkT, tkbT, tqT = toks
            yield
            b = bank()
            p = PE(many(*[mm(b.ap[:, 128 * h:128 * h + 128], [(KT[:, h], KBT[:, h])]) for h in hs]), tkT, tkbT, b.free)
            lt = DVE(tt(LT, v3(b.ap, 4), DEC, ALU.mult), p, dec, free)
            b.free = [lt]
            b = bank()
            p = PE(many(*[mm(b.ap[:, 128 * h:128 * h + 128], [(KT[:, h], QT[:, h])]) for h in hs]), tqT, b.free)
            qk0 = DVE(tt(QK, v3(b.ap, 4), DEC, ALU.mult), p, free)
            b.free = [qk0]
            qk = POOL(tt(QK, QK, rep(PRE, 4), ALU.mult), qk0)
            yield
            xx = [x0, x1]
            py = None
            for l in range(7):
                m = POOL(tt(LTM, LT, rep(MK[:, 128 * l:128 * l + 128], 4), ALU.mult), lt, qk0, py)
                b = bank()
                py = PE(many(*[mm(b.ap[:, 128 * h:128 * h + 128], [(LTM[:, h], XX[:, h, 0])]) for h in hs]),
                        m, xx, b.free)
                y = ACT(copy(Y, v3(b.ap, 4)), py)
                b.free = [y]
                yield
                b0, b1 = bank(), bank()
                fns = []
                for h in hs:
                    bb = (b0, b1)[h // 2].ap[:, 256 * (h % 2):256 * (h % 2) + 256]
                    fns.append(mm(bb[:, 0:128], [(XX[:, h, 1], Y[:, h])]))
                    fns.append(mm(bb[:, 128:256], [(Y[:, h], XX[:, h, 1])]))
                p = PE(many(*fns), y, b0.free, b1.free)
                xx = []
                for j, bb in enumerate((b0, b1)):
                    o = XX[:, 2 * j:2 * j + 2].rearrange("p h x n -> p (h x n)")
                    u = DVE(tt(o, o, bb.ap, ALU.subtract), p)
                    bb.free = [u]
                    xx.append(u)
                yield
            rv = DVE(tt(RV, vz, bc(BETA[:, i, hsl], 128), ALU.mult), tv, dec, qk0)
            bu = bank()
            pu = PE(many(*[mm(bu.ap[:, 128 * h:128 * h + 128], [(XX[:, h, 1], RV[:, h])]) for h in hs]),
                    rv, xx, bu.free)
            U = KB
            if i == 0:
                u = ACT(copy(U, v3(bu.ap, 4)), pu, tkbT)
                bu.free = [u]
                KD = RW
                kd = POOL(tt(KD, kz, bc(EG[:, i, 8 + 4 * hf:12 + 4 * hf], 128), ALU.mult), eg, lt, qk0)
                yield
                bs = bank()
                ps = PE(many(*[mm(bs.ap[:, 128 * h:128 * h + 128], [(KD[:, h], U[:, h])]) for h in hs]),
                        u, kd, bs.free)
                s = DVE(cp(S, v3(bs.ap, 4)), ps, free)
                bs.free = [s]
                bo = bank()
                po = PE(many(*[mm(bo.ap[:, 128 * h:128 * h + 128], [(QK[:, h], U[:, h])]) for h in hs]), qk, u, bo.free)
                carry["s"] = s
                used = [po, ps]
            else:
                rw = POOL(tt(RW, KB, bc(EG[:, i, hsl], 128), ALU.mult), eg, lt, qk0)
                bw = bank()
                pw = PE(many(*[mm(bw.ap[:, 128 * h:128 * h + 128], [(RW[:, h], XX[:, h, 1])]) for h in hs]),
                        rw, bw.free)
                WT = KBT
                wt = ACT(copy(WT, v3(bw.ap, 4)), pw)
                bw.free = [wt]
                QE = Y
                qe = POOL(tt(QE, qz, bc(EG[:, i, hsl], 128), ALU.mult), eg, tq, xx)
                u0 = ACT(copy(U, v3(bu.ap, 4)), pu, rw, tkbT)
                bu.free = [u0]
                yield
                bs = bank()
                ps = PE(many(*[mm(bs.ap[:, 128 * h:128 * h + 128], [(WT[:, h], S[:, h])]) for h in hs]),
                        wt, carry["s"], bs.free)
                u = DVE(tt(U, U, v3(bs.ap, 4), ALU.subtract), ps, u0)
                bs.free = [u]
                bq = bank()
                pq = PE(many(*[tr(bq.ap[:, 128 * h:128 * h + 128], QE[:, h]) for h in hs]), qe, bq.free)
                qt = ACT(copy(QT, v3(bq.ap, 4)), pq, py)
                bq.free = [qt]
                yield
                bo = bank()
                po = PE(many(*[mm(bo.ap[:, 128 * h:128 * h + 128], [(QT[:, h], S[:, h]), (QK[:, h], U[:, h])])
                               for h in hs]), qt, u, qk, bo.free)
                used = [po]
            w = ACT(copy(zcol(i, 4096 + 512 * hf, 512), bo.ap), po, tqT, used)
            bo.free = [w]
            zt[("ob", hf, i)] = w
            done["g"] = [used, w]
            yield

        def out_gate(o, g, gain, to, tg, key, base, free):
            o3, g3 = v3(o, 4), v3(g, 4)
            e_ = w3(base, 512, 4)
            ss = TMP[:, 64 + base // 128:68 + base // 128]
            a = POOL(tt(e_, o3, o3, ALU.mult), to, free)
            a = DVE(red(ss, e_, ALU.add), a)
            r = rstd(ss, ss, 128, a)
            m = DVE(tt(o3, o3, bc(ss, 128), ALU.mult), r)
            m = POOL(tt(o3, o3, rep(gain, 4), ALU.mult), m)
            e = ACT(act(e_, g3, ACTF.Silu), tg, a)
            zt[key] = POOL(tt(o3, o3, e_, ALU.mult), e, m)
            return zt[key]

        def gdn():
            yield from need((8192, 1))
            yield from gdn_gates()
            for hf in range(2):
                carry = {}
                for i in range(2):
                    yield from gdn_group(hf, i, carry)
            for hf in range(2):
                yield from need((7168 + 512 * hf, 1))
                for i in range(2):
                    out_gate(zcol(i, 4096 + 512 * hf, 512), zcol(i, 7168 + 512 * hf, 512), DG,
                             zt[("ob", hf, i)], zt[(7168 + 512 * hf, i)], ("o", 1, hf, i), 512 * (2 * hf + i), done["g"])
                    yield

        def convs():
            for hf in range(2):
                yield from conv_half(hf)
            zt["convs"] = True

        def hgrn():
            for hf in range(2):
                yield from need("convs", *[(c + 512 * hf, 1) for c in (1024, 0, 2048)])
                KK = w3(5632, 1024, 2)
                L1 = w3(6656, 1024, 2)
                x = Z[:, :, 1024 + 512 * hf:1536 + 512 * hf]
                tz = [zt[(1024 + 512 * hf, t)] for t in range(2)]
                a = ACT(act(L1, x, ACTF.Abs), tz, done["h"])
                a = ACT(act(L1, L1, ACTF.Exp, scale=-1.0), a)
                a = ACT(act(L1, L1, ACTF.Ln, bias=one_b), a)
                k0 = DVE(stt(KK, x, 0.0, L1, ALU.max, ALU.add), a, done["h"])
                lf = DVE(stt(x, x, 0.0, L1, ALU.min, ALU.subtract), a, k0)
                kk = ACT(act(KK, KK, ACTF.Exp, scale=-1.0), k0)
                yield
                o0 = 6656
                QKT = [w3(o0 + 256 * j, 256, 2) for j in range(2)]
                E = [w3(o0 + 512 + 512 * j, 512, 4) for j in range(2)]
                QE = E
                KE = [w3(o0 + 1536 + 512 * j, 512, 4) for j in range(2)]
                KE7 = WORK[:, o0 + 2560:o0 + 2688]
                ATM = w3(o0 + 2688, 1024, 8)
                AT = [WORK[:, o0 + 3712 + 128 * j:o0 + 3840 + 128 * j] for j in range(3)]
                start = [lf, done["h"]]
                fr = {"qk": [start, start], "e": [start, start], "s": [start, start], "atm": start,
                      "at": [start] * 4, "ke7": start}
                ends = []
                units = [{"h": h, "i": i, "cq": 512 * hf + 128 * h} for h in range(4) for i in range(2)]

                def factors(n, u):
                    h, i, cq = u["h"], u["i"], u["cq"]
                    qk_ = QKT[n % 2]
                    b = bank()
                    p = PE(many(tr(b.ap[:, 0:128], zcol(i, cq, 128)),
                                tr(b.ap[:, 128:256], KK[:, i, 128 * h:128 * h + 128])),
                           zt[(512 * hf, i)], kk, b.free)
                    u["tqk"] = ACT(copy(qk_, v3(b.ap[:, 0:256], 2)), p, fr["qk"][n % 2])
                    b.free = [u["tqk"]]
                    pref = zcol(i, 1024 + cq, 128)
                    u["es"] = []
                    for g in range(2):
                        b = bank()
                        if g == 1 and i == 1:
                            f = many(mm(b.ap[:, 0:384], [(pref, WC[:, 512:896])]),
                                     mm(b.ap[:, 384:512], [(pref, PRE)]))
                        else:
                            f = mm(b.ap, [(pref, WC[:, 512 * g:512 * g + 512])])
                        p = PE(f, lf, b.free)
                        e = ACT(act(E[g], v3(b.ap, 4), ACTF.Exp), p, fr["e"][g])
                        b.free = [e]
                        u["es"].append(e)

                def scores(n, u):
                    i, es, tqk = u["i"], u["es"], u["tqk"]
                    qT, kT = QKT[n % 2][:, 0], QKT[n % 2][:, 1]
                    u["at"] = []
                    for g in range(2):
                        k7 = None
                        if g == 1 and i == 0:
                            ke = POOL(tt(KE[g][:, 0:3], E[g][:, 0:3], rep(kT, 3), ALU.mult), es[g], tqk, fr["s"][g])
                            k7 = fr["k7"] = POOL(tt(KE7, E[g][:, 3], kT, ALU.mult), es[g], tqk, fr["ke7"])
                        else:
                            ke = POOL(tt(KE[g], E[g], rep(kT, 4), ALU.mult), es[g], tqk, fr["s"][g])
                        qe = DVE(tt(QE[g], E[g], rep(qT, 4), ALU.mult), ke, k7)
                        b = bank()
                        fns = [mm(b.ap[:, 128 * l:128 * l + 128], [(KE[g][:, l], QE[g][:, l])])
                               for l in range(4 - g)]
                        if g == 1:
                            fns.append(mm(b.ap[:, 384:512], [(kT, qT)]))
                        p = PE(many(*fns), qe, ke, b.free)
                        mtok = DVE(tt(ATM[:, 4 * g:4 * g + 4].rearrange("p a b -> p (a b)"), b.ap,
                                      MK[:, 512 * g:512 * g + 512], ALU.mult), p, fr["atm"])
                        b.free = [mtok]
                        fr["s"][g] = fr["e"][g] = [p]
                        u["at"].append(mtok)
                        if g == 1 and i == 1:
                            b = bank()
                            p = PE(mm(b.ap[:, 0:128], [(KE7, QE[1][:, 3])]), fr["k7"], b.free)
                            fr["ke7"] = [p]
                            fr["s"][1] = fr["e"][1] = [p]
                            u["c7"] = ACT(copy(AT[2], b.ap[:, 0:128]), p, fr["at"][2])
                            b.free = [u["c7"]]
                    fr["qk"][n % 2] = [p, qe, ke]

                def sum_levels(n, u):
                    u["ra"] = DVE(red(AT[n % 2], ATM.rearrange("p l t -> p t l"), ALU.add), u["at"], fr["at"][n % 2])
                    fr["atm"] = [u["ra"]]

                def values(n, u):
                    i, cq = u["i"], u["cq"]
                    pairs = [(AT[n % 2], zcol(i, 2048 + cq, 128))]
                    if i == 1:
                        pairs.append((AT[2], zcol(0, 2048 + cq, 128)))
                    b = bank()
                    p = PE(mm(b.ap[:, 0:128], pairs), u["ra"], u.get("c7"), zt[(2048 + 512 * hf, 0)],
                           zt[(2048 + 512 * hf, 1)], b.free)
                    fr["at"][n % 2] = [p]
                    if i == 1:
                        fr["at"][2] = [p]
                    w = ACT(copy(zcol(i, cq, 128), b.ap[:, 0:128]), p)
                    b.free = [w]
                    ends.append(w)
                    return p

                factors(0, units[0])
                yield
                for n, u in enumerate(units):
                    scores(n, u)
                    if n + 1 < len(units):
                        factors(n + 1, units[n + 1])
                    yield
                    sum_levels(n, u)
                    yield
                    p = values(n, u)
                done["h"] = [ends, p]
                zt[("oa", hf)] = ends
            for hf in range(2):
                yield from need((3072 + 512 * hf, 1))
                for i in range(2):
                    out_gate(zcol(i, 512 * hf, 512), zcol(i, 3072 + 512 * hf, 512), HG, zt[("oa", hf)],
                             zt[(3072 + 512 * hf, i)], ("o", 0, hf, i), 5632 + 512 * (2 * hf + i), done["h"])
                    yield

        ZN = v3(BIG[:, 0:2 * 5168], 2)
        SP0 = 2 * 5168

        def nsa_sink(c, t, ap, tok):
            a, b = order_nsa[c]
            zt[("n", a, t)] = ACT(copy(ZN[:, t, a:b], ap, HR[:, t:t + 1]), tok, zt["r"])
            return zt[("n", a, t)]

        def nsa(tables):
            W1 = BIG[:, SP0:SP0 + 4096].rearrange("p (l n) -> p l n", l=32)
            BLK = BIG[:, SP0 + 4096:SP0 + 6016].rearrange("p (j g l) -> p j g l", j=15, g=4)
            POS = w3(0, 64, 2)
            W2 = w3(64, 256, 2)
            CT = WORK[:, 320:1344].rearrange("p (g t) -> p g t", g=4)
            HC = WORK[:, 1344:1404]
            HE = WORK[:, 1404:1464]
            KC = WORK[:, 1472:1532].rearrange("p (j g) -> p j g", g=4)
            VC = w3(1536, 512, 4)
            GT = v3(SM[:, 32:128], 2)
            ST = SM[:, 128:192]
            DB = WORK[:, 7168:8704]
            DC = v3(SM[:, 200:320], 2)
            MC = v3(SM[:, 320:440], 2)
            tp = POOL.dma(lambda e: e.dma_start(POS, A["pos"]), d_par[1], tables)
            tp = POOL.dma(lambda e: e.dma_start(W2, A["nsa_cmp_w2"][0].rearrange("c p n -> p c n")), d_par[1], tables)
            for dst, nm in ((DB, "c_db"), (SM[:, 200:320], "c_dc"), (SM[:, 320:440], "c_mc")):
                td = POOL.dma(lambda e, d=dst, nm=nm: e.dma_start(d, A[nm]), d_par[1], tables)
            tp = td
            def compress():
                w1free, cfree = tables, tables
                kc = vc = None
                tw = POOL.dma(lambda e: e.dma_start(
                    W1, A["nsa_cmp_w1"][0, 0].rearrange("(l p) n -> p l n", p=128)), d_par[2], w1free)
                for part in range(2):
                    c0 = 2048 + 512 * part
                    yield from need(("n", c0, 0), ("n", c0, 1))
                    z = [zt[("n", c0, t)] for t in range(2)]
                    cw = []
                    for pr in range(2):
                        b = bank()
                        p = PE(many(*[tr(b.ap[:, 256 * j + 128 * t:256 * j + 128 * t + 128],
                                         ZN[:, t, c0 + 256 * pr + 128 * j:c0 + 256 * pr + 128 * j + 128])
                                      for j in range(2) for t in range(2)]), z, b.free)
                        w = ACT(copy(CT[:, 2 * pr:2 * pr + 2], v3(b.ap, 2)), p, cfree)
                        b.free = [w]
                        cw.append(w)
                    yield
                    bl = []
                    for j in range(15):
                        eng = POOL if j % 2 else DVE
                        bl.append(eng(tt(BLK[:, j], CT[:, :, 16 * j:16 * j + 32], rep(POS[:, part], 4), ALU.add),
                                      cw, tp, w1free))
                    yield
                    b = bank()
                    p = PE(mm(b.ap[:, 0:60], [(W1[:, l], BLK[:, :, :, l].rearrange("p j g -> p (j g)"))
                                              for l in range(32)]), tw, bl, b.free)
                    w1free = [p]
                    cfree = bl
                    if part == 0:
                        tw = POOL.dma(lambda e: e.dma_start(
                            W1, A["nsa_cmp_w1"][0, 1].rearrange("(l p) n -> p l n", p=128)), d_par[2], w1free)
                    e = ACT(act(HE, b.ap[:, 0:60], ACTF.Exp, scale=-1.0), p, kc, vc)
                    e = sigm(HE, e)
                    e = DVE(tt(HC, HE, b.ap[:, 0:60], ALU.mult), e)
                    b.free = [e]
                    yield
                    b = bank()
                    if part == 0:
                        p = PE(mm(b.ap[:, 0:60], [(W2[:, 0], HC)]), e, b.free)
                        kc = ACT(copy(KC.rearrange("p j g -> p (j g)"), b.ap[:, 0:60]), p)
                        b.free = [kc]
                        zt["kc"] = kc
                    else:
                        hc = HC.rearrange("p (j g) -> p j g", g=4)
                        p = PE(many(*[mm(b.ap[0:15, 128 * g:128 * g + 128], [(hc[:, :, g], W2[:, 1])])
                                      for g in range(4)]), e, b.free)
                        vc = ACT(copy(VC[0:15], v3(b.ap[0:15, :], 4)), p)
                        b.free = [vc]
                        zt["w1free"] = w1free
                        zt["vc"] = vc
                    yield
                yield from need(("n", 5120, 0), ("n", 5120, 1))
                gt = ACT(act(GT, ZN[:, :, 5120:5168], ACTF.Exp, scale=-1.0), [zt[("n", 5120, t)] for t in range(2)])
                zt["gt"] = sigm(GT, gt)

            P4 = [BIG[:, SP0 + 1024 * j:SP0 + 1024 * j + 1024] for j in range(2)]
            PT = [BIG[:, SP0 + 2048 + 1024 * j:SP0 + 3072 + 1024 * j].rearrange("p (a b) -> p a b", a=8) for j in range(2)]
            K2 = [w3(2048 + 512 * j, 512, 2) for j in range(2)]
            QT = [w3(3072 + 512 * j, 512, 4) for j in range(4)]
            OT = [w3(5120 + 512 * j, 512, 4) for j in range(4)]

            def stream(u):
                P, T, K = P4[u], PT[u], K2[u]
                yield from need("vc", "kc", "gt")
                kc, vc, gt = zt["kc"], zt["vc"], zt["gt"]
                f_p, f_pt, f_k2, f_q, f_o = [zt["w1free"]], [zt["w1free"]], [tables], [[tables]] * 2, [[tables]] * 2
                for g in (u, u + 2):
                    yield from need(*[("n", a, t) for a in (3072, 3584, 4096, 4608) for t in range(2)])
                    zk = [zt[("n", a, t)] for a in (3072, 4096) for t in range(2)]
                    zv = [zt[("n", a, t)] for a in (3584, 4608) for t in range(2)]
                    kts = []
                    for br in range(2):
                        b = bank()
                        p = PE(many(*[tr(b.ap[:, 128 * t:128 * t + 128],
                                         ZN[:, t, 3072 + 1024 * br + 128 * g:3200 + 1024 * br + 128 * g])
                                      for t in range(2)]), zk, b.free)
                        w = ACT(copy(K[:, br], b.ap[:, 0:256]), p, f_k2)
                        b.free = [w]
                        kts.append(w)
                    yield
                    yield from need(("n", 512 * g, 0), ("n", 512 * g, 1))
                    k_readers = []
                    for i in range(2):
                        Q, O = QT[2 * u + i], OT[2 * u + i]
                        b = bank()
                        p = PE(many(*[tr(b.ap[:, 128 * h:128 * h + 128],
                                         ZN[:, i, 512 * g + 128 * h:512 * g + 128 * h + 128])
                                      for h in range(4)]), zt[("n", 512 * g, i)], b.free)
                        tq = ACT(copy(Q, v3(b.ap, 4), QSCALE), p, f_q[i])
                        q_read = p
                        b.free = [tq]
                        osum = None
                        for br in range(3):
                            nk = 15 if br == 0 else 128 * (i + 1)
                            ktile = 1 if br == 0 else i + 1
                            P_ = v3(P[:, 0:4 * nk], 4)
                            c0 = 16 + 16 * u
                            mx, sm, rs = ST[:, c0:c0 + 4], ST[:, c0 + 4:c0 + 8], ST[:, c0 + 8:c0 + 12]
                            if br == 0:
                                b = bank()
                                p = PE(many(*[mm(b.ap[:, 15 * h:15 * h + 15], [(Q[:, h], KC[:, :, g])])
                                              for h in range(4)]), tq, kc, b.free)
                                s = [DVE(stt(P[:, 0:60], DC[:, i], 4.0 ** -g, b.ap[:, 0:60], ALU.mult, ALU.add),
                                         p, td, f_p)]
                                b.free = s
                            else:
                                s = []
                                for hb in range(i + 1):
                                    b = bank()
                                    hh = range(2 * hb, 2 * hb + 2) if i else range(4)
                                    p = PE(many(*[mm(b.ap[:, nk * (h - hh[0]):nk * (h - hh[0]) + nk],
                                                     [(Q[:, h], K[:, br - 1, 0:nk])]) for h in hh]), tq, kts, b.free)
                                    k_readers.append(p)
                                    o_ = P[:, 512 * hb:512 * hb + 512]
                                    dd = DB[:, 512 * i + 512 * hb:512 * i + 512 * hb + 512]
                                    w = DVE(stt(o_, dd, 4.0 ** -g, b.ap, ALU.mult, ALU.add), p, td, f_p)
                                    b.free = [w]
                                    s.append(w)
                            yield
                            if br == 0:
                                m = DVE(red(mx, P_, ALU.max), s)
                                x = DVE(tt(P_, P_, bc(mx, 15), ALU.subtract), m)
                                x = ACT(act(P_, P_, ACTF.Exp), x)
                                x = DVE(red(sm, P_, ALU.add), x)
                                xs = [DVE(tt(P[:, 0:60], P[:, 0:60], MC[:, i], ALU.mult), x)]
                            else:
                                m = DVE(lambda e, mx=mx, P_=P_: e.tensor_reduce(mx, P_, AX, ALU.max, negate=True), s)
                                xs = [ACT(act(P_[:, h], P_[:, h], ACTF.Exp, bias=mx[:, h:h + 1],
                                              accum_out=sm[:, h:h + 1]), m) for h in range(4)]
                            r = DVE(rec(rs, sm), xs)
                            gv = GT[:, i, 12 * g:12 * g + 12].rearrange("p (h b) -> p h b", b=3)[:, :, br]
                            r = DVE(tt(rs, rs, gv, ALU.mult), r, gt)
                            yield
                            evs = []
                            for kt_ in range(ktile):
                                b = bank()
                                w_ = 15 if br == 0 else 128
                                p = PE(many(*[tr(b.ap[0:w_, 128 * h:128 * h + 128], P_[:, h, 128 * kt_:128 * kt_ + w_])
                                              for h in range(4)]), xs, b.free)
                                w = ACT(copy(T[0:w_, 4 * kt_:4 * kt_ + 4], v3(b.ap[0:w_, :], 4)), p, f_pt)
                                b.free = [w]
                                evs.append(w)
                            f_p = [p]
                            yield
                            b = bank()
                            fns = []
                            for h in range(4):
                                if br == 0:
                                    prs = [(T[0:15, h], VC[0:15, g])]
                                else:
                                    c = (3584, 4608)[br - 1] + 128 * g
                                    prs = [(T[:, 4 * kt_ + h], ZN[:, kt_, c:c + 128]) for kt_ in range(ktile)]
                                fns.append(mm(b.ap[:, 128 * h:128 * h + 128], prs))
                            p = PE(many(*fns), evs, vc, zv, b.free)
                            f_pt = [p]
                            if br == 0:
                                osum = DVE(tt(O, v3(b.ap, 4), bc(rs, 128), ALU.mult), p, r, f_o[i])
                                b.free = [osum]
                            else:
                                tmp = v3(P[:, 0:512], 4)
                                w = DVE(tt(tmp, v3(b.ap, 4), bc(rs, 128), ALU.mult), p, r)
                                b.free = [w]
                                dst = O if br == 1 else v3(ZN[:, i, 512 * g:512 * g + 512], 4)
                                osum = POOL(tt(dst, O, tmp, ALU.add), w, osum, q_read)
                                f_p = [osum]
                            yield
                        f_q[i] = k_readers[-1:]
                        f_o[i] = [osum]
                        zt[("no", g, i)] = osum
                    f_k2 = k_readers

            return compress(), stream(0), stream(1)

        Z2 = v3(BIG[:, 0:4096], 2)

        def z2_sink(c, t, ap, tok):
            zt[("z2", c, t)] = ACT(copy(Z2[:, t, 512 * c:512 * c + 512], ap, HR[:, t:t + 1]), tok, zt["r"])
            return zt[("z2", c, t)]

        RT = BIG[:, 4096:4096 + 128]
        RT16 = BIG[:, 4224:4224 + 64]
        LC = BIG[:, 4288:4288 + 384]
        CA = BIG[:, 4672:4672 + 384]
        LTT = BIG[:, 5056:5056 + 128]
        ROT = BIG[:, 5184:5184 + 1024]
        SLN = BIG[:, 6208:6272]
        LAM = BIG[:, 6272:6400]
        QF = BIG[:, 6400:6400 + 4096]
        Y2 = v3(BIG[:, 10496:10496 + 1024], 2)
        TB = BIG[:, 11520:11520 + 2048]
        LAMV = SM[:, 200:210]

        def block2_tables(after):
            for dst, nm in ((RT, "c_r32"), (RT16, "c_r16"), (LC, "c_lc"), (CA, "c_ca"), (LTT, "c_lt")):
                t = POOL.dma(lambda e, d=dst, n=nm: e.dma_start(d, A[n]), d_par[3], after)
            t = POOL.dma(lambda e: e.dma_start(SLN, A["diff_subln_g_2"][0].partition_broadcast(128)), d_par[3], after)
            t = POOL.dma(lambda e: e.dma_start(LAM, A["diff_lam_2"][0].rearrange("a b -> (a b)").partition_broadcast(128)),
                       d_par[3], after)
            return t

        def rope(chunk, half, tab, tt_):
            n = 512 // (2 * half)
            res = []
            for t in range(2):
                x = Z2[:, t, 512 * chunk:512 * chunk + 512].rearrange("p (a two d) -> p a two d", two=2, d=half)
                x1, x2 = x[:, :, 0], x[:, :, 1]
                base = 3072 + 1024 * (chunk + t)
                r = WORK[:, base:base + 1024].rearrange("p (k a d) -> p k a d", k=4, d=half)
                cos = rep(tab[:, 2 * half * t:2 * half * t + half], n)
                sin = rep(tab[:, 2 * half * t + half:2 * half * t + 2 * half], n)
                z = [zt[("z2", chunk, t)], tt_]
                a = DVE(tt(r[:, 0], x1, cos, ALU.mult), z)
                b = POOL(tt(r[:, 1], x2, sin, ALU.mult), z)
                c = POOL(tt(r[:, 2], x1, sin, ALU.mult), z)
                d = DVE(tt(r[:, 3], x2, cos, ALU.mult), z)
                e = DVE(tt(x1, r[:, 0], r[:, 1], ALU.subtract), a, b, c, d)
                f = POOL(tt(x2, r[:, 2], r[:, 3], ALU.add), c, d, b, a)
                res.append([e, f])
            return res

        def feature(chunk, dh, mem, ready, free):
            n = 512 // dh
            dst = mem[0:dh, 0:n * 256].rearrange("p (a t) -> p a t", a=n)
            w = []
            for a in range(0, n, 2):
                b = bank()
                p = PE(many(*[tr(b.ap[0:dh, 256 * j + 128 * t:256 * j + 128 * t + 128],
                                 Z2[:, t, 512 * chunk + dh * (a + j):512 * chunk + dh * (a + j) + dh])
                              for j in range(2) for t in range(2)]), ready, b.free)
                x = ACT(copy(dst[:, a:a + 2], v3(b.ap[0:dh, :], 2)), p, free)
                b.free = [x]
                w.append(x)
            return dst, w

        def softmax_unit(q, k, nk, scale, bias, tabtok, tq, u, st, fq):
            P = TB[:, 512 * u:512 * u + nk]
            b = bank()
            p = PE(mm(b.ap[:, 0:nk], [(q, k)]), tq, b.free)
            s = DVE(stt(P, b.ap[:, 0:nk], scale, bias, ALU.mult, ALU.add), p, tabtok, fq["tb"])
            b.free = [s]
            m = DVE(lambda e: e.tensor_reduce(st[:, 0:1], P, AX, ALU.max, negate=True), s)
            x = ACT(act(P, P, ACTF.Exp, bias=st[:, 0:1], accum_out=st[:, 1:2]), m)
            r = DVE(rec(st[:, 2:3], st[:, 1:2]), x)
            return P, x, r

        def pv_transpose(P, x, nt, u, fq):
            T = TB[:, 512 * u + 256:512 * u + 256 + 128 * nt]
            b = bank()
            p = PE(many(*[tr(b.ap[:, 128 * k:128 * k + 128], P[:, 128 * k:128 * k + 128]) for k in range(nt)]), x, b.free)
            w = ACT(copy(T, b.ap[:, 0:128 * nt]), p, fq["pt"])
            b.free = [w]
            fq["tb"] = [p]
            return T, w

        def pv_product(T, w, nt, v, tv, fq):
            b = bank()
            p = PE(mm(b.ap[:, 0:64], [(T[:, 128 * k:128 * k + 128], v(k)) for k in range(nt)]), w, tv, b.free)
            fq["pt"] = [p]
            return b, p

        def gate2(chunk, dst_c, i, ready):
            g = Z2[:, i, 512 * chunk + 256:512 * chunk + 512]
            base = 2048 + 256 * (i + chunk - 1)
            e_ = WORK[:, base:base + 256]
            y = Y2[:, i, dst_c:dst_c + 256]
            a = ACT(act(e_, g, ACTF.Exp, scale=-1.0), zt[("z2", chunk, i)])
            a = sigm(e_, a)
            a = POOL(tt(e_, e_, g, ALU.mult), a)
            return POOL(tt(y, y, e_, ALU.mult), a, ready)

        def attend2(layer, tabs):
            st = SM[:, 64:256]
            ends = {}

            def vals(c):
                return [zt[("z2", c, t)] for t in range(2)]

            def setup(chunk, dh, mem, tab):
                yield from need(("z2", chunk, 0), ("z2", chunk, 1))
                ready = vals(chunk) if tab is None else rope(chunk, dh // 2, tab, tabs)
                yield
                zt[("qk", layer, chunk)] = feature(chunk, dh, mem, ready, [])
                yield

            def plain(br, par):
                u = 2 * br + par
                yield from need(("qk", layer, 2 * br), ("z2", 2 * br + 1, 1))
                qk, w = zt[("qk", layer, 2 * br)]
                bias = (LC, CA)[br]
                fq = {"tb": [], "pt": []}
                for i in range(2):
                    nk = 128 * (i + 1)
                    for h in (par, par + 2):
                        s_ = st[:, 16 * u + 4 * (h // 2):16 * u + 4 * (h // 2) + 4]
                        P, x, r = softmax_unit(qk[:, h, 128 * i:128 * i + 128], qk[:, 4 + h, 0:nk], nk, 0.125,
                                               bias[:, 128 * i:128 * i + nk], tabs, w, u, s_, fq)
                        yield
                        T, w2 = pv_transpose(P, x, i + 1, u, fq)
                        yield
                        c = 512 * (2 * br + 1) + 64 * h
                        b, p = pv_product(T, w2, i + 1, lambda k, c=c: Z2[:, k, c:c + 64], vals(2 * br + 1), fq)
                        d = DVE(ts(Y2[:, i, 256 * br + 64 * h:256 * br + 64 * h + 64], b.ap[:, 0:64], s_[:, 2:3],
                                   None, ALU.mult), p, r)
                        b.free = [d]
                        ends.setdefault((br, i), []).append(d)
                        yield

            def close(br, chunk):
                for i in range(2):
                    while len(ends.get((br, i), [])) < 4:
                        yield
                    zt[("y2", layer, br, i)] = gate2(chunk, 256 * br, i, ends[(br, i)])

            if layer == 0:
                return [setup(0, 64, QF, RT), setup(2, 64, QF[:, 2048:], RT), plain(0, 0), plain(0, 1),
                        plain(1, 0), plain(1, 1), close(0, 1), close(1, 3)]
            li = 0.8 - 0.6 * float(np.exp(-0.3))

            def lam_value():
                l = LAM.rearrange("p (g a b) -> p g a b", g=2, a=2)
                pr = v3(ROT[:, 0:64], 2)
                a = DVE(tt(pr, l[:, :, 0], l[:, :, 1], ALU.mult), tabs)
                a = DVE(red(LAMV[:, 0:2], pr, ALU.add), a)
                a = ACT(act(LAMV[:, 2:4], LAMV[:, 0:2], ACTF.Exp), a)
                a = DVE(tt(LAMV[:, 4:5], LAMV[:, 3:4], LAMV[:, 2:3], ALU.subtract), a)
                return DVE(ts(LAMV[:, 5:6], LAMV[:, 4:5], -li, None, ALU.add), a)

            lam = lam_value()

            def diff(par):
                yield from need(("qk", layer, 0), ("z2", 1, 1))
                qk, w = zt[("qk", layer, 0)]
                fqs = [{"tb": [], "pt": []} for _ in range(2)]
                for i in range(2):
                    nk = 128 * (i + 1)
                    for h in (par, par + 2):
                        s2 = [st[:, 16 * par + 8 * (h // 2) + 4 * j:16 * par + 8 * (h // 2) + 4 * j + 4] for j in range(2)]
                        (P0, x0, r0), (P1, x1, r1) = [
                            softmax_unit(qk[:, 2 * h + j, 128 * i:128 * i + 128], qk[:, 8 + 2 * h + j, 0:nk], nk,
                                         32 ** -0.5, CA[:, 128 * i:128 * i + nk], tabs, w, 2 * par + j, s2[j], fqs[j])
                            for j in range(2)]
                        yield
                        c1 = DVE(tt(s2[1][:, 2:3], s2[1][:, 2:3], LAMV[:, 5:6], ALU.mult), r1, lam)
                        a = DVE(ts(P0, P0, s2[0][:, 2:3], None, ALU.mult), r0, x0)
                        a = DVE(stt(P0, P1, s2[1][:, 2:3], P0, ALU.mult, ALU.add), a, c1, x1)
                        fqs[1]["tb"] = [a]
                        T, w2 = pv_transpose(P0, a, i + 1, 2 * par, fqs[0])
                        yield
                        b, p = pv_product(T, w2, i + 1, lambda k, h=h: Z2[:, k, 512 + 64 * h:576 + 64 * h],
                                          vals(1), fqs[0])
                        d = ACT(copy(Y2[:, i, 64 * h:64 * h + 64], b.ap[:, 0:64]), p)
                        b.free = [d]
                        ends.setdefault((0, i), []).append(d)
                        yield

            def close_diff():
                for i in range(2):
                    while len(ends.get((0, i), [])) < 4:
                        yield
                    y = v3(Y2[:, i, 0:256], 4)
                    sq = v3(ROT[:, 256 + 256 * i:512 + 256 * i], 4)
                    ss = st[:, 64 + 4 * i:68 + 4 * i]
                    a = POOL(tt(sq, y, y, ALU.mult), ends[(0, i)])
                    a = DVE(red(ss, sq, ALU.add), a)
                    r = rstd(ss, ss, 64, a, 1.0 - li)
                    a = DVE(tt(y, y, bc(ss, 64), ALU.mult), r)
                    a = POOL(tt(y, y, rep(SLN, 4), ALU.mult), a)
                    zt[("y2", layer, 0, i)] = gate2(1, 0, i, a)
                    yield

            def stick(u):
                yield from need(("qk", layer, 2), ("z2", 3, 1))
                qd, wd = zt[("qk", layer, 2)]
                base = 13696 + 768 * u
                Zs, L = BIG[:, base:base + 384], BIG[:, base + 384:base + 768]
                prev = None
                for h in (u, u + 2):
                    b = bank()
                    q, k = qd[:, h], qd[:, 4 + h]
                    p = PE(many(mm(b.ap[:, 0:256], [(k[:, 0:128], q)]),
                                mm(b.ap[:, 256:384], [(k[:, 128:256], q[:, 128:256])])), wd, b.free)
                    zz = ACT(copy(Zs, b.ap[:, 0:384], 0.125), p, prev)
                    b.free = [zz]
                    a = ACT(act(L, Zs, ACTF.Abs), zz, prev)
                    a = ACT(act(L, L, ACTF.Exp, scale=-1.0), a)
                    a = ACT(act(L, L, ACTF.Ln, bias=one_b), a)
                    yield
                    a = DVE(stt(L, Zs, 0.0, L, ALU.max, ALU.add), a)
                    m1 = POOL(tt(L[:, 0:128], L[:, 0:128], LTT, ALU.mult), a)
                    m2 = POOL(tt(L[:, 256:384], L[:, 256:384], LTT, ALU.mult), a)
                    yield
                    b = bank()
                    p = PE(many(mm(b.ap[:, 0:128], [(SUFI, L[:, 0:128])]),
                                mm(b.ap[:, 128:256], [(SUFI, L[:, 128:256]), (ONE, L[:, 256:384])]),
                                mm(b.ap[:, 256:384], [(SUFI, L[:, 256:384])])), m1, m2, tabs2, b.free)
                    a = DVE(tt(Zs, Zs, b.ap[:, 0:384], ALU.subtract), p)
                    b.free = [a]
                    a = DVE(ts(Zs, Zs, 0.0, None, ALU.min), a)
                    a = ACT(act(L, Zs, ACTF.Exp), a)
                    yield
                    m1 = POOL(tt(L[:, 0:128], L[:, 0:128], LTT, ALU.mult), a)
                    m2 = POOL(tt(L[:, 256:384], L[:, 256:384], LTT, ALU.mult), a)
                    yield
                    b = bank()
                    c = 1536 + 64 * h
                    p = PE(many(mm(b.ap[:, 0:64], [(L[:, 0:128], Z2[:, 0, c:c + 64])]),
                                mm(b.ap[:, 64:128], [(L[:, 128:256], Z2[:, 0, c:c + 64]),
                                                     (L[:, 256:384], Z2[:, 1, c:c + 64])])),
                           m1, m2, vals(3), b.free)
                    prev = p
                    d = ACT(copy(Y2[:, :, 256 + 64 * h:320 + 64 * h], v3(b.ap[:, 0:128], 2)), p)
                    b.free = [d]
                    for i in range(2):
                        ends.setdefault((1, i), []).append(d)
                    yield

            return [setup(0, 32, QF, RT16), setup(2, 64, WORK, None), diff(0), diff(1), stick(0), stick(1),
                    close_diff(), close(1, 3)]

        SUFI = BIG[:, 13568:13696]
        tabs2 = None

        def whole():
            nonlocal tabs2
            h = {(t, n): t_const for t in range(2) for n in range(4)}
            u, feed = pre_norm(GP[:, 0], h)
            together(use_cols([b - a for a, b in order_even], UTH, UTL, u, feed, z_sink_even),
                     convs(), gdn(), hgrn())
            gs = [zt[("o", a, hf, i)] for a in range(2) for hf in range(2) for i in range(2)]
            if STAGE == 1:
                cps = [POOL(cp(H[:, t, 1024 * a:1024 * a + 1024], zcol(t, 4096 * a, 1024)), gs) for t in range(2) for a in range(2)]
                finish(cps)
                return
            t_gb = load_gb(A["norm_g"][0, 1], 0, gs)
            last = out_proj(NKT, lambda k, t: zcol(t, 128 * k if k < 8 else 4096 + 128 * (k - 8), 128),
                            [[zt[("o", k // 8, k % 8 // 4, i)] for i in range(2)] for k in range(NKT)])
            h = post_norm(t_gb, last)
            if STAGE == 2:
                return finish(all_of(h))
            h = ffn(0, A["norm_g"][0, 3], GP[:, 1], h)
            if STAGE == 3:
                return finish(all_of(h))
            u, feed = pre_norm(GP[:, 2], h)
            parts = nsa(all_of(h))
            together(use_cols([b - a for a, b in order_nsa], UTH, UTL, u, feed, nsa_sink), *parts)
            t_gb = load_gb(A["norm_g"][1, 1], 0, all_of(h))
            last = out_proj(NKT, lambda k, t: ZN[:, t, 128 * k:128 * k + 128],
                            [[zt[("no", k // 4, i)] for i in range(2)] for k in range(NKT)])
            h = post_norm(t_gb, last)
            if STAGE == 4:
                return finish(all_of(h))
            h = ffn(1, A["norm_g"][1, 3], GP[:, 3], h)
            if STAGE == 5:
                return finish(all_of(h))
            tabs = block2_tables(all_of(h))
            tabs2 = POOL(ts(SUFI, LTT, -1.0, 1.0, ALU.mult, ALU.add), tabs)
            t_gb = load_gb(A["final_norm_g_2"], 0, all_of(h))
            for layer in range(2):
                for key in [k for k in zt if isinstance(k, tuple) and k[0] == "z2"]:
                    del zt[key]
                u, feed = pre_norm(GP[:, 4 + layer], h)
                together(use_cols([512] * 4, UTH, UTL, u, feed, z2_sink), *attend2(layer, tabs))
                last = out_proj(4, lambda k, t: Y2[:, t, 128 * k:128 * k + 128],
                                [[zt[("y2", layer, k // 2, i)] for i in range(2)] for k in range(4)])
                h = plain_add(last)
                if STAGE == 6 + layer:
                    return finish(all_of(h))
            sq = [square(t, n, h[(t, n)]) for n in range(4) for t in range(2)]
            a = DVE(red(HS2, v3(HSQ, 2), ALU.add), sq)
            r = rstd(HR, HS2, D, a)
            ends = [DVE(stt(H[:, t], H[:, t], HR[:, t:t + 1], GB, ALU.mult, ALU.mult), r, t_gb) for t in range(2)]
            finish(ends)

        whole()

        block = ctx.enter_context(nc.Block())

        @block.sync
        def _(e):
            SP.emit(e)

        @block.scalar
        def _(e):
            ACT.emit(e)

        @block.vector
        def _(e):
            DVE.emit(e)

        @block.gpsimd
        def _(e):
            POOL.emit(e)

        @block.tensor
        def _(e):
            PE.emit(e)


_NAMES = ["x", "norm_g", "ab_w_in", "gdn_a_log", "gdn_dt_bias", "hgrn_norm_g", "gdn_norm_g", "ab_w_out",
          "nsa_w_in", "nsa_cmp_w1", "nsa_cmp_w2", "nsa_w_out", "ffn_w_gu", "ffn_w_down",
          "w_in_2", "w_out_2", "diff_lam_2", "diff_subln_g_2", "final_norm_g_2"]


def kernel(**inputs):
    import concourse.bacc as _bacc
    from concourse.bass_utils import run_bass_kernel_spmd as _run

    nc = _bacc.Bacc("TRN2", target_bir_lowering=False, num_devices=1)
    host = {n: np.ascontiguousarray(inputs[n]) for n in _NAMES}
    ng, n2 = np.asarray(inputs["norm_g"]), np.asarray(inputs["norm_g_2"])
    pre = np.stack([ng[0, 0], ng[0, 2], ng[1, 0], ng[1, 2], n2[0], n2[1]])
    host["g_pre"] = np.ascontiguousarray(pre.reshape(6, 16, 128).transpose(2, 0, 1))
    host["conv_w"] = np.ascontiguousarray(np.asarray(inputs["gdn_conv_w"])[0].reshape(4, 24, 128).transpose(2, 1, 0))
    host["pos"] = np.ascontiguousarray(np.asarray(inputs["nsa_cmp_pos"])[0].transpose(2, 0, 1))
    host.update(constants())
    arrays, A = {}, {}
    for name, a in host.items():
        arrays[f"in_{name}"] = a
        A[name] = nc.dram_tensor(f"in_{name}", a.shape, mybir.dt.from_np(a.dtype), kind="ExternalInput").ap()
    out = nc.dram_tensor("out_0", (1, 256, 2048), F32, kind="ExternalOutput").ap()
    build(nc, A, out)
    r = _run(nc, [arrays], core_ids=[0])
    return r.results[0]["out_0"]
```

```python
from contextlib import ExitStack

import numpy as np

import concourse.bass as bass
from concourse import mybir

F32 = mybir.dt.float32
F32R = mybir.dt.float32r
ALU = mybir.AluOpType
ACTF = mybir.ActivationFunctionType
AX = mybir.AxisListType.X

D = 2048
NKT = 16
DFF = 5632
SLOT = 1024
NRAW = 4
NW = 3
LEAD = 2
EPS = 1e-6
QSCALE = 128 ** -0.5
CHUNKS_EVEN = 8208
STAGE = 99


def constants():
    r = np.arange(128)[:, None]
    t = np.arange(128)[None, :]
    levels = [1, 2, 4, 8, 16, 32, 64]
    wc, mk = [], []
    for m in levels:
        same = (r // (2 * m)) == (t // (2 * m))
        mid = (t // (2 * m)) * 2 * m + m
        second = (t >= mid) & (r >= mid) & (r <= t)
        first = (t < mid) & (r > t) & (r < mid)
        wc.append((same & (second | first)).astype(np.float32))
        mk.append((same & (r < mid) & (t >= mid)).astype(np.float32))
    wc.append((r > t).astype(np.float32))
    wc.append((r <= t).astype(np.float32))
    mk.append((r == t).astype(np.float32))
    out = {
        "c_wc": np.concatenate(wc, 1),
        "c_mk": np.concatenate(mk, 1),
        "c_one": np.ones((128, 128), np.float32),
    }
    slope = 2.0 ** (-8.0 * np.arange(1, 5) / 16)
    tt = np.arange(256)
    db = []
    for i in range(2):
        nk = 128 * (i + 1)
        dist = tt[128 * i:128 * i + 128, None] - tt[None, :nk]
        dist = np.where(dist >= 0, dist, 1e32)
        db.append((-slope[None, :, None] * dist[:, None, :]).reshape(128, -1))
    out["c_db"] = np.concatenate(db, 1).astype(np.float32)
    cst = np.arange(15) * 16 + 31
    dc = tt[:, None] - cst[None, :]
    mc = (dc >= 0).astype(np.float32)
    dc = np.where(dc >= 0, dc, 1e32)
    dc4 = -slope[None, :, None] * dc[:, None, :]
    out["c_dc"] = np.concatenate([dc4[:128].reshape(128, -1), dc4[128:].reshape(128, -1)], 1).astype(np.float32)
    mc4 = np.repeat(mc[:, None, :], 4, 1)
    out["c_mc"] = np.concatenate([mc4[:128].reshape(128, -1), mc4[128:].reshape(128, -1)], 1)
    dist = tt[:, None] - tt[None, :]
    cnt = ((dist >= 0) & (dist <= 128)).astype(int) + ((dist >= 0) & (dist % 4 == 0)) + ((dist >= 0) & (dist % 16 == 0))
    lc = np.where(cnt > 0, np.log(np.maximum(cnt, 1)), -1e30).astype(np.float32)
    ca = np.where(dist >= 0, 0.0, -1e30).astype(np.float32)
    out["c_lc"] = np.concatenate([lc[:128, :128], lc[128:, :]], 1)
    out["c_ca"] = np.concatenate([ca[:128, :128], ca[128:, :]], 1)

    def rope(half):
        inv = np.float32(10000.0) ** (-np.arange(half, dtype=np.float32) / np.float32(half))
        ang = (tt.astype(np.float32)[:, None] * inv.astype(np.float32)[None, :]).astype(np.float64)
        cs = np.concatenate([np.cos(ang), np.sin(ang)], 1).astype(np.float32)
        return cs.reshape(2, 128, 2 * half).transpose(1, 0, 2).reshape(128, 4 * half)

    out["c_r32"] = rope(32)
    out["c_r16"] = rope(16)
    out["c_lt"] = (r < t).astype(np.float32)
    return {k: np.ascontiguousarray(v) for k, v in out.items()}


def tokens(after):
    out = []
    for a in after:
        if isinstance(a, list):
            out += tokens(a)
        elif a is not None:
            out.append(a)
    return out


class Queue:

    def __init__(self, sem):
        self.sem, self.items, self.count = sem, [], 0

    def __call__(self, fn, *after):
        self.count += 1
        self.items.append((fn, tokens(after), self.sem, 1))
        return (self.sem, self.count)

    def dma(self, fn, sem_count, *after):
        sem_count[1] += 16
        self.items.append((fn, tokens(after), sem_count[0], 16))
        return (sem_count[0], sem_count[1])

    def wait(self, *after):
        self.items.append((None, tokens(after), None, 0))

    def emit(self, eng):
        seen = {}

        for fn, after, sem, inc in self.items:
            need = {}
            for s, n in after:
                if n > max(seen.get(id(s), 0), need.get(id(s), (s, 0))[1]):
                    need[id(s)] = (s, n)
            for s, n in need.values():
                seen[id(s)] = n
                eng.wait_ge(s, n)
            if fn is not None:
                fn(eng).then_inc(sem, inc)


class Bank:

    def __init__(self, ap):
        self.ap, self.free = ap, []


def build(nc, A, out):
    with ExitStack() as ctx:
        def sb(name, n, dt=F32):
            return ctx.enter_context(nc.sbuf_tensor(name, [128, n], dt))

        def sem(name):
            return ctx.enter_context(nc.semaphore(name))

        H = sb("H", 2 * D)[:].rearrange("p (t n) -> p t n", t=2)
        UTH = sb("UTH", NKT * 256, F32R)[:].rearrange("p (k n) -> p k n", k=NKT)
        UTL = sb("UTL", NKT * 256, F32R)[:].rearrange("p (k n) -> p k n", k=NKT)
        RAW = [sb(f"RAW{i}", SLOT)[:] for i in range(NRAW)]
        WH = [sb(f"WH{i}", SLOT, F32R)[:] for i in range(NW)]
        WL = [sb(f"WL{i}", SLOT, F32R)[:] for i in range(NW)]
        XS = [(UTH[:, i], UTL[:, i]) for i in range(3)]
        BIG = sb("BIG", 2 * CHUNKS_EVEN)[:]
        WORK = sb("WORK", 10752)[:]
        GB = WORK[:, 8704:10752]
        WC = sb("WC", 9 * 128)[:]
        MK = sb("MK", 8 * 128)[:]
        ONE = sb("ONE", 128)[:]
        SM = sb("SM", 512)[:]
        GP = sb("GP", 96)[:].rearrange("p (v k) -> p v k", v=6)
        ident = MK[:, 896:1024]
        PRE = WC[:, 1024:1152]
        SUF = WC[:, 896:1024]
        PS = ctx.enter_context(nc.psum_tensor("PS", [128, 8, 512], F32))
        banks = [Bank(PS[:, i, :]) for i in range(8)]

        sPE, sACT, sDVE, sPOOL = sem("s_pe"), sem("s_act"), sem("s_dve"), sem("s_pool")
        PE, ACT, DVE, POOL, SP = Queue(sPE), Queue(sACT), Queue(sDVE), Queue(sPOOL), Queue(None)
        raw_sems = [[sem(f"s_raw{i}"), 0] for i in range(NRAW)]
        d_const = [sem("s_const"), 0]
        d_par = [[sem(f"s_par{i}"), 0] for i in range(4)]
        d_first = [sem("s_first"), 0]
        d_x = [[sem(f"s_x{i}"), 0] for i in range(4)]
        d_out = [sem("s_out"), 0]

        def mm(out_, pairs, start=True, stop=True):
            def fn(e):
                last = None
                for j, (l, r) in enumerate(pairs):
                    last = e.matmul(out_, l, r, start=start and j == 0, stop=stop and j == len(pairs) - 1)
                return last
            return fn

        def many(*fns):
            def fn(e):
                last = None
                for f in fns:
                    last = f(e)
                return last
            return fn

        def tr(out_, in_):
            p = in_.shape[0]
            return lambda e: e.transpose(out_, in_, ident[0:p, 0:p])

        def copy(o, i, scale=1.0):
            return lambda e: e.activation(o, i, ACTF.Copy, scale=scale)

        def act(o, i, f, **k):
            return lambda e: e.activation(o, i, f, **k)

        def tt(o, a, b, op):
            return lambda e: e.tensor_tensor(o, a, b, op)

        def ts(o, a, s1, s2, op0, op1=None):
            if op1 is None:
                return lambda e: e.tensor_scalar(o, a, s1, None, op0)
            return lambda e: e.tensor_scalar(o, a, s1, s2, op0, op1)

        def stt(o, a, s, b, op0, op1):
            return lambda e: e.scalar_tensor_tensor(out=o, in0=a, scalar=s, in1=b, op0=op0, op1=op1)

        def cp(o, i):
            return lambda e: e.tensor_copy(o, i)

        def red(o, i, op):
            return lambda e: e.tensor_reduce(o, i, AX, op)

        def bc(ap, n):
            return ap.unsqueeze(2).to_broadcast([ap.shape[0], ap.shape[1], n])

        def rep(ap, n):
            return ap.unsqueeze(1).to_broadcast([ap.shape[0], n, ap.shape[1]])

        def v3(ap, a):
            return ap.rearrange("p (a b) -> p a b", a=a)

        SP.dma(lambda e: e.dma_start(ident, A["c_mk"][:, 896:1024]), d_first)
        t_first = SP.dma(lambda e: e.dma_start(GP, A["g_pre"]), d_first)
        t_x = [SP.dma(lambda e, c=512 * n: e.dma_start(
            H[:, :, c:c + 512], A["x"].rearrange("o (t p) n -> p (o t) n", p=128)[:, :, c:c + 512]), d_x[n])
            for n in range(4)]

        stream = []

        def add_cols(w, n0, n1, ktiles=NKT):
            wd = n1 - n0
            kk = min(ktiles, SLOT // 512 if wd > 64 else SLOT // wd)
            for k in range(0, ktiles, kk):
                src = w[128 * k:128 * (k + kk), n0:n1].rearrange("(k p) n -> p k n", p=128)
                stream.append((src, kk, wd))

        def add_rows(w, ktiles):
            for k in range(ktiles):
                for hf in range(2):
                    stream.append((w[128 * k:128 * k + 128, 1024 * hf:1024 * hf + 1024].unsqueeze(1), 1, 1024))

        def cuts(n):
            return [(a, min(a + 512, n)) for a in range(0, n, 512)]

        order_even = [(a, a + 512) for a in (4096, 5120, 6144)] + [(8192, 8208)] + [
            (a, a + 512) for a in (4608, 5632, 6656, 1024, 0, 2048, 1536, 512, 2560, 7168, 3072, 7680, 3584)]
        for a, b in order_even:
            if b - a < 512:
                for k in (0, 8):
                    stream.append((v3(A["ab_w_in_rest"], NKT)[:, k:k + 8], 8, b - a))
            else:
                add_cols(A["ab_w_in"][0], a, b)
        add_rows(A["ab_w_out"][0], 16)

        def add_ffn(l):
            for c in range(11):
                add_cols(A["ffn_w_gu"][l], 512 * c, 512 * c + 512)
                add_cols(A["ffn_w_gu"][l], DFF + 512 * c, DFF + 512 * c + 512)
            add_rows(A["ffn_w_down"][l], 44)

        add_ffn(0)
        order_nsa = [(a, a + 512) for a in (2048, 2560)] + [(5120, 5168)] + [
            (a, a + 512) for a in (3072, 0, 3584, 4096, 512, 4608, 1024, 1536)]
        for a, b in order_nsa:
            if b - a < 512:
                for k in (0, 8):
                    stream.append((v3(A["nsa_w_in_rest"], NKT)[:, k:k + 8], 8, b - a))
            else:
                add_cols(A["nsa_w_in"][0], a, b)
        add_rows(A["nsa_w_out"][0], 16)
        add_ffn(1)
        order_2 = (0, 2, 1, 3)
        for l in range(2):
            for c in order_2:
                add_cols(A["w_in_2"][l], 512 * c, 512 * c + 512)
            add_rows(A["w_out_2"][l], 4)

        hi_tok, lo_tok, used_tok = {}, {}, {}
        state = {"dma": 0, "prep": 0, "use": 0}

        def load(i):
            src, kk, wd = stream[i]
            dst = v3(RAW[i % NRAW][:, 0:kk * wd], kk)
            SP_tok = SP.dma(lambda e: e.dma_start(dst, src), raw_sems[i % NRAW],
                            hi_tok.get(i - NRAW), lo_tok.get(i - NRAW))
            return SP_tok

        raw_tok = {}

        def prep(upto):
            while state["prep"] <= min(upto, len(stream) - 1):
                i = state["prep"]
                while state["dma"] < min(i + NRAW, len(stream)):
                    raw_tok[state["dma"]] = load(state["dma"])
                    state["dma"] += 1
                kk, wd = stream[i][1:]
                n = kk * wd
                if wd < 64:
                    raw = v3(RAW[i % NRAW][:, 0:n], kk)
                    both = v3(WH[i % NW][:, 0:2 * n], kk)
                    wh, wl = both[:, :, 0:wd], both[:, :, wd:2 * wd]
                else:
                    raw, wh, wl = (x[:, 0:n] for x in (RAW[i % NRAW], WH[i % NW], WL[i % NW]))
                hi_tok[i] = ACT(copy(wh, raw), raw_tok[i], used_tok.get(i - NW))
                lo_tok[i] = DVE(tt(wl, raw, wh.bitcast(F32), ALU.subtract), hi_tok[i], used_tok.get(i - NW))
                state["prep"] += 1

        while state["dma"] < NRAW:
            raw_tok[state["dma"]] = load(state["dma"])
            state["dma"] += 1
        SP.dma(lambda e: e.dma_start(MK[:, 0:896], A["c_mk"][:, 0:896]), d_const)
        for dst, name in ((WC, "c_wc"), (ONE, "c_one")):
            SP.dma(lambda e, d=dst, n=name: e.dma_start(d, A[n]), d_const)

        def next_slot():
            i = state["use"]
            state["use"] += 1
            prep(i + LEAD)
            kk, wd = stream[i][1:]
            if wd < 64:
                return i, v3(WH[i % NW][:, 0:2 * kk * wd], kk), None
            return i, v3(WH[i % NW][:, 0:kk * wd], kk), v3(WL[i % NW][:, 0:kk * wd], kk)

        def narrow(c, wd, xh, xl, pair, sink, spare):
            acc = pair[0].ap[0:2 * wd, 0:256]
            for k in (0, 8):
                i, both, _ = next_slot()
                fns = [mm(acc, [(both[:, j], xh[:, k + j]), (both[:, j], xl[:, k + j])],
                          start=k + j == 0, stop=k + j == NKT - 1) for j in range(8)]
                used_tok[i] = PE(many(*fns), hi_tok[i], lo_tok[i], pair[0].free)
                if k == 0:
                    yield
            T, S = spare[0:2 * wd, 0:256], v3(spare[:, 256:256 + 2 * wd], 2)
            w = ACT(copy(T, acc), used_tok[i])
            pair[0].free = [w]
            yield
            p = PE(many(*[tr(pair[1].ap[:, 128 * t:128 * t + 2 * wd], T[:, 128 * t:128 * t + 128])
                          for t in range(2)]), w, pair[1].free)
            ps = v3(pair[1].ap[:, 0:256], 2)
            a = ACT(copy(S, ps[:, :, 0:wd]), p)
            a = DVE(tt(S, S, ps[:, :, wd:2 * wd], ALU.add), a)
            pair[1].free = [a]
            used_tok[i] = [a] + [sink(c, t, S[:, t], a) for t in range(2)]
            yield

        def use_cols(widths, xh, xl, after, feed, sink, spare=None, ktiles=NKT):
            ring["wide"] = False
            for c, wd in enumerate(widths):
                pair = [banks[2 * (c % 2) + t] for t in range(2)]
                if wd < 64:
                    yield from narrow(c, wd, xh, xl, pair, sink, spare)
                    continue
                k = 0
                while k < ktiles:
                    kk = stream[state["use"]][1]
                    while len(after) < min(k + kk + 2, ktiles):
                        next(feed)
                    i, wh, wl = next_slot()
                    fns = []
                    for j in range(kk):
                        for t in range(2):
                            o = pair[t].ap[:, 0:wd]
                            lh, ll = xh[:, k + j, 128 * t:128 * t + 128], xl[:, k + j, 128 * t:128 * t + 128]
                            fns.append(mm(o, [(lh, wh[:, j]), (lh, wl[:, j]), (ll, wh[:, j])],
                                          start=k + j == 0, stop=k + j == ktiles - 1))
                    used_tok[i] = PE(many(*fns), hi_tok[i], lo_tok[i], [after[j] for j in range(k, k + kk)],
                                     pair[0].free, pair[1].free)
                    k += kk
                    if k < ktiles:
                        yield
                drain(feed)
                for t in range(2):
                    pair[t].free = [sink(c, t, pair[t].ap[:, 0:wd], used_tok[i])]
                yield

        def use_rows(ktiles, operand, after):
            busy = [b.free for b in banks]
            for k in range(ktiles):
                xh, xl, ready = operand(k)
                for hf in range(2):
                    i, wh, wl = next_slot()
                    fns = []
                    for t in range(2):
                        for n in range(2):
                            o = banks[4 * t + 2 * hf + n].ap
                            cs = slice(512 * n, 512 * n + 512)
                            lh, ll = xh[:, 128 * t:128 * t + 128], xl[:, 128 * t:128 * t + 128]
                            fns.append(mm(o, [(lh, wh[:, 0, cs]), (lh, wl[:, 0, cs]), (ll, wh[:, 0, cs])],
                                          start=k == 0, stop=k == ktiles - 1))
                    used_tok[i] = PE(many(*fns), hi_tok[i], lo_tok[i], after, ready, busy)
                yield used_tok[i]

        ring = {"n": 0, "wide": False}

        def bank():
            ring["n"] += 1
            return banks[ring["n"] % 8 if ring["wide"] else 4 + ring["n"] % 4]

        def drain(g):
            last = None
            for x in g:
                last = x if x is not None else last
            return last

        def together(main, *sides):
            sides = list(sides)
            for _ in main:
                for g in sides:
                    next(g, None)
            ring["wide"] = True
            while sides:
                sides = [g for g in sides if next(g, "end") != "end"]

        def need(*keys):
            while any(k not in zt for k in keys):
                yield

        def to_T(toks, src, tiles, after, gain=None):
            for k in range(0, tiles, 2):
                b = bank()
                fns = [tr(b.ap[:, 256 * j + 128 * t:256 * j + 128 * t + 128], src(k + j, t))
                       for j in range(2) for t in range(2)]
                p = PE(many(*fns), after[k], after[k + 1], b.free, t_first)
                if gain is None:
                    hi = ACT(copy(UTH[:, k:k + 2], v3(b.ap, 2)), p)
                    lo = DVE(tt(UTL[:, k:k + 2], v3(b.ap, 2), UTH[:, k:k + 2].bitcast(F32), ALU.subtract), hi)
                else:
                    for j in range(2):
                        hi = ACT(copy(UTH[:, k + j], b.ap[:, 256 * j:256 * j + 256], gain[:, k + j:k + j + 1]), p)
                    for j in range(2):
                        lo = DVE(stt(UTL[:, k + j], b.ap[:, 256 * j:256 * j + 256], gain[:, k + j:k + j + 1],
                                     UTH[:, k + j].bitcast(F32), ALU.mult, ALU.subtract), hi)
                b.free = [lo]
                toks += [[hi, lo]] * 2
                yield

        RSQ = sb("RSQ", 8 * 24)[:]
        rsq = {"n": 0, "free": [None] * 8}
        JUNK = BIG[:, 15360:15872]
        NS = SM[:, 440:504]
        BNS, BNA = v3(NS[:, 32:56], 4), NS[:, 56:58]
        HSQ, HS2, HR, MSQ, MS2, MR = (NS[:, a:b] for a, b in ((0, 8), (8, 10), (10, 12), (12, 20), (20, 22), (22, 24)))

        def rstd(o, ss, n, after, gain=1.0, free=None):
            j = rsq["n"] % 8
            rsq["n"] += 1
            w = ss.shape[1]
            x, y, z = (RSQ[:, 24 * j + 8 * i:24 * j + 8 * i + w] for i in range(3))
            a = DVE(ts(x, ss, 1.0 / n, EPS, ALU.mult, ALU.add), after, rsq["free"][j])
            b = ACT(act(y, x, ACTF.Sqrt), a)
            b = DVE(rec(y, y), b)
            a = DVE(tt(z, y, y, ALU.mult), b)
            a = DVE(tt(z, z, x, ALU.mult), a)
            a = DVE(ts(z, z, -0.5 * gain, 1.5 * gain, ALU.mult, ALU.add), a)
            a = DVE(tt(o, y, z, ALU.mult), a, free)
            rsq["free"][j] = a
            return a

        def rec(o, i):
            return lambda e: e.reciprocal(o, i)

        def sigm(e_, after):
            a = DVE(ts(e_, e_, 1.0, None, ALU.add), after)
            return DVE(rec(e_, e_), a)

        junk = {"tok": None}

        def square(t, n, after):
            junk["tok"] = ACT(act(JUNK, H[:, t, 512 * n:512 * n + 512], ACTF.Square,
                                  accum_out=HSQ[:, 4 * t + n:4 * t + n + 1]), after, junk["tok"])
            return junk["tok"]

        def pre_norm(gain, h):
            toks = []

            def feed():
                sq = h["sq"] = []
                inner = to_T(toks, lambda k, t: H[:, t, 128 * k:128 * k + 128], NKT,
                             [[h[(t, k // 4)] for t in range(2)] for k in range(NKT)], gain)
                for k, _ in enumerate(inner):
                    if k % 2:
                        for t in range(2):
                            sq.append(square(t, k // 2, h[(t, k // 2)]))
                    if k < NKT // 2 - 1:
                        yield
                a = DVE(red(HS2, v3(HSQ, 2), ALU.add), sq)
                zt["r"] = rstd(HR, HS2, D, a, 1.0, h.get("z"))
                yield

            return toks, feed()

        def warm(func):
            ACT(act(SM[:, 31:32], one_b, func), ones_act)

        def load_gb(row, n, after):
            return POOL.dma(lambda e: e.dma_start(GB, row.partition_broadcast(128)), d_par[n], after)

        def post_norm(t_gb, after, z=None):
            sq = [[], []]
            for n in range(4):
                junk["tok"] = ACT(act(JUNK, banks[n].ap, ACTF.Square, accum_out=MSQ[:, n:n + 1]), after, junk["tok"])
                sq[0].append(junk["tok"])
                sq[1].append(DVE(lambda e, n=n: e.bn_stats(out=BNS[:, n], in_=banks[4 + n].ap), after))
            a = DVE(lambda e: e.bn_aggr(out=BNA, in_=BNS), sq[1])
            a = DVE(stt(MS2[:, 1:2], BNA[:, 0:1], BNA[:, 0:1], BNA[:, 1:2], ALU.mult, ALU.add), a)
            a = [DVE(ts(MS2[:, 1:2], MS2[:, 1:2], float(D), None, ALU.mult), a)]
            a.append(DVE(red(MS2[:, 0:1], MSQ[:, 0:4], ALU.add), sq[0]))
            r = rstd(MR, MS2, D, a)
            h, adds = {}, []
            for n in range(4):
                for t in (1, 0):
                    j = 2 * n + 1 - t
                    bk = banks[4 * t + n]
                    tmp = WORK[:, 1024 + 512 * (j % 4):1536 + 512 * (j % 4)]
                    m = DVE(stt(tmp, bk.ap, MR[:, t:t + 1], GB[:, 512 * n:512 * n + 512],
                                ALU.mult, ALU.mult), r, t_gb, adds[j - 4] if j >= 4 else None)
                    bk.free = [m]
                    hc = H[:, t, 512 * n:512 * n + 512]
                    adds.append((POOL if t else DVE)(tt(hc, hc, tmp, ALU.add), m))
                    h[(t, n)] = adds[-1]
            h["z"] = z
            return h

        def plain_add(after):
            h = {}
            for n in range(4):
                for t in range(2):
                    hc = H[:, t, 512 * n:512 * n + 512]
                    m = DVE(tt(hc, banks[4 * t + n].ap, hc, ALU.add), after)
                    banks[4 * t + n].free = [m]
                    h[(t, n)] = m
            return h

        def out_proj(tiles, src, after):
            u = []
            drain(to_T(u, src, tiles, after))
            warm(ACTF.Sqrt)
            return drain(use_rows(tiles, lambda k: (UTH[:, k], UTL[:, k], u[k]), None))

        def finish(after):
            o = out.rearrange("o (t p) n -> p (o t) n", p=128)
            SP.dma(lambda e: e.dma_start(o, H), d_out, after)
            SP.wait((d_out[0], d_out[1]))

        def all_of(h):
            return [h[(t, n)] for t in range(2) for n in range(4)]

        def ffn(l, row, gain, h):
            u, feed = pre_norm(gain, h)
            t_gb = load_gb(row, 0, all_of(h))
            HT = BIG[:, 0:44 * 256].rearrange("p (k n) -> p k n", k=44)
            G = [[BIG[:, 11264 + 1024 * x + 512 * t:11264 + 1024 * x + 512 * t + 512] for t in range(2)]
                 for x in range(4)]
            gate_tok, trs_tok, ht_tok, z = {}, {}, [], []

            def sink(c, t, ap, tok):
                x = (c // 2) % 2
                g = G[x][t]
                if c % 2 == 0:
                    gate_tok[t] = ACT(act(g, ap, ACTF.Silu, scale=HR[:, t:t + 1]), tok, zt["r"], trs_tok.get((x, t)))
                    return gate_tok[t]
                f = DVE(stt(g, ap, HR[:, t:t + 1], g, ALU.mult, ALU.mult), tok, gate_tok[t], zt["r"])
                z.append(f)
                b = bank()
                fns = [tr(b.ap[:, 128 * j:128 * j + 128], g[:, 128 * j:128 * j + 128]) for j in range(4)]
                p = PE(many(*fns), f, b.free)
                trs_tok[(x, t)] = p
                k = 4 * (c // 2)
                e = ACT(copy(HT[:, k:k + 4, 128 * t:128 * t + 128], v3(b.ap, 4)), p)
                b.free = [e]
                ht_tok.append(e)
                return f

            drain(use_cols([512] * 22, UTH, UTL, u, feed, sink))
            warm(ACTF.Sqrt)

            used = {}

            def operand(k):
                xh, xl = XS[k % 3]
                hi = ACT(copy(xh, HT[:, k]), ht_tok, used.get(k - 3))
                lo = DVE(tt(xl, HT[:, k], xh.bitcast(F32), ALU.subtract), hi, used.get(k - 3))
                return xh, xl, [hi, lo]

            pending = {0: operand(0), 1: operand(1)}

            def ahead(k):
                return pending[k]

            last = None
            for k, last in enumerate(use_rows(44, ahead, None)):
                used[k] = last
                if k + 2 < 44:
                    pending[k + 2] = operand(k + 2)
            return post_norm(t_gb, last, z)

        Z = v3(BIG, 2)

        def zcol(t, c, n):
            return Z[:, t, c:c + n]

        zt = {}

        def z_sink_even(c, t, ap, tok):
            a, b = order_even[c]
            zt[(a, t)] = ACT(copy(zcol(t, a, b - a), ap, HR[:, t:t + 1]), tok, zt["r"])
            return zt[(a, t)]

        SMG = SM[:, 32:512]
        LD = v3(SMG[:, 0:16], 2)
        BETA = v3(SMG[:, 16:32], 2)
        EG = v3(SMG[:, 32:80], 2)
        TMP = SMG[:, 80:240]
        DTB, NEA = SMG[:, 240:248], SMG[:, 248:256]
        HG = sb("HG", 128)[:]
        DG = sb("DG", 128)[:]
        CW = sb("CW", 96)[:].rearrange("p (c j) -> p c j", j=4)
        for dst, src in ((DTB, A["gdn_dt_bias"][0:1]), (NEA, A["gdn_a_log"][0:1]),
                         (HG, A["hgrn_norm_g"][0:1]), (DG, A["gdn_norm_g"][0:1])):
            t_const = SP.dma(lambda e, d=dst, s=src: e.dma_start(d, s[0].partition_broadcast(128)), d_const)
        t_const = SP.dma(lambda e: e.dma_start(CW, A["conv_w"]), d_const)
        ones_act = POOL(lambda e: e.memset(SM[:, 30:31], 1.0))
        one_b = SM[:, 30:31]

        def gdn_gates():
            ba = Z[:, :, 8192:8200]
            bb = Z[:, :, 8200:8208]
            z = [zt[(8192, 0)], zt[(8192, 1)]]
            x, ax, e1, l1 = (v3(TMP[:, 16 * j:16 * j + 16], 2) for j in range(4))
            a = DVE(tt(x, ba, rep(DTB, 2), ALU.add), z, t_const)
            b = ACT(act(ax, x, ACTF.Abs), a)
            b = ACT(act(e1, ax, ACTF.Exp, scale=-1.0), b)
            b = ACT(act(l1, e1, ACTF.Ln, bias=one_b), b, ones_act)
            c = DVE(stt(x, x, 0.0, l1, ALU.max, ALU.add), b)
            n = ACT(act(NEA, NEA, ACTF.Exp), t_const)
            n = DVE(ts(NEA, NEA, -1.0, None, ALU.mult), n)
            ld = DVE(tt(LD, x, rep(NEA, 2), ALU.mult), c, n)
            s = ACT(act(e1, bb, ACTF.Exp, scale=-1.0), z, c)
            beta = DVE(ts(e1, e1, 1.0, None, ALU.add), s)
            beta = DVE(rec(BETA, e1), beta)
            yield
            b_ = bank()
            fns = []
            for i in range(2):
                for j, m in enumerate((PRE, SUF, ONE)):
                    fns.append(mm(b_.ap[:, 24 * i + 8 * j:24 * i + 8 * j + 8], [(m, LD[:, i])]))
            p = PE(many(*fns), ld, b_.free)
            eg = ACT(act(EG, v3(b_.ap[:, 0:48], 2), ACTF.Exp), p)
            b_.free = [eg]
            zt["gates"] = [ld, beta, eg]
            yield

        def w3(o, n, a):
            return v3(WORK[:, o:o + n], a)

        done = {"g": [], "h": []}

        def conv_half(hf):
            F = [w3(5632, 1024, 4), w3(6656, 1024, 4)]
            E = [w3(7680, 1024, 4), w3(8704, 1024, 4)]
            last = {}
            normed = None
            for part, c0 in enumerate((4096, 5120, 6144)):
                yield from need((c0 + 512 * hf, 0), (c0 + 512 * hf, 1))
                f, e_ = F[part % 2], E[part % 2]
                z = [zt[(c0 + 512 * hf, t)] for t in range(2)]
                taps = []
                trs = []
                for pr in range(2):
                    b = bank()
                    fns = [tr(b.ap[:, 256 * j + 128 * t:256 * j + 128 * t + 128],
                              zcol(t, c0 + 512 * hf + 256 * pr + 128 * j, 128)) for j in range(2) for t in range(2)]
                    p = PE(many(*fns), z, b.free)
                    trs.append(p)
                    rd = []
                    for j in range(2):
                        ch = 8 * part + 4 * hf + 2 * pr + j
                        k0 = ACT(copy(f[:, 2 * pr + j], b.ap[:, 256 * j:256 * j + 256], CW[:, ch, 3:4]),
                                 p, last.get(part - 2), done["h"], t_const)
                    for j in range(2):
                        h = 2 * pr + j
                        ch = 8 * part + 4 * hf + h
                        k = k0
                        for d in range(1, 4):
                            k = DVE(stt(f[:, h, d:256], b.ap[:, 256 * j:256 * j + 256 - d], CW[:, ch, 3 - d:4 - d],
                                        f[:, h, d:256], ALU.mult, ALU.add), k)
                        rd.append(k)
                    b.free = rd
                    taps += rd
                    yield
                s = ACT(act(f, f, ACTF.Silu), taps)
                yield
                reads, sums = [], []
                for t in range(2):
                    b = bank()
                    p = PE(many(*[tr(b.ap[:, 128 * j:128 * j + 128], f[:, j, 128 * t:128 * t + 128])
                                  for j in range(4)]), s, b.free)
                    reads.append(p)
                    dst = zcol(t, c0 + 512 * hf, 512)
                    w = ACT(copy(dst, b.ap), p, trs)
                    b.free = [w]
                    if part == 2:
                        zt[("n", part, hf, t)] = w
                        yield
                        continue
                    sq = ACT(act(e_[:, 2 * t:2 * t + 2], v3(dst, 2), ACTF.Square), w, s)
                    ss = TMP[:, 8 * part:8 * part + 8]
                    r = DVE(red(ss[:, 4 * t:4 * t + 4], e_[:, 2 * t:2 * t + 2].rearrange("p a (b c) -> p (a b) c", b=2),
                                ALU.add), sq, normed)
                    reads.append(r)
                    sums.append(r)
                    yield
                if part < 2:
                    r = rstd(ss, ss, 1, sums, QSCALE if part == 0 else 1.0)
                    yield
                    normed = []
                    for t in range(2):
                        dst = v3(zcol(t, c0 + 512 * hf, 512), 4)
                        w = DVE(tt(dst, dst, bc(ss[:, 4 * t:4 * t + 4], 128), ALU.mult), r, trs)
                        normed.append(w)
                        zt[("n", part, hf, t)] = w
                last[part] = reads
            done["h"] = [last[p] for p in range(3)] + [zt[("n", p, hf, t)] for p in range(3) for t in range(2)]

        def gdn_group(hf, i, carry):
            yield from need("gates", *[("n", p, hf, i) for p in range(3)])
            ld, beta, eg = zt["gates"]
            free = done["g"]
            hs = range(4)
            ADEC, DEC, KB, KT = (w3(512 * j, 512, 4) for j in range(4))
            KBT, QT, LT, QK = (w3(2048 + 512 * j, 512, 4) for j in range(4))
            XX = WORK[:, 4096:5120].rearrange("p (h x n) -> p h x n", h=4, x=2)
            Y, LTM = KT, QT
            S = w3(5120, 512, 4)
            RV, RW = ADEC, DEC
            qz, kz, vz = (v3(zcol(i, c + 512 * hf, 512), 4) for c in (4096, 5120, 6144))
            tq, tk, tv = (zt[("n", p, hf, i)] for p in range(3))
            hsl = slice(4 * hf, 4 * hf + 4)
            a = POOL(tt(ADEC, rep(SUF, 4), bc(LD[:, i, hsl], 128), ALU.mult), ld, free)
            kb = DVE(tt(KB, kz, bc(BETA[:, i, hsl], 128), ALU.mult), beta, tk, free)
            x0 = POOL(cp(XX[:, :, 0], rep(ident, 4)), free)
            x1 = POOL(cp(XX[:, :, 1], rep(ident, 4)), free)
            yield
            b = bank()
            p = PE(many(*[mm(b.ap[:, 128 * h:128 * h + 128], [(ADEC[:, h], PRE)]) for h in hs]), a, b.free)
            dec = ACT(act(DEC, v3(b.ap, 4), ACTF.Exp), p, free)
            b.free = [dec]
            toks = []
            for src, dst, tok, eng in ((kz, KT, tk, 0), (KB, KBT, kb, 1), (qz, QT, tq, 0)):
                b = bank()
                p = PE(many(*[tr(b.ap[:, 128 * h:128 * h + 128], src[:, h]) for h in hs]), tok, b.free)
                if eng:
                    w = DVE(cp(dst, v3(b.ap, 4)), p, free)
                else:
                    w = ACT(copy(dst, v3(b.ap, 4)), p, free)
                b.free = [w]
                toks.append(w)
            tkT, tkbT, tqT = toks
            yield
            b = bank()
            p = PE(many(*[mm(b.ap[:, 128 * h:128 * h + 128], [(KT[:, h], KBT[:, h])]) for h in hs]), tkT, tkbT, b.free)
            lt = DVE(tt(LT, v3(b.ap, 4), DEC, ALU.mult), p, dec, free)
            b.free = [lt]
            b = bank()
            p = PE(many(*[mm(b.ap[:, 128 * h:128 * h + 128], [(KT[:, h], QT[:, h])]) for h in hs]), tqT, b.free)
            qk0 = DVE(tt(QK, v3(b.ap, 4), DEC, ALU.mult), p, free)
            b.free = [qk0]
            qk = POOL(tt(QK, QK, rep(PRE, 4), ALU.mult), qk0)
            yield
            xx = [x0, x1]
            py = None
            m = POOL(tt(LTM, LT, rep(MK[:, 0:128], 4), ALU.mult), lt, qk0)
            rv = DVE(tt(RV, vz, bc(BETA[:, i, hsl], 128), ALU.mult), tv, dec, qk0)
            if i == 0:
                KD = RW
                kd = POOL(tt(KD, kz, bc(EG[:, i, 8 + 4 * hf:12 + 4 * hf], 128), ALU.mult), eg, lt, qk0)
            else:
                rw = POOL(tt(RW, KB, bc(EG[:, i, hsl], 128), ALU.mult), eg, lt, qk0)
            yield
            for l in range(7):
                b = bank()
                py = PE(many(*[mm(b.ap[:, 128 * h:128 * h + 128], [(LTM[:, h], XX[:, h, 0])]) for h in hs]),
                        m, xx, b.free)
                y = ACT(copy(Y, v3(b.ap, 4)), py)
                b.free = [y]
                if l < 6:
                    m = POOL(tt(LTM, LT, rep(MK[:, 128 * (l + 1):128 * (l + 2)], 4), ALU.mult), py)
                yield
                b0, b1 = bank(), bank()
                fns = []
                for h in hs:
                    bb = (b0, b1)[h // 2].ap[:, 256 * (h % 2):256 * (h % 2) + 256]
                    fns.append(mm(bb[:, 0:128], [(XX[:, h, 1], Y[:, h])]))
                    fns.append(mm(bb[:, 128:256], [(Y[:, h], XX[:, h, 1])]))
                p = PE(many(*fns), y, b0.free, b1.free)
                xx = []
                for j, bb in enumerate((b0, b1)):
                    o = XX[:, 2 * j:2 * j + 2].rearrange("p h x n -> p (h x n)")
                    u = DVE(tt(o, o, bb.ap, ALU.subtract), p)
                    bb.free = [u]
                    xx.append(u)
                yield
            bu = bank()
            pu = PE(many(*[mm(bu.ap[:, 128 * h:128 * h + 128], [(XX[:, h, 1], RV[:, h])]) for h in hs]),
                    rv, xx, bu.free)
            U = KB
            if i == 0:
                u = ACT(copy(U, v3(bu.ap, 4)), pu, tkbT)
                bu.free = [u]
                yield
                bs = bank()
                ps = PE(many(*[mm(bs.ap[:, 128 * h:128 * h + 128], [(KD[:, h], U[:, h])]) for h in hs]),
                        u, kd, bs.free)
                s = DVE(cp(S, v3(bs.ap, 4)), ps, free)
                bs.free = [s]
                bo = bank()
                po = PE(many(*[mm(bo.ap[:, 128 * h:128 * h + 128], [(QK[:, h], U[:, h])]) for h in hs]), qk, u, bo.free)
                carry["s"] = s
                used = [po, ps]
            else:
                bw = bank()
                pw = PE(many(*[mm(bw.ap[:, 128 * h:128 * h + 128], [(RW[:, h], XX[:, h, 1])]) for h in hs]),
                        rw, bw.free)
                WT = KBT
                wt = ACT(copy(WT, v3(bw.ap, 4)), pw)
                bw.free = [wt]
                QE = Y
                qe = POOL(tt(QE, qz, bc(EG[:, i, hsl], 128), ALU.mult), eg, tq, xx)
                u0 = ACT(copy(U, v3(bu.ap, 4)), pu, rw, tkbT)
                bu.free = [u0]
                yield
                bs = bank()
                ps = PE(many(*[mm(bs.ap[:, 128 * h:128 * h + 128], [(WT[:, h], S[:, h])]) for h in hs]),
                        wt, carry["s"], bs.free)
                u = DVE(tt(U, U, v3(bs.ap, 4), ALU.subtract), ps, u0)
                bs.free = [u]
                bq = bank()
                pq = PE(many(*[tr(bq.ap[:, 128 * h:128 * h + 128], QE[:, h]) for h in hs]), qe, bq.free)
                qt = ACT(copy(QT, v3(bq.ap, 4)), pq, py)
                bq.free = [qt]
                yield
                bo = bank()
                po = PE(many(*[mm(bo.ap[:, 128 * h:128 * h + 128], [(QT[:, h], S[:, h]), (QK[:, h], U[:, h])])
                               for h in hs]), qt, u, qk, bo.free)
                used = [po]
            w = ACT(copy(zcol(i, 4096 + 512 * hf, 512), bo.ap), po, tqT, used)
            bo.free = [w]
            zt[("ob", hf, i)] = [w, used]
            done["g"] = [used, w]
            yield

        def out_gate(a, hf, gain, *keys):
            c0, gc, ec = 4096 * a + 512 * hf, (3072, 7168)[a] + 512 * hf, (1024, 5120)[a] + 512 * hf
            yield from need((gc, 1))
            o3, g3, e3 = ([v3(zcol(i, c, 512), 4) for i in range(2)] for c in (c0, gc, ec))
            sg = [ACT(act(g3[i], g3[i], ACTF.Silu), zt[(gc, i)]) for i in range(2)]
            sg = [POOL(tt(g3[i], g3[i], rep(gain, 4), ALU.mult), sg[i], t_const) for i in range(2)]
            yield
            yield from need(*keys)
            ready = [zt[k] for k in keys]
            ss = TMP[:, 64 + 16 * a + 8 * hf:72 + 16 * a + 8 * hf]
            sq = [ACT(act(e3[i], o3[i], ACTF.Square), ready) for i in range(2)]
            sq = [DVE(red(ss[:, 4 * i:4 * i + 4], e3[i], ALU.add), sq[i]) for i in range(2)]
            yield
            r = rstd(ss, ss, 128, sq)
            yield
            for i in range(2):
                m = DVE(tt(o3[i], o3[i], bc(ss[:, 4 * i:4 * i + 4], 128), ALU.mult), r)
                zt[("o", a, hf, i)] = POOL(tt(o3[i], o3[i], g3[i], ALU.mult), m, sg[i])

        def gdn():
            yield from need((8192, 1))
            yield from gdn_gates()
            for hf in range(2):
                carry = {}
                for i in range(2):
                    yield from gdn_group(hf, i, carry)

        def convs():
            for hf in range(2):
                yield from conv_half(hf)
            zt["convs"] = True

        def hgrn():
            for hf in range(2):
                yield from need("convs", *[(c + 512 * hf, 1) for c in (1024, 0, 2048)])
                KK = w3(5632, 1024, 2)
                L1 = w3(6656, 1024, 2)
                x = Z[:, :, 1024 + 512 * hf:1536 + 512 * hf]
                tz = [zt[(1024 + 512 * hf, t)] for t in range(2)]
                a = ACT(act(L1, x, ACTF.Abs), tz, done["h"])
                a = ACT(act(L1, L1, ACTF.Exp, scale=-1.0), a)
                a = ACT(act(L1, L1, ACTF.Ln, bias=one_b), a)
                k0 = DVE(stt(KK, x, 0.0, L1, ALU.max, ALU.add), a, done["h"])
                lf = DVE(stt(x, x, 0.0, L1, ALU.min, ALU.subtract), a, k0)
                kk = ACT(act(KK, KK, ACTF.Exp, scale=-1.0), k0)
                yield
                o0 = 6656
                QKT = [w3(o0 + 256 * j, 256, 2) for j in range(2)]
                E = [w3(o0 + 512 + 512 * j, 512, 4) for j in range(2)]
                QE = E
                KE = [w3(o0 + 1536 + 512 * j, 512, 4) for j in range(2)]
                KE7 = WORK[:, o0 + 2560:o0 + 2688]
                ATM = w3(o0 + 2688, 1024, 8)
                AT = [WORK[:, o0 + 3712 + 128 * j:o0 + 3840 + 128 * j] for j in range(3)]
                start = [lf, done["h"]]
                fr = {"qk": [start, start], "e": [start, start], "s": [start, start], "atm": start,
                      "at": [start] * 4, "ke7": start}
                ends = []
                units = [{"h": h, "i": i, "cq": 512 * hf + 128 * h} for h in range(4) for i in range(2)]

                def factors(n, u):
                    h, i, cq = u["h"], u["i"], u["cq"]
                    qk_ = QKT[n % 2]
                    b = bank()
                    p = PE(many(tr(b.ap[:, 0:128], zcol(i, cq, 128)),
                                tr(b.ap[:, 128:256], KK[:, i, 128 * h:128 * h + 128])),
                           zt[(512 * hf, i)], kk, b.free)
                    u["tqk"] = ACT(copy(qk_, v3(b.ap[:, 0:256], 2)), p, fr["qk"][n % 2])
                    b.free = [u["tqk"]]
                    pref = zcol(i, 1024 + cq, 128)
                    u["es"] = []
                    for g in range(2):
                        b = bank()
                        if g == 1 and i == 1:
                            f = many(mm(b.ap[:, 0:384], [(pref, WC[:, 512:896])]),
                                     mm(b.ap[:, 384:512], [(pref, PRE)]))
                        else:
                            f = mm(b.ap, [(pref, WC[:, 512 * g:512 * g + 512])])
                        p = PE(f, lf, b.free)
                        e = ACT(act(E[g], v3(b.ap, 4), ACTF.Exp), p, fr["e"][g])
                        b.free = [e]
                        u["es"].append(e)

                def products(n, u):
                    i, es, tqk = u["i"], u["es"], u["tqk"]
                    qT, kT = QKT[n % 2][:, 0], QKT[n % 2][:, 1]
                    u["kq"] = []
                    for g in range(2):
                        k7 = None
                        if g == 1 and i == 0:
                            ke = POOL(tt(KE[g][:, 0:3], E[g][:, 0:3], rep(kT, 3), ALU.mult), es[g], tqk, fr["s"][g])
                            k7 = fr["k7"] = POOL(tt(KE7, E[g][:, 3], kT, ALU.mult), es[g], tqk, fr["ke7"])
                        else:
                            ke = POOL(tt(KE[g], E[g], rep(kT, 4), ALU.mult), es[g], tqk, fr["s"][g])
                        qe = DVE(tt(QE[g], E[g], rep(qT, 4), ALU.mult), ke, k7)
                        u["kq"].append([ke, qe])

                def scores(n, u):
                    i = u["i"]
                    qT, kT = QKT[n % 2][:, 0], QKT[n % 2][:, 1]
                    u["at"] = []
                    for g in range(2):
                        ke, qe = u["kq"][g]
                        b = bank()
                        fns = [mm(b.ap[:, 128 * l:128 * l + 128], [(KE[g][:, l], QE[g][:, l])])
                               for l in range(4 - g)]
                        if g == 1:
                            fns.append(mm(b.ap[:, 384:512], [(kT, qT)]))
                        p = PE(many(*fns), qe, ke, b.free)
                        mtok = DVE(tt(ATM[:, 4 * g:4 * g + 4].rearrange("p a b -> p (a b)"), b.ap,
                                      MK[:, 512 * g:512 * g + 512], ALU.mult), p, fr["atm"])
                        b.free = [mtok]
                        fr["s"][g] = fr["e"][g] = [p]
                        u["at"].append(mtok)
                        if g == 1 and i == 1:
                            b = bank()
                            p = PE(mm(b.ap[:, 0:128], [(KE7, QE[1][:, 3])]), fr["k7"], b.free)
                            fr["ke7"] = [p]
                            fr["s"][1] = fr["e"][1] = [p]
                            u["c7"] = ACT(copy(AT[2], b.ap[:, 0:128]), p, fr["at"][2])
                            b.free = [u["c7"]]
                    fr["qk"][n % 2] = [p, u["kq"]]

                def sum_levels(n, u):
                    u["ra"] = DVE(red(AT[n % 2], ATM.rearrange("p l t -> p t l"), ALU.add), u["at"], fr["at"][n % 2])
                    fr["atm"] = [u["ra"]]

                def values(n, u):
                    i, cq = u["i"], u["cq"]
                    pairs = [(AT[n % 2], zcol(i, 2048 + cq, 128))]
                    if i == 1:
                        pairs.append((AT[2], zcol(0, 2048 + cq, 128)))
                    b = bank()
                    p = PE(mm(b.ap[:, 0:128], pairs), u["ra"], u.get("c7"), zt[(2048 + 512 * hf, 0)],
                           zt[(2048 + 512 * hf, 1)], b.free)
                    fr["at"][n % 2] = [p]
                    if i == 1:
                        fr["at"][2] = [p]
                    w = ACT(copy(zcol(i, cq, 128), b.ap[:, 0:128]), p)
                    b.free = [w]
                    ends.append(w)
                    return p

                factors(0, units[0])
                yield
                products(0, units[0])
                yield
                for n, u in enumerate(units):
                    scores(n, u)
                    if n + 1 < len(units):
                        factors(n + 1, units[n + 1])
                    yield
                    sum_levels(n, u)
                    if n + 1 < len(units):
                        products(n + 1, units[n + 1])
                    yield
                    p = values(n, u)
                done["h"] = [ends, p]
                zt[("oa", hf)] = [ends, p]

        ZN = v3(BIG[:, 0:2 * 5168], 2)
        SP0 = 2 * 5168

        def nsa_sink(c, t, ap, tok):
            a, b = order_nsa[c]
            zt[("n", a, t)] = ACT(copy(ZN[:, t, a:b], ap, HR[:, t:t + 1]), tok, zt["r"])
            return zt[("n", a, t)]

        def nsa(tables):
            W1 = BIG[:, SP0:SP0 + 4096].rearrange("p (l n) -> p l n", l=32)
            BLK = BIG[:, SP0 + 4096:SP0 + 6016].rearrange("p (j g l) -> p j g l", j=15, g=4)
            POS = w3(0, 64, 2)
            W2 = w3(64, 256, 2)
            CT = WORK[:, 320:1344].rearrange("p (g t) -> p g t", g=4)
            HC = WORK[:, 1344:1404]
            HE = WORK[:, 1404:1464]
            KC = WORK[:, 1472:1532].rearrange("p (j g) -> p j g", g=4)
            VC = w3(1536, 512, 4)
            GT = v3(SM[:, 32:128], 2)
            ST = SM[:, 128:192]
            DB = WORK[:, 7168:8704]
            DC = v3(SM[:, 200:320], 2)
            MC = v3(SM[:, 320:440], 2)
            tp = POOL.dma(lambda e: e.dma_start(POS, A["pos"]), d_par[1], tables)
            tp = POOL.dma(lambda e: e.dma_start(W2, A["nsa_cmp_w2"][0].rearrange("c p n -> p c n")), d_par[1], tables)
            for dst, nm in ((DB, "c_db"), (SM[:, 200:320], "c_dc"), (SM[:, 320:440], "c_mc")):
                td = POOL.dma(lambda e, d=dst, nm=nm: e.dma_start(d, A[nm]), d_par[1], tables)
            tp = td
            def compress():
                w1free, cfree = tables, tables
                kc = vc = None
                tw = POOL.dma(lambda e: e.dma_start(
                    W1, A["nsa_cmp_w1"][0, 0].rearrange("(l p) n -> p l n", p=128)), d_par[2], w1free)
                for part in range(2):
                    c0 = 2048 + 512 * part
                    yield from need(("n", c0, 0), ("n", c0, 1))
                    z = [zt[("n", c0, t)] for t in range(2)]
                    cw = []
                    for pr in range(2):
                        b = bank()
                        p = PE(many(*[tr(b.ap[:, 256 * j + 128 * t:256 * j + 128 * t + 128],
                                         ZN[:, t, c0 + 256 * pr + 128 * j:c0 + 256 * pr + 128 * j + 128])
                                      for j in range(2) for t in range(2)]), z, b.free)
                        w = ACT(copy(CT[:, 2 * pr:2 * pr + 2], v3(b.ap, 2)), p, cfree)
                        b.free = [w]
                        cw.append(w)
                    yield
                    bl = []
                    for j in range(15):
                        eng = POOL if j % 2 else DVE
                        bl.append(eng(tt(BLK[:, j], CT[:, :, 16 * j:16 * j + 32], rep(POS[:, part], 4), ALU.add),
                                      cw, tp, w1free))
                    yield
                    b = bank()
                    p = PE(mm(b.ap[:, 0:60], [(W1[:, l], BLK[:, :, :, l].rearrange("p j g -> p (j g)"))
                                              for l in range(32)]), tw, bl, b.free)
                    w1free = [p]
                    cfree = bl
                    if part == 0:
                        tw = POOL.dma(lambda e: e.dma_start(
                            W1, A["nsa_cmp_w1"][0, 1].rearrange("(l p) n -> p l n", p=128)), d_par[2], w1free)
                    e = ACT(act(HE, b.ap[:, 0:60], ACTF.Exp, scale=-1.0), p, kc, vc)
                    e = sigm(HE, e)
                    e = DVE(tt(HC, HE, b.ap[:, 0:60], ALU.mult), e)
                    b.free = [e]
                    yield
                    b = bank()
                    if part == 0:
                        p = PE(mm(b.ap[:, 0:60], [(W2[:, 0], HC)]), e, b.free)
                        kc = ACT(copy(KC.rearrange("p j g -> p (j g)"), b.ap[:, 0:60]), p)
                        b.free = [kc]
                        zt["kc"] = kc
                    else:
                        hc = HC.rearrange("p (j g) -> p j g", g=4)
                        p = PE(many(*[mm(b.ap[0:15, 128 * g:128 * g + 128], [(hc[:, :, g], W2[:, 1])])
                                      for g in range(4)]), e, b.free)
                        vc = ACT(copy(VC[0:15], v3(b.ap[0:15, :], 4)), p)
                        b.free = [vc]
                        zt["w1free"] = w1free
                        zt["ctfree"] = bl
                        zt["vc"] = vc
                    yield
                yield from need(("n", 5120, 0), ("n", 5120, 1))
                gt = ACT(act(GT, ZN[:, :, 5120:5168], ACTF.Exp, scale=-1.0), [zt[("n", 5120, t)] for t in range(2)])
                zt["gt"] = sigm(GT, gt)

            P4 = [[WORK[:, 320 + 512 * j:832 + 512 * j], BIG[:, SP0 + 1024 * j:SP0 + 1024 * j + 1024]] for j in range(2)]
            PT = [[v3(BIG[:, SP0 + 4096 + 512 * j:SP0 + 4608 + 512 * j], 4),
                   v3(BIG[:, SP0 + 2048 + 1024 * j:SP0 + 3072 + 1024 * j], 8)] for j in range(2)]
            K2 = [w3(2048 + 512 * j, 512, 2) for j in range(2)]
            QT = [w3(3072 + 512 * j, 512, 4) for j in range(4)]
            OT = [w3(5120 + 512 * j, 512, 4) for j in range(4)]
            k_read = {}

            def keys(u):
                for g in (u, u + 2):
                    for br in range(2):
                        c = 3072 + 1024 * br
                        yield from need(("n", c, 0), ("n", c, 1))
                        if g >= 2:
                            yield from need(("kr", g - 2, 0, br), ("kr", g - 2, 1, br))
                        b = bank()
                        p = PE(many(*[tr(b.ap[:, 128 * t:128 * t + 128], ZN[:, t, c + 128 * g:c + 128 * g + 128])
                                      for t in range(2)]), [zt[("n", c, t)] for t in range(2)], b.free)
                        w = ACT(copy(K2[u][:, br], b.ap[:, 0:256]), p, tables,
                                [zt.get(("kr", g - 2, i, br)) for i in range(2)])
                        b.free = [w]
                        zt[("kt", g, br)] = [w]
                        yield

            def stream(u, i):
                P, T, K = P4[u][i], PT[u][i], K2[u]
                Q, O = QT[2 * u + i], OT[2 * u + i]
                yield from need("vc", "kc", "gt")
                kc, vc, gt = zt["kc"], zt["vc"], zt["gt"]
                f_p, f_pt, f_q, f_o = [zt["w1free"], zt["ctfree"]], [zt["w1free"]], [tables], [tables]
                for g in (u, u + 2):
                    yield from need(("n", 512 * g, i))
                    b = bank()
                    p = PE(many(*[tr(b.ap[:, 128 * h:128 * h + 128],
                                     ZN[:, i, 512 * g + 128 * h:512 * g + 128 * h + 128])
                                  for h in range(4)]), zt[("n", 512 * g, i)], b.free)
                    tq = ACT(copy(Q, v3(b.ap, 4), QSCALE), p, f_q)
                    q_read = p
                    b.free = [tq]
                    yield
                    osum = None
                    for br in range(3):
                        nk = 15 if br == 0 else 128 * (i + 1)
                        ktile = 1 if br == 0 else i + 1
                        P_ = v3(P[:, 0:4 * nk], 4)
                        c0 = 16 * (2 * u + i)
                        mx, sm, rs = ST[:, c0:c0 + 4], ST[:, c0 + 4:c0 + 8], ST[:, c0 + 8:c0 + 12]
                        if br == 0:
                            b = bank()
                            p = PE(many(*[mm(b.ap[:, 15 * h:15 * h + 15], [(Q[:, h], KC[:, :, g])])
                                          for h in range(4)]), tq, kc, b.free)
                            s = [DVE(stt(P[:, 0:60], DC[:, i], 4.0 ** -g, b.ap[:, 0:60], ALU.mult, ALU.add),
                                     p, td, f_p)]
                            b.free = s
                        else:
                            s = []
                            yield from need(("kt", g, br - 1))
                            kts = zt[("kt", g, br - 1)]
                            for hb in range(i + 1):
                                b = bank()
                                hh = range(2 * hb, 2 * hb + 2) if i else range(4)
                                p = PE(many(*[mm(b.ap[:, nk * (h - hh[0]):nk * (h - hh[0]) + nk],
                                                 [(Q[:, h], K[:, br - 1, 0:nk])]) for h in hh]), tq, kts, b.free)
                                o_ = P[:, 512 * hb:512 * hb + 512]
                                dd = DB[:, 512 * i + 512 * hb:512 * i + 512 * hb + 512]
                                w = DVE(stt(o_, dd, 4.0 ** -g, b.ap, ALU.mult, ALU.add), p, td, f_p)
                                b.free = [w]
                                s.append(w)
                            zt[("kr", g, i, br - 1)] = p
                        yield
                        if br == 0:
                            m = DVE(red(mx, P_, ALU.max), s)
                            x = DVE(tt(P_, P_, bc(mx, 15), ALU.subtract), m)
                            x = ACT(act(P_, P_, ACTF.Exp), x)
                            x = DVE(red(sm, P_, ALU.add), x)
                            xs = [DVE(tt(P[:, 0:60], P[:, 0:60], MC[:, i], ALU.mult), x)]
                        else:
                            m = DVE(lambda e, mx=mx, P_=P_: e.tensor_reduce(mx, P_, AX, ALU.max, negate=True), s)
                            xs = [ACT(act(P_[:, h], P_[:, h], ACTF.Exp, bias=mx[:, h:h + 1],
                                          accum_out=sm[:, h:h + 1]), m) for h in range(4)]
                        r = DVE(rec(rs, sm), xs)
                        gv = GT[:, i, 12 * g:12 * g + 12].rearrange("p (h b) -> p h b", b=3)[:, :, br]
                        r = DVE(tt(rs, rs, gv, ALU.mult), r, gt)
                        yield
                        evs = []
                        for kt_ in range(ktile):
                            b = bank()
                            w_ = 15 if br == 0 else 128
                            p = PE(many(*[tr(b.ap[0:w_, 128 * h:128 * h + 128], P_[:, h, 128 * kt_:128 * kt_ + w_])
                                          for h in range(4)]), xs, b.free)
                            w = ACT(copy(T[0:w_, 4 * kt_:4 * kt_ + 4], v3(b.ap[0:w_, :], 4)), p, f_pt)
                            b.free = [w]
                            evs.append(w)
                        f_p = [p]
                        zv = None
                        if br:
                            c = (3584, 4608)[br - 1]
                            yield from need(("n", c, 0), ("n", c, 1))
                            zv = [zt[("n", c, t)] for t in range(2)]
                        yield
                        b = bank()
                        fns = []
                        for h in range(4):
                            if br == 0:
                                prs = [(T[0:15, h], VC[0:15, g])]
                            else:
                                c = (3584, 4608)[br - 1] + 128 * g
                                prs = [(T[:, 4 * kt_ + h], ZN[:, kt_, c:c + 128]) for kt_ in range(ktile)]
                            fns.append(mm(b.ap[:, 128 * h:128 * h + 128], prs))
                        p = PE(many(*fns), evs, vc, zv, b.free)
                        f_pt = [p]
                        if br == 0:
                            osum = DVE(tt(O, v3(b.ap, 4), bc(rs, 128), ALU.mult), p, r, f_o)
                            b.free = [osum]
                        else:
                            tmp = v3(P[:, 0:512], 4)
                            w = DVE(tt(tmp, v3(b.ap, 4), bc(rs, 128), ALU.mult), p, r)
                            b.free = [w]
                            dst = O if br == 1 else v3(ZN[:, i, 512 * g:512 * g + 512], 4)
                            osum = POOL(tt(dst, O, tmp, ALU.add), w, osum, q_read)
                            f_p = [osum]
                        yield
                    f_q = [zt[("kr", g, i, 1)]]
                    f_o = [osum]
                    zt[("no", g, i)] = osum

            return compress(), keys(0), keys(1), *[stream(u, i) for u in range(2) for i in range(2)]

        Z2 = v3(BIG[:, 0:4096], 2)

        def z2_sink(c, t, ap, tok):
            c = order_2[c]
            zt[("z2", c, t)] = ACT(copy(Z2[:, t, 512 * c:512 * c + 512], ap, HR[:, t:t + 1]), tok, zt["r"])
            return zt[("z2", c, t)]

        RT = BIG[:, 4096:4096 + 128]
        RT16 = BIG[:, 4224:4224 + 64]
        LC = BIG[:, 4288:4288 + 384]
        CA = BIG[:, 4672:4672 + 384]
        LTT = BIG[:, 5056:5056 + 128]
        ROT = BIG[:, 5184:5184 + 1024]
        SLN = BIG[:, 6208:6272]
        LAM = BIG[:, 6272:6400]
        QF = BIG[:, 6400:6400 + 4096]
        Y2 = v3(BIG[:, 10496:10496 + 1024], 2)
        TB = BIG[:, 11520:11520 + 2048]
        LAMV = SM[:, 200:210]

        def block2_tables(after):
            for dst, nm in ((RT, "c_r32"), (RT16, "c_r16"), (LC, "c_lc"), (CA, "c_ca"), (LTT, "c_lt")):
                t = POOL.dma(lambda e, d=dst, n=nm: e.dma_start(d, A[n]), d_par[3], after)
            t = POOL.dma(lambda e: e.dma_start(SLN, A["diff_subln_g_2"][0].partition_broadcast(128)), d_par[3], after)
            t = POOL.dma(lambda e: e.dma_start(LAM, A["diff_lam_2"][0].rearrange("a b -> (a b)").partition_broadcast(128)),
                       d_par[3], after)
            return t

        def rope(chunk, half, tab, tt_):
            n = 512 // (2 * half)
            res = []
            for t in range(2):
                x = Z2[:, t, 512 * chunk:512 * chunk + 512].rearrange("p (a two d) -> p a two d", two=2, d=half)
                x1, x2 = x[:, :, 0], x[:, :, 1]
                base = 3072 + 1024 * (chunk + t)
                r = WORK[:, base:base + 1024].rearrange("p (k a d) -> p k a d", k=4, d=half)
                cos = rep(tab[:, 2 * half * t:2 * half * t + half], n)
                sin = rep(tab[:, 2 * half * t + half:2 * half * t + 2 * half], n)
                z = [zt[("z2", chunk, t)], tt_]
                a = DVE(tt(r[:, 0], x1, cos, ALU.mult), z)
                b = POOL(tt(r[:, 1], x2, sin, ALU.mult), z)
                c = POOL(tt(r[:, 2], x1, sin, ALU.mult), z)
                d = DVE(tt(r[:, 3], x2, cos, ALU.mult), z)
                e = DVE(tt(x1, r[:, 0], r[:, 1], ALU.subtract), a, b, c, d)
                f = POOL(tt(x2, r[:, 2], r[:, 3], ALU.add), c, d, b, a)
                res.append([e, f])
            return res

        def feature(chunk, dh, mem, ready, free):
            n = 512 // dh
            dst = mem[0:dh, 0:n * 256].rearrange("p (a t) -> p a t", a=n)
            w = []
            for a in range(0, n, 2):
                b = bank()
                p = PE(many(*[tr(b.ap[0:dh, 256 * j + 128 * t:256 * j + 128 * t + 128],
                                 Z2[:, t, 512 * chunk + dh * (a + j):512 * chunk + dh * (a + j) + dh])
                              for j in range(2) for t in range(2)]), ready, b.free)
                x = ACT(copy(dst[:, a:a + 2], v3(b.ap[0:dh, :], 2)), p, free)
                b.free = [x]
                w.append(x)
            return dst, w

        def softmax_pair(pairs, nk, scale, bias, tabtok, tq, P, st):
            P = v3(P, 2)
            b = bank()
            p = PE(many(*[mm(b.ap[:, nk * j:nk * j + nk], [qk]) for j, qk in enumerate(pairs)]), tq, b.free)
            s = DVE(stt(P, v3(b.ap[:, 0:2 * nk], 2), scale, rep(bias, 2), ALU.mult, ALU.add), p, tabtok)
            b.free = [s]
            m = DVE(lambda e: e.tensor_reduce(st[:, 0:2], P, AX, ALU.max, negate=True), s)
            x = [ACT(act(P[:, j], P[:, j], ACTF.Exp, bias=st[:, j:j + 1], accum_out=st[:, 2 + j:3 + j]), m)
                 for j in range(2)]
            r = DVE(rec(st[:, 4:6], st[:, 2:4]), x)
            return P, x, r

        def transposed(srcs, T, x):
            b = bank()
            p = PE(many(*[tr(b.ap[:, 128 * k:128 * k + 128], a) for k, a in enumerate(srcs)]), x, b.free)
            w = ACT(copy(T, b.ap[:, 0:128 * len(srcs)]), p)
            b.free = [w]
            return w

        def gate2(chunk, i):
            g = Z2[:, i, 512 * chunk + 256:512 * chunk + 512]
            base = 2048 + 256 * (i + chunk - 1)
            e_ = WORK[:, base:base + 256]
            a = ACT(act(e_, g, ACTF.Exp, scale=-1.0), zt[("z2", chunk, i)])
            a = sigm(e_, a)
            return e_, POOL(tt(e_, e_, g, ALU.mult), a)

        def attend2(layer, tabs):
            st = SM[:, 64:256]
            ends = {}

            def vals(c):
                return [zt[("z2", c, t)] for t in range(2)]

            def setup(chunk, dh, mem, tab):
                yield from need(("z2", chunk, 0), ("z2", chunk, 1))
                ready = vals(chunk) if tab is None else rope(chunk, dh // 2, tab, tabs)
                yield
                zt[("qk", layer, chunk)] = feature(chunk, dh, mem, ready, [])
                yield

            def plain(br, par, i):
                u = 2 * br + par
                yield from need(("qk", layer, 2 * br))
                qk, w = zt[("qk", layer, 2 * br)]
                base = (WORK[:, 0:1536], WORK[:, 7168:8704], TB, BIG[:, 13696:15232])[u]
                nk = 128 * (i + 1)
                P = base[:, 512 * i:512 * i + 2 * nk]
                T = base[:, 512 * i + 2 * nk:512 * i + 4 * nk]
                s_ = st[:, 8 * (2 * u + i):8 * (2 * u + i) + 8]
                P, x, r = softmax_pair([(qk[:, h, 128 * i:128 * i + 128], qk[:, 4 + h, 0:nk]) for h in (par, par + 2)],
                                       nk, 0.125, (LC, CA)[br][:, 128 * i:128 * i + nk], tabs, w, P, s_)
                yield
                w2 = transposed([P[:, j, 128 * k:128 * k + 128] for j in range(2) for k in range(i + 1)], T, x)
                yield from need(("z2", 2 * br + 1, 1))
                yield
                b = bank()
                c = 512 * (2 * br + 1) + 64 * par
                p = PE(many(*[mm(b.ap[:, 64 * j:64 * j + 64],
                                 [(T[:, 128 * ((i + 1) * j + k):128 * ((i + 1) * j + k) + 128],
                                   Z2[:, k, c + 128 * j:c + 128 * j + 64]) for k in range(i + 1)])
                              for j in range(2)]), w2, vals(2 * br + 1), b.free)
                y = Y2[:, i, 256 * br:256 * br + 256].rearrange("p (a b) -> p a b", a=2)[:, :, 64 * par:64 * par + 64]
                d = DVE(tt(y, v3(b.ap[:, 0:128], 2), bc(s_[:, 4:6], 64), ALU.mult), p, r)
                b.free = [d]
                ends.setdefault((br, i), []).append(d)
                yield

            def close(br, chunk, n):
                yield from need(("z2", chunk, 1))
                g = [gate2(chunk, i) for i in range(2)]
                yield
                for i in range(2):
                    while len(ends.get((br, i), [])) < n:
                        yield
                    y = Y2[:, i, 256 * br:256 * br + 256]
                    zt[("y2", layer, br, i)] = POOL(tt(y, y, g[i][0], ALU.mult), g[i][1], ends[(br, i)])

            if layer == 0:
                return [setup(0, 64, QF, RT), setup(2, 64, QF[:, 2048:], RT)] + [
                    plain(br, par, i) for br in range(2) for par in range(2) for i in range(2)] + [
                    close(0, 1, 2), close(1, 3, 2)]
            li = 0.8 - 0.6 * float(np.exp(-0.3))

            def lam_value():
                l = LAM.rearrange("p (g a b) -> p g a b", g=2, a=2)
                pr = v3(ROT[:, 0:64], 2)
                a = DVE(tt(pr, l[:, :, 0], l[:, :, 1], ALU.mult), tabs)
                a = DVE(red(LAMV[:, 0:2], pr, ALU.add), a)
                a = ACT(act(LAMV[:, 2:4], LAMV[:, 0:2], ACTF.Exp), a)
                a = DVE(tt(LAMV[:, 4:5], LAMV[:, 3:4], LAMV[:, 2:3], ALU.subtract), a)
                return DVE(ts(LAMV[:, 5:6], LAMV[:, 4:5], -li, None, ALU.add), a)

            lam = lam_value()

            def diff(h, i):
                yield from need(("qk", layer, 0))
                qk, w = zt[("qk", layer, 0)]
                base = TB if h == 3 else WORK[:, 5120 + 1152 * h:6272 + 1152 * h]
                nk = 128 * (i + 1)
                P = base[:, 384 * i:384 * i + 2 * nk]
                T = base[:, 384 * i + 2 * nk:384 * i + 3 * nk]
                s_ = st[:, 8 * (2 * h + i):8 * (2 * h + i) + 8]
                P, x, r = softmax_pair([(qk[:, 2 * h + j, 128 * i:128 * i + 128], qk[:, 8 + 2 * h + j, 0:nk])
                                        for j in range(2)],
                                       nk, 32 ** -0.5, CA[:, 128 * i:128 * i + nk], tabs, w, P, s_)
                yield
                c1 = DVE(tt(s_[:, 5:6], s_[:, 5:6], LAMV[:, 5:6], ALU.mult), r, lam)
                a = DVE(ts(P[:, 0], P[:, 0], s_[:, 4:5], None, ALU.mult), r, x)
                a = DVE(stt(P[:, 0], P[:, 1], s_[:, 5:6], P[:, 0], ALU.mult, ALU.add), a, c1)
                yield
                w2 = transposed([P[:, 0, 128 * k:128 * k + 128] for k in range(i + 1)], T, a)
                yield from need(("z2", 1, 1))
                yield
                b = bank()
                p = PE(mm(b.ap[:, 0:64], [(T[:, 128 * k:128 * k + 128], Z2[:, k, 512 + 64 * h:576 + 64 * h])
                                          for k in range(i + 1)]), w2, vals(1), b.free)
                d = ACT(copy(Y2[:, i, 64 * h:64 * h + 64], b.ap[:, 0:64]), p)
                b.free = [d]
                ends.setdefault((0, i), []).append(d)
                yield

            def close_diff():
                yield from need(("z2", 1, 1))
                g = [gate2(1, i) for i in range(2)]
                yield
                for i in range(2):
                    while len(ends.get((0, i), [])) < 4:
                        yield
                    y = v3(Y2[:, i, 0:256], 4)
                    sq = v3(ROT[:, 256 + 256 * i:512 + 256 * i], 4)
                    ss = st[:, 64 + 4 * i:68 + 4 * i]
                    a = POOL(tt(sq, y, y, ALU.mult), ends[(0, i)])
                    a = DVE(red(ss, sq, ALU.add), a)
                    r = rstd(ss, ss, 64, a, 1.0 - li)
                    a = DVE(tt(y, y, bc(ss, 64), ALU.mult), r)
                    a = POOL(tt(y, y, rep(SLN, 4), ALU.mult), a)
                    y = Y2[:, i, 0:256]
                    zt[("y2", layer, 0, i)] = POOL(tt(y, y, g[i][0], ALU.mult), g[i][1], a)
                    yield

            def stick(h):
                yield from need(("qk", layer, 2))
                qd, wd = zt[("qk", layer, 2)]
                base = 13696 + 768 * h if h < 3 else 11520 + 1152
                Zs, L = BIG[:, base:base + 384], BIG[:, base + 384:base + 768]
                b = bank()
                q, k = qd[:, h], qd[:, 4 + h]
                p = PE(many(mm(b.ap[:, 0:256], [(k[:, 0:128], q)]),
                            mm(b.ap[:, 256:384], [(k[:, 128:256], q[:, 128:256])])), wd, b.free)
                zz = ACT(copy(Zs, b.ap[:, 0:384], 0.125), p)
                b.free = [zz]
                a = ACT(act(L, Zs, ACTF.Abs), zz)
                a = ACT(act(L, L, ACTF.Exp, scale=-1.0), a)
                yield
                a = ACT(act(L, L, ACTF.Ln, bias=one_b), a, ones_act)
                yield
                a = DVE(stt(L, Zs, 0.0, L, ALU.max, ALU.add), a)
                m1 = POOL(tt(L[:, 0:128], L[:, 0:128], LTT, ALU.mult), a)
                m2 = POOL(tt(L[:, 256:384], L[:, 256:384], LTT, ALU.mult), a)
                yield
                b = bank()
                p = PE(many(mm(b.ap[:, 0:128], [(SUFI, L[:, 0:128])]),
                            mm(b.ap[:, 128:256], [(SUFI, L[:, 128:256]), (ONE, L[:, 256:384])]),
                            mm(b.ap[:, 256:384], [(SUFI, L[:, 256:384])])), m1, m2, tabs2, b.free)
                a = DVE(tt(Zs, Zs, b.ap[:, 0:384], ALU.subtract), p)
                b.free = [a]
                a = DVE(ts(Zs, Zs, 0.0, None, ALU.min), a)
                a = ACT(act(L, Zs, ACTF.Exp), a)
                yield
                m1 = POOL(tt(L[:, 0:128], L[:, 0:128], LTT, ALU.mult), a)
                m2 = POOL(tt(L[:, 256:384], L[:, 256:384], LTT, ALU.mult), a)
                yield from need(("z2", 3, 1))
                yield
                b = bank()
                c = 1536 + 64 * h
                p = PE(many(mm(b.ap[:, 0:64], [(L[:, 0:128], Z2[:, 0, c:c + 64])]),
                            mm(b.ap[:, 64:128], [(L[:, 128:256], Z2[:, 0, c:c + 64]),
                                                 (L[:, 256:384], Z2[:, 1, c:c + 64])])),
                       m1, m2, vals(3), b.free)
                d = ACT(copy(Y2[:, :, 256 + 64 * h:320 + 64 * h], v3(b.ap[:, 0:128], 2)), p)
                b.free = [d]
                for i in range(2):
                    ends.setdefault((1, i), []).append(d)
                yield

            return [setup(0, 32, QF, RT16), setup(2, 64, WORK, None)] + [
                diff(h, i) for h in range(4) for i in range(2)] + [stick(h) for h in range(4)] + [
                close_diff(), close(1, 3, 4)]

        SUFI = BIG[:, 13568:13696]
        tabs2 = None

        def whole():
            nonlocal tabs2
            h = {(t, n): t_x[n] for t in range(2) for n in range(4)}
            u, feed = pre_norm(GP[:, 0], h)
            together(use_cols([b - a for a, b in order_even], UTH, UTL, u, feed, z_sink_even, BIG[:, 15888:16400]),
                     convs(), gdn(), hgrn(), out_gate(1, 0, DG, ("ob", 0, 0), ("ob", 0, 1)),
                     out_gate(0, 0, HG, ("oa", 0)), out_gate(1, 1, DG, ("ob", 1, 0), ("ob", 1, 1)),
                     out_gate(0, 1, HG, ("oa", 1)))
            gs = [zt[("o", a, hf, i)] for a in range(2) for hf in range(2) for i in range(2)]
            if STAGE == 1:
                cps = [POOL(cp(H[:, t, 1024 * a:1024 * a + 1024], zcol(t, 4096 * a, 1024)), gs) for t in range(2) for a in range(2)]
                finish(cps)
                return
            t_gb = load_gb(A["norm_g"][0, 1], 0, gs)
            last = out_proj(NKT, lambda k, t: zcol(t, 128 * k if k < 8 else 4096 + 128 * (k - 8), 128),
                            [[zt[("o", k // 8, k % 8 // 4, i)] for i in range(2)] for k in range(NKT)])
            h = post_norm(t_gb, last)
            if STAGE == 2:
                return finish(all_of(h))
            h = ffn(0, A["norm_g"][0, 3], GP[:, 1], h)
            if STAGE == 3:
                return finish(all_of(h))
            u, feed = pre_norm(GP[:, 2], h)
            parts = nsa(all_of(h))
            together(use_cols([b - a for a, b in order_nsa], UTH, UTL, u, feed, nsa_sink, WORK[:, 8704:9216]), *parts)
            t_gb = load_gb(A["norm_g"][1, 1], 0, all_of(h) + [zt[("n", 5120, t)] for t in range(2)])
            last = out_proj(NKT, lambda k, t: ZN[:, t, 128 * k:128 * k + 128],
                            [[zt[("no", k // 4, i)] for i in range(2)] for k in range(NKT)])
            h = post_norm(t_gb, last)
            if STAGE == 4:
                return finish(all_of(h))
            h = ffn(1, A["norm_g"][1, 3], GP[:, 3], h)
            if STAGE == 5:
                return finish(all_of(h))
            tabs = block2_tables(all_of(h))
            tabs2 = POOL(ts(SUFI, LTT, -1.0, 1.0, ALU.mult, ALU.add), tabs)
            t_gb = load_gb(A["final_norm_g_2"], 0, all_of(h))
            for layer in range(2):
                for key in [k for k in zt if isinstance(k, tuple) and k[0] == "z2"]:
                    del zt[key]
                u, feed = pre_norm(GP[:, 4 + layer], h)
                together(use_cols([512] * 4, UTH, UTL, u, feed, z2_sink), *attend2(layer, tabs))
                last = out_proj(4, lambda k, t: Y2[:, t, 128 * k:128 * k + 128],
                                [[zt[("y2", layer, k // 2, i)] for i in range(2)] for k in range(4)])
                h = plain_add(last)
                if STAGE == 6 + layer:
                    return finish(all_of(h))
            o = out.rearrange("o (t p) n -> p (o t) n", p=128)
            sq = [[], []]
            for n in range(4):
                sq[0].append(square(0, n, h[(0, n)]))
                sq[1].append(DVE(lambda e, n=n: e.bn_stats(out=BNS[:, n], in_=H[:, 1, 512 * n:512 * n + 512]), h[(1, n)]))
            a = DVE(lambda e: e.bn_aggr(out=BNA, in_=BNS), sq[1])
            a = DVE(stt(HS2[:, 1:2], BNA[:, 0:1], BNA[:, 0:1], BNA[:, 1:2], ALU.mult, ALU.add), a)
            a = [DVE(ts(HS2[:, 1:2], HS2[:, 1:2], float(D), None, ALU.mult), a)]
            a.append(DVE(red(HS2[:, 0:1], HSQ[:, 0:4], ALU.add), sq[0]))
            r = rstd(HR, HS2, D, a)
            for n in range(4):
                c = slice(512 * n, 512 * n + 512)
                e0 = DVE(stt(H[:, 0, c], H[:, 0, c], HR[:, 0:1], GB[:, c], ALU.mult, ALU.mult), r, t_gb)
                e1 = ACT(copy(H[:, 1, c], H[:, 1, c], HR[:, 1:2]), r)
                e1 = (POOL if n < 3 else DVE)(tt(H[:, 1, c], H[:, 1, c], GB[:, c], ALU.mult), e1, t_gb)
                SP.dma(lambda e, c=c: e.dma_start(o[:, :, c], H[:, :, c]), d_out, e0, e1)
            SP.wait((d_out[0], d_out[1]))

        whole()

        block = ctx.enter_context(nc.Block())

        @block.sync
        def _(e):
            SP.emit(e)

        @block.scalar
        def _(e):
            ACT.emit(e)

        @block.vector
        def _(e):
            DVE.emit(e)

        @block.gpsimd
        def _(e):
            POOL.emit(e)

        @block.tensor
        def _(e):
            PE.emit(e)


_NAMES = ["x", "norm_g", "ab_w_in", "gdn_a_log", "gdn_dt_bias", "hgrn_norm_g", "gdn_norm_g", "ab_w_out",
          "nsa_w_in", "nsa_cmp_w1", "nsa_cmp_w2", "nsa_w_out", "ffn_w_gu", "ffn_w_down",
          "w_in_2", "w_out_2", "diff_lam_2", "diff_subln_g_2", "final_norm_g_2"]


def kernel(**inputs):
    import concourse.bacc as _bacc
    from concourse.bass_utils import run_bass_kernel_spmd as _run

    nc = _bacc.Bacc("TRN2", target_bir_lowering=False, num_devices=1)
    host = {n: np.ascontiguousarray(inputs[n]) for n in _NAMES}
    ng, n2 = np.asarray(inputs["norm_g"]), np.asarray(inputs["norm_g_2"])
    pre = np.stack([ng[0, 0], ng[0, 2], ng[1, 0], ng[1, 2], n2[0], n2[1]])
    host["g_pre"] = np.ascontiguousarray(pre.reshape(6, 16, 128).transpose(2, 0, 1))
    host["conv_w"] = np.ascontiguousarray(np.asarray(inputs["gdn_conv_w"])[0].reshape(4, 24, 128).transpose(2, 1, 0))
    host["pos"] = np.ascontiguousarray(np.asarray(inputs["nsa_cmp_pos"])[0].transpose(2, 0, 1))
    for name, c0 in (("ab_w_in", 8192), ("nsa_w_in", 5120)):
        w = np.asarray(inputs[name])[0][:, c0:]
        host[name + "_rest"] = np.ascontiguousarray(w.reshape(16, 128, -1).transpose(1, 0, 2).reshape(128, -1))
    host.update(constants())
    arrays, A = {}, {}
    for name, a in host.items():
        arrays[f"in_{name}"] = a
        A[name] = nc.dram_tensor(f"in_{name}", a.shape, mybir.dt.from_np(a.dtype), kind="ExternalInput").ap()
    out = nc.dram_tensor("out_0", (1, 256, 2048), F32, kind="ExternalOutput").ap()
    build(nc, A, out)
    r = _run(nc, [arrays], core_ids=[0])
    return r.results[0]["out_0"]
```
